# Optimizing a Trainium2 kernel written in Bass

```python
import math
import jax, jax.numpy as jnp
from jax import lax
import numpy as np

D_MODEL = 1024
BATCH = 1
SEQ = 1024
DEPTH = 1

SB_HEADS = 8
SB_HEAD_DIM = 64
SB_WIDTH = SB_HEADS * SB_HEAD_DIM
Q_BLOCK = 128
SGU_GROUPS = 8
SGU_GROUP_DIM = 64
SGU_WIDTH = SGU_GROUPS * SGU_GROUP_DIM
CHUNK = 128
IN_SPLITS = (SB_WIDTH, SB_WIDTH, SB_WIDTH, SGU_WIDTH, SGU_WIDTH, D_MODEL, D_MODEL)
IN_WIDTH = sum(IN_SPLITS)
N_GROUPS = 4
EXPERTS_PER_GROUP = 8
N_EXPERTS = N_GROUPS * EXPERTS_PER_GROUP
TOP_K = 2
EXPERT_FF = 512
MOE_BLOCK = 128
PLE_DIM = 256
EPS = 1e-6

kernel_name = "hybrid_stickbreak_sgu_hmoe_trunk"

def rms_norm(x, g):
    xf = x.astype(jnp.float32)
    y = xf * lax.rsqrt(jnp.mean(xf * xf, axis=-1, keepdims=True) + EPS)
    return (y * g.astype(jnp.float32)).astype(x.dtype)

def stick_breaking_attention(q, k, v):
    b, h, s, dh = q.shape
    q = q.astype(jnp.float32)
    k = k.astype(jnp.float32)
    v = v.astype(jnp.float32)
    nqb = s // Q_BLOCK
    q_blocks = q.reshape(b, h, nqb, Q_BLOCK, dh).transpose(2, 0, 1, 3, 4)
    starts = jnp.arange(nqb, dtype=jnp.int32) * Q_BLOCK
    key_pos = jnp.arange(s, dtype=jnp.int32)
    scale = 1.0 / math.sqrt(dh)

    def block(args):
        q_blk, t0 = args
        z = jnp.einsum('bhqd,bhkd->bhqk', q_blk, k) * scale
        q_pos = t0 + jnp.arange(Q_BLOCK, dtype=jnp.int32)
        causal = key_pos[None, :] < q_pos[:, None]
        log_beta = jax.nn.log_sigmoid(z)
        log_keep = jnp.where(causal, log_beta - z, 0.0)
        after = lax.cumsum(log_keep, axis=3, reverse=True) - log_keep
        a = jnp.where(causal, jnp.exp(log_beta + after), 0.0)
        return jnp.einsum('bhqk,bhkd->bhqd', a, v)

    o = lax.map(block, (q_blocks, starts))
    return o.transpose(1, 2, 0, 3, 4).reshape(b, h, s, dh)

def chunk_spatial_gating(u, v, w_s, b_s):
    b, s, g, dg = v.shape
    nc = s // CHUNK
    vc = v.reshape(b, nc, CHUNK, g, dg)
    tril = jnp.tril(jnp.ones((CHUNK, CHUNK), dtype=bool))
    w = jnp.where(tril[None], w_s, 0.0).astype(v.dtype)
    mixed = jnp.einsum('gts,bcsgd->bctgd', w, vc) + b_s.T.astype(v.dtype)[None, None, :, :, None]
    return u * mixed.reshape(b, s, g, dg)

def hierarchical_moe(h, w_gr, b_gr, w_er, b_er, w_e_in, w_e_out):
    bsz, s, d = h.shape
    n = bsz * s
    hf = h.reshape(n, d)
    g_logits = (hf @ w_gr).astype(jnp.float32) + b_gr.astype(jnp.float32)
    g_prob = jax.nn.softmax(g_logits, axis=-1)
    grp = jnp.argmax(g_prob, axis=-1).astype(jnp.int32)
    grp_w = jnp.max(g_prob, axis=-1)
    e_logits = ((hf @ w_er).astype(jnp.float32) + b_er.astype(jnp.float32))
    e_logits = e_logits.reshape(n, N_GROUPS, EXPERTS_PER_GROUP)
    e_logits = jnp.take_along_axis(e_logits, grp[:, None, None], axis=1)[:, 0]
    e_prob = jax.nn.softmax(e_logits, axis=-1)
    top_w, top_i = lax.top_k(e_prob, TOP_K)
    top_w = top_w / jnp.sum(top_w, axis=-1, keepdims=True)
    wts = (grp_w[:, None] * top_w).reshape(-1)
    eid = (grp[:, None] * EXPERTS_PER_GROUP + top_i.astype(jnp.int32)).reshape(-1)
    tok = jnp.repeat(jnp.arange(n, dtype=jnp.int32), TOP_K)
    order = jnp.argsort(eid)
    se = eid[order]
    counts = jnp.bincount(eid, length=N_EXPERTS).astype(jnp.int32)
    padded = (counts + MOE_BLOCK - 1) // MOE_BLOCK * MOE_BLOCK
    off = jnp.cumsum(counts) - counts
    pend = jnp.cumsum(padded)
    poff = pend - padded
    rank = jnp.arange(n * TOP_K, dtype=jnp.int32) - off[se]
    dest = poff[se] + rank
    cap = n * TOP_K + N_EXPERTS * MOE_BLOCK
    slot_tok = jnp.full((cap,), n, dtype=jnp.int32).at[dest].set(tok[order])
    slot_w = jnp.zeros((cap,), jnp.float32).at[dest].set(wts[order])
    nblk = cap // MOE_BLOCK
    blk_start = jnp.arange(nblk, dtype=jnp.int32) * MOE_BLOCK
    blk_e = jnp.minimum(jnp.sum(pend[None, :] <= blk_start[:, None], axis=1), N_EXPERTS - 1)
    hp = jnp.concatenate([hf, jnp.zeros((1, d), hf.dtype)], axis=0)
    xs = hp[slot_tok].reshape(nblk, MOE_BLOCK, d)

    def expert_block(args):
        xb, e = args
        gate, up = jnp.split(xb @ w_e_in[e], 2, axis=-1)
        return (jax.nn.silu(gate) * up) @ w_e_out[e]

    ys = lax.map(expert_block, (xs, blk_e)).reshape(cap, d)
    ys = ys * slot_w[:, None].astype(ys.dtype)
    out = jnp.zeros((n + 1, d), ys.dtype).at[slot_tok].add(ys)[:n]
    return out.reshape(bsz, s, d)

def setup_inputs(seed: int = 0) -> dict:
    key = jax.random.key(seed)
    ks = jax.random.split(key, 24)
    f32 = jnp.float32
    nrm = lambda k, shape, scale: jax.random.normal(k, shape, f32) * scale
    gain = lambda k, shape: 1.0 + 0.01 * jax.random.normal(k, shape, f32)
    L, D = DEPTH, D_MODEL
    return {
        "x": nrm(ks[0], (BATCH, SEQ, D), 1.0),
        "p": nrm(ks[1], (DEPTH, BATCH, SEQ, PLE_DIM), 1.0),
        "norm_mix": gain(ks[2], (L, D)),
        "w_in": nrm(ks[3], (L, D, IN_WIDTH), D ** -0.5),
        "q_norm": gain(ks[4], (L, SB_HEAD_DIM)),
        "k_norm": gain(ks[5], (L, SB_HEAD_DIM)),
        "sgu_norm": gain(ks[6], (L, SGU_WIDTH)),
        "w_spatial": nrm(ks[7], (L, SGU_GROUPS, CHUNK, CHUNK), CHUNK ** -0.5),
        "b_spatial": gain(ks[8], (L, SGU_GROUPS, CHUNK)),
        "w_up_a": nrm(ks[9], (L, SB_WIDTH, D), SB_WIDTH ** -0.5),
        "w_up_b": nrm(ks[10], (L, SGU_WIDTH, D), SGU_WIDTH ** -0.5),
        "w_out": nrm(ks[11], (L, D, D), D ** -0.5),
        "norm_ffn": gain(ks[12], (L, D)),
        "w_group_router": nrm(ks[13], (L, D, N_GROUPS), D ** -0.5),
        "b_group_router": nrm(ks[14], (L, N_GROUPS), 0.01),
        "w_expert_router": nrm(ks[15], (L, D, N_EXPERTS), D ** -0.5),
        "b_expert_router": nrm(ks[16], (L, N_EXPERTS), 0.01),
        "w_expert_in": nrm(ks[17], (L, N_EXPERTS, D, 2 * EXPERT_FF), D ** -0.5),
        "w_expert_out": nrm(ks[18], (L, N_EXPERTS, EXPERT_FF, D), EXPERT_FF ** -0.5),
        "norm_ple": gain(ks[19], (L, D)),
        "w_ple_gate": nrm(ks[20], (L, D, D), D ** -0.5),
        "w_ple_proj": nrm(ks[21], (L, PLE_DIM, D), PLE_DIM ** -0.5),
    }

def reference(x, p, norm_mix, w_in, q_norm, k_norm, sgu_norm, w_spatial, b_spatial,
              w_up_a, w_up_b, w_out, norm_ffn, w_group_router, b_group_router,
              w_expert_router, b_expert_router, w_expert_in, w_expert_out,
              norm_ple, w_ple_gate, w_ple_proj):
    bsz, s, d = x.shape
    cuts = list(np.cumsum(IN_SPLITS)[:-1])
    for i in range(DEPTH):
        h = rms_norm(x, norm_mix[i])
        z = h @ w_in[i]
        q, k, v, u_s, v_s, g_a, g_b = jnp.split(z, cuts, axis=-1)
        q = rms_norm(q.reshape(bsz, s, SB_HEADS, SB_HEAD_DIM), q_norm[i]).transpose(0, 2, 1, 3)
        k = rms_norm(k.reshape(bsz, s, SB_HEADS, SB_HEAD_DIM), k_norm[i]).transpose(0, 2, 1, 3)
        v = v.reshape(bsz, s, SB_HEADS, SB_HEAD_DIM).transpose(0, 2, 1, 3)
        o_a = stick_breaking_attention(q, k, v).astype(x.dtype)
        o_a = o_a.transpose(0, 2, 1, 3).reshape(bsz, s, SB_WIDTH)
        u_s = jax.nn.gelu(u_s).reshape(bsz, s, SGU_GROUPS, SGU_GROUP_DIM)
        v_s = rms_norm(jax.nn.gelu(v_s), sgu_norm[i]).reshape(bsz, s, SGU_GROUPS, SGU_GROUP_DIM)
        o_b = chunk_spatial_gating(u_s, v_s, w_spatial[i], b_spatial[i]).reshape(bsz, s, SGU_WIDTH)
        merged = jax.nn.sigmoid(g_a) * (o_a @ w_up_a[i]) + jax.nn.sigmoid(g_b) * (o_b @ w_up_b[i])
        x = x + merged @ w_out[i]
        h2 = rms_norm(x, norm_ffn[i])
        x = x + hierarchical_moe(h2, w_group_router[i], b_group_router[i],
                                 w_expert_router[i], b_expert_router[i],
                                 w_expert_in[i], w_expert_out[i])
        gate = jax.nn.sigmoid(rms_norm(x, norm_ple[i]) @ w_ple_gate[i])
        x = x + gate * (p[i].astype(x.dtype) @ w_ple_proj[i])
    return x


_drawn_inputs = setup_inputs


def setup_inputs(seed=0):
    import zlib

    import numpy as np

    out = dict(_drawn_inputs(seed))
    spreads = {}
    factors = {'norm_mix': 3.616,
     'q_norm': 95.167,
     'k_norm': 31.635,
     'sgu_norm': 33.829,
     'b_spatial': 20.025,
     'norm_ffn': 9.516,
     'b_group_router': 26.126,
     'b_expert_router': 19.694,
     'norm_ple': 200.0,
     'p': 6.103,
     'w_ple_gate': 8.0,
     'w_ple_proj': 6.106}
    for name, (base, spread) in spreads.items():
        noise = np.random.default_rng([zlib.crc32(name.encode()), seed]).standard_normal(out[name].shape)
        drawn = base * np.exp(spread * noise) if base else spread * noise
        out[name] = __import__('jax').numpy.asarray(drawn.astype(out[name].dtype))
    for name, factor in factors.items():
        out[name] = (out[name] * factor).astype(out[name].dtype)
    return out
```

```python
from contextlib import ExitStack

import concourse.bass as bass
from concourse import mybir

F32 = mybir.dt.float32
F32R = mybir.dt.float32r
I32 = mybir.dt.int32
U32 = mybir.dt.uint32
ALU = mybir.AluOpType
ACT = mybir.ActivationFunctionType
AX = mybir.AxisListType

P = 128
D = 1024
T = 1024
KT = D // P
TT = T // P
HALF = 512
HEADS, HD = 8, 64
PAIRS = HEADS // 2
SBW = HEADS * HD
GROUPS, GD = 8, 64
NG, EPG = 4, 8
NE = NG * EPG
FF = 512
PLE = 256
EPS = 1e-6
PARTS = ((0, 0), (0, 1), (1, 0))


class Chain:

    def __init__(self, eng, sem):
        self.eng, self.sem, self.n = eng, sem, 0

    def __call__(self, ins):
        self.n += 1
        ins.then_inc(self.sem, 1)
        self.eng.wait_ge(self.sem, self.n)


def constants(nc, ctx):
    sb = lambda name, shape, dt=F32: ctx.enter_context(nc.sbuf_tensor("c_" + name, shape, dt))
    ident = sb("ident", [P, P])
    headones = sb("headones", [P, P])
    ones = sb("ones", [P, P])
    below = sb("below", [P, P])
    causal = sb("causal", [P, P])
    eps = sb("eps", [P, 1])
    with nc.semaphore("c_set") as c_set, nc.semaphore("c_sel") as c_sel, nc.Block() as block:
        @block.gpsimd
        def _(pool):
            nc.gpsimd.memset(ident[:, :], 0.0).then_inc(c_set, 1)
            nc.gpsimd.memset(headones[:, :], 1.0).then_inc(c_set, 1)
            nc.gpsimd.memset(ones[:, :], 1.0).then_inc(c_set, 1)
            nc.gpsimd.memset(eps[:, :], EPS).then_inc(c_set, 1)
            pool.wait_ge(c_set, 4)
            nc.gpsimd.affine_select(out=ident[:, :], in_=ident[:, :], compare_op=ALU.not_equal, fill=1.0, base=0,
                                    pattern=[[-1, P]], channel_multiplier=1).then_inc(c_sel, 1)
            nc.gpsimd.affine_select(out=below[:, :], in_=ones[:, :], compare_op=ALU.is_gt, fill=0.0, base=0,
                                    pattern=[[1, P]], channel_multiplier=-1).then_inc(c_sel, 1)
            nc.gpsimd.affine_select(out=causal[:, :], in_=ones[:, :], compare_op=ALU.is_gt, fill=0.0, base=0,
                                    pattern=[[-1, P]], channel_multiplier=1).then_inc(c_sel, 1)
            nc.gpsimd.affine_select(out=headones[:, 0:HD], in_=headones[:, 0:HD], compare_op=ALU.is_ge, fill=0.0,
                                    base=HD - 1, pattern=[[0, HD]], channel_multiplier=-1).then_inc(c_sel, 1)
            nc.gpsimd.affine_select(out=headones[:, HD:P], in_=headones[:, HD:P], compare_op=ALU.is_ge, fill=0.0,
                                    base=-HD, pattern=[[0, HD]], channel_multiplier=1).then_inc(c_sel, 1)
            pool.wait_ge(c_sel, 5)
    return {"ident": ident[:, :], "headones": headones[:, :], "ones": ones[:, :], "below": below[:, :],
            "causal": causal[:, :], "eps": eps[:, 0:1]}


def refined_rstd(nc, link, out, sumsq, root, tmp, width):
    link(nc.vector.tensor_scalar(tmp, sumsq, 1.0 / width, EPS, ALU.mult, ALU.add))
    link(nc.vector.reciprocal(out, root))
    link(nc.vector.tensor_tensor(tmp, tmp, out, ALU.mult))
    link(nc.vector.tensor_tensor(tmp, tmp, out, ALU.mult))
    link(nc.vector.tensor_scalar(tmp, tmp, -0.5, 1.5, ALU.mult, ALU.add))
    link(nc.vector.tensor_tensor(out, out, tmp, ALU.mult))


def mix_projection(nc, c, io, dr):
    with ExitStack() as ctx:
        sb = lambda name, shape, dt=F32: ctx.enter_context(nc.sbuf_tensor("a_" + name, shape, dt))
        ps = lambda name, shape: ctx.enter_context(nc.psum_tensor("a_" + name, shape, F32))
        sem = lambda name: ctx.enter_context(nc.semaphore("a_" + name))
        XR, RAW, RING, ST = 2, 4, 8, 3
        hT = [sb(f"hT{i}", [P, KT, T], F32R) for i in range(2)]
        wS = [sb(f"w{i}", [P, RING, D], F32R) for i in range(2)]
        raw = sb("raw", [P, RAW, D])
        xt = sb("xt", [P, XR, D])
        hn = sb("hn", [P, D])
        gain = sb("gain", [P, D])
        vs = sb("vs", [P, TT, SBW])
        wT = sb("wT", [P, GROUPS, P])
        bsp = sb("bsp", [P, PAIRS, P])
        sgain = sb("sgain", [P, PAIRS])
        qkgain = sb("qkgain", [P, 2])
        st = sb("st", [P, ST, HALF])
        sq = sb("sq", [P, 2, HALF])
        rt = sb("rt", [P, 2, HALF])
        vv = sb("vv", [P, 2, HALF])
        tmp = sb("tmp", [P, TT])
        ssq = sb("ssq", [P, TT]); srt = sb("srt", [P, TT]); rstd = sb("rstd", [P, TT])
        vss = sb("vss", [P, TT]); vsr = sb("vsr", [P, TT]); vrs = sb("vrs", [P, TT])
        psP = [ps(f"psP{i}", [P, HALF]) for i in range(4)]
        psT = [ps(f"psT{i}", [P, HALF]) for i in range(2)]
        psS = [ps(f"psS{i}", [P, HALF]) for i in range(2)]

        x_in = [sem(f"x_in{i}") for i in range(XR)]; consts_in = sem("consts_in"); wsp_in = sem("wsp_in")
        raw_in = [sem(f"raw_in{i}") for i in range(RAW)]
        w_split = sem("w_split"); w_hi = sem("w_hi")
        ssq_done = sem("ssq_done"); srt_done = sem("srt_done"); dve_step = sem("dve_step")
        hn_done = sem("hn_done"); hn_turned = sem("hn_turned"); hi_done = sem("hi_done"); hT_done = sem("hT_done")
        wmask = sem("wmask"); wt_turned = sem("wt_turned"); wT_done = sem("wT_done")
        proj = sem("proj"); freed = [sem("freed_act"), sem("freed_dve")]
        vs_gelu = sem("vs_gelu"); vs_sq = sem("vs_sq"); vs_rt = sem("vs_rt"); vs_done = sem("vs_done")
        mixed = sem("mixed"); u_gelu = sem("u_gelu"); ob_a = sem("ob_a")
        sq_done = sem("sq_done"); ssum = sem("ssum"); rt_done = sem("rt_done"); vv_done = sem("vv_done")
        staged_a = sem("staged_a"); staged_d = sem("staged_d")
        stored = [sem(f"stored{i}") for i in range(ST)]

        w_in = io["w_in"][0]
        QCOL, KCOL, VCOL, UCOL, VSCOL, GCOL = 0, SBW, 2 * SBW, 3 * SBW, 4 * SBW, 5 * SBW
        granules = [w_in[2 * j * P:(2 * j + 2) * P, col:col + HALF].rearrange("(k p) n -> p k n", p=P)
                    for col in (VSCOL, VCOL) for j in range(4)]
        fcols = [UCOL + P * i for i in range(4)] + [P * i for i in range(8)] + [GCOL + P * i for i in range(16)]
        granules += [w_in[:, col:col + P].rearrange("(k p) n -> p k n", p=P) for col in fcols]
        NGR = len(granules)
        UU, UQ, UG = 16, 24, 40
        NU = UG + 32

        def unit_done_needs(g):
            return 8 * (g // 4 + 1) if g < 8 else 16 + 2 * (g - 8 + 1)

        def unit_owner(n):
            if n < 8 or UU <= n < UQ or n >= UG:
                return 0
            return 1

        def frees_before(n):
            m = n - 4
            who = unit_owner(m)
            return who, sum(unit_owner(i) == who for i in range(m + 1))

        def destination(n):
            if 8 <= n < 16:
                return dr["v"][(n - 8) * P:(n - 7) * P, :]
            i, half = divmod(n - UU, 2)
            cols = slice(half * HALF, (half + 1) * HALF)
            if n < UQ:
                return dr["ob"][i, :, cols]
            if n < UG:
                return dr["qk"][i - 4, :, cols]
            return dr["gates"][i - 12, :, cols]
        stores = list(range(8, NU))

        with nc.Block() as block:
            @block.sync
            def _(sp):
                for i in range(XR):
                    sp.dma_start(xt[:, i], io["x"][0, i * P:(i + 1) * P, :]).then_inc(x_in[i], 16)
                sp.dma_start(gain[:, :], io["norm_mix"].to_broadcast([P, D])).then_inc(consts_in, 16)
                for g in range(RAW):
                    sp.dma_start(raw[:, g].rearrange("p (k n) -> p k n", n=granules[g].shape[-1]), granules[g]).then_inc(raw_in[g], 16)
                with nc.allow_non_contiguous_dma(reason="gains, a few hundred words"):
                    sp.dma_start(sgain[:, :], io["sgu_norm"][0].rearrange("(a p) -> p a", p=P)).then_inc(consts_in, 16)
                    for i, name in enumerate(("q_norm", "k_norm")):
                        for h in range(2):
                            sp.dma_start(qkgain[h * HD:(h + 1) * HD, i:i + 1],
                                         io[name].rearrange("a p -> p a")).then_inc(consts_in, 16)
                for g in range(GROUPS):
                    sp.dma_start(bsp[(g % 2) * GD:(g % 2 + 1) * GD, g // 2, :],
                                 io["b_spatial"][0, g:g + 1, :].to_broadcast([GD, P])).then_inc(consts_in, 16)
                for i in range(XR, TT):
                    sp.wait_ge(ssq_done, i - XR + 1)
                    sp.wait_ge(hn_done, i - XR + 1)
                    sp.dma_start(xt[:, i % XR], io["x"][0, i * P:(i + 1) * P, :]).then_inc(x_in[i % XR], 16)
                sp.wait_ge(ssq_done, TT)
                sp.wait_ge(hn_done, TT)
                sp.dma_start(xt[:, 0].rearrange("p (g s) -> p g s", g=GROUPS),
                             io["w_spatial"][0].rearrange("g t s -> t g s")).then_inc(wsp_in, 16)
                for g in range(RAW, NGR):
                    sp.wait_ge(w_split, g - RAW + 1)
                    sp.dma_start(raw[:, g % RAW].rearrange("p (k n) -> p k n", n=granules[g].shape[-1]),
                                 granules[g]).then_inc(raw_in[g % RAW], 16)

            @block.gpsimd
            def _(pool):
                for g in range(NGR):
                    if g == 6:
                        pool.wait_ge(wsp_in, 16)
                        v = xt[:, 0].rearrange("p (g s) -> p g s", g=GROUPS)
                        nc.gpsimd.affine_select(out=v, in_=v, compare_op=ALU.is_ge, fill=0.0, base=0,
                                                pattern=[[0, GROUPS], [-1, P]], channel_multiplier=1).then_inc(wmask, 1)
                    pool.wait_ge(raw_in[g % RAW], 16 * (g // RAW + 1))
                    if g >= RING:
                        pool.wait_ge(proj, unit_done_needs(g - RING))
                    r = raw[:, g % RAW, :]
                    hi, lo = (w[:, g % RING, :] for w in wS)
                    nc.gpsimd.tensor_tensor(hi, r, c["ones"][:, 0:1].to_broadcast([P, D]), ALU.mult).then_inc(w_hi, 1)
                    pool.wait_ge(w_hi, g + 1)
                    nc.gpsimd.tensor_tensor(lo, r, hi.bitcast(F32), ALU.subtract).then_inc(w_split, 1)

            def staging(eng, n):
                i = stores.index(n)
                if i >= ST:
                    eng.wait_ge(stored[i % ST], 16 * (i // ST))
                return st[:, i % ST, :]

            @block.scalar
            def _(act):
                def store(n):
                    i = stores.index(n)
                    act.wait_ge(staged_a if n >= UG else staged_d, n - UG + 1 if n >= UG else i + 1)
                    act.dma_start(destination(n), st[:, i % ST]).then_inc(stored[i % ST], 16)

                for t in range(TT):
                    act.wait_ge(x_in[t % XR], 16 * (t // XR + 1))
                    if t >= 1:
                        act.wait_ge(hn_done, t)
                        act.wait_ge(hn_turned, 2 * t)
                    nc.scalar.activation(hn[:, :], xt[:, t % XR], ACT.Square, accum_out=ssq[:, t:t + 1]).then_inc(ssq_done, 1)
                    act.wait_ge(ssq_done, t + 1)
                    nc.scalar.activation(srt[:, t:t + 1], ssq[:, t:t + 1], ACT.Sqrt, bias=c["eps"], scale=1.0 / D).then_inc(srt_done, 1)
                    for h in range(2):
                        act.wait_ge(hn_turned, 2 * t + h + 1)
                        nc.scalar.copy(hT[0][:, 4 * h:4 * h + 4, t * P:(t + 1) * P],
                                       psT[h][:, :].rearrange("p (k n) -> p k n", k=4)).then_inc(hi_done, 1)
                for h in range(2):
                    act.wait_ge(wt_turned, h + 1)
                    nc.scalar.copy(wT[:, 4 * h:4 * h + 4, :], psT[h][:, :].rearrange("p (k n) -> p k n", k=4)).then_inc(wT_done, 1)
                for t in range(TT):
                    act.wait_ge(proj, t + 1)
                    nc.scalar.activation(vs[:, t, :], psP[t % 4][:, :], ACT.Gelu_apprx_tanh).then_inc(freed[0], 1)
                    act.wait_ge(freed[0], t + 1)
                    if t == 0:
                        act.wait_ge(hn_turned, 2 * TT)
                    else:
                        act.wait_ge(vs_sq, t)
                    nc.scalar.activation(hn[:, 0:HALF], vs[:, t, :], ACT.Square, accum_out=vss[:, t:t + 1]).then_inc(vs_sq, 1)
                act.wait_ge(vs_sq, TT)
                nc.scalar.activation(vsr[:, :], vss[:, :], ACT.Sqrt, bias=c["eps"], scale=1.0 / SBW).then_inc(vs_rt, 1)
                for n in range(8, UU):
                    store(n)
                for n in range(UU, UQ):
                    act.wait_ge(proj, n + 1)
                    m = n - UU
                    if m >= 2:
                        act.wait_ge(staged_d, 8 + m - 1)
                    nc.scalar.activation(rt[:, m % 2, :], psP[n % 4][:, :], ACT.Gelu_apprx_tanh).then_inc(freed[0], 1)
                    if m >= 1:
                        store(n - 1)
                for n in range(UQ, UG):
                    m = n - UQ
                    act.wait_ge(proj, n + 1)
                    if m >= 2:
                        act.wait_ge(ssum, m - 1)
                    nc.scalar.activation(sq[:, m % 2, :], psP[n % 4][:, :], ACT.Square).then_inc(sq_done, 1)
                    act.wait_ge(ssum, m + 1)
                    act.wait_ge(staged_d, 16 + m - 1 if m >= 2 else 16)
                    nc.scalar.activation(vv[:, m % 2, :], psS[m % 2][:, :], ACT.Identity, bias=c["eps"], scale=1.0 / HD).then_inc(vv_done, 1)
                    nc.scalar.activation(rt[:, m % 2, :], psS[m % 2][:, :], ACT.Sqrt, bias=c["eps"], scale=1.0 / HD).then_inc(rt_done, 1)
                    store(n - 1)
                store(UG - 1)
                for n in range(UG, NU):
                    act.wait_ge(proj, n + 1)
                    out = staging(act, n)
                    nc.scalar.activation(out, psP[n % 4][:, :], ACT.Sigmoid).then_inc(staged_a, 1)
                    store(n)
                for i in range(ST):
                    act.wait_ge(stored[i], 16 * len(range(i, len(stores), ST)))

            @block.vector
            def _(dve):
                link = Chain(dve, dve_step)
                dve.wait_ge(consts_in, 16 * (1 + 1 + 4 + GROUPS))
                link(nc.vector.tensor_scalar(qkgain[:, 0:1], qkgain[:, 0:1], HD ** -0.5, None, ALU.mult))
                for t in range(TT):
                    dve.wait_ge(srt_done, t + 1)
                    refined_rstd(nc, link, rstd[:, t:t + 1], ssq[:, t:t + 1], srt[:, t:t + 1], tmp[:, 0:1], D)
                    nc.vector.scalar_tensor_tensor(hn[:, :], xt[:, t % XR], rstd[:, t:t + 1], gain[:, :],
                                                   ALU.mult, ALU.mult).then_inc(hn_done, 1)
                    for h in range(2):
                        dve.wait_ge(hi_done, 2 * t + h + 1)
                        cols = slice(t * P, (t + 1) * P)
                        nc.vector.tensor_tensor(hT[1][:, 4 * h:4 * h + 4, cols], psT[h][:, :].rearrange("p (k n) -> p k n", k=4),
                                                hT[0][:, 4 * h:4 * h + 4, cols].bitcast(F32), ALU.subtract).then_inc(hT_done, 1)
                for n in range(8, 16):
                    dve.wait_ge(proj, n + 1)
                    out = staging(dve, n)
                    nc.vector.tensor_copy(out, psP[n % 4][:, :]).then_inc(staged_d, 1)
                    if n == 11:
                        dve.wait_ge(vs_rt, 1)
                        refined_rstd(nc, link, vrs[:, :], vss[:, :], vsr[:, :], tmp[:, :], SBW)
                        for t in range(TT):
                            nc.vector.tensor_scalar(vs[:, t, :], vs[:, t, :], vrs[:, t:t + 1], None, ALU.mult).then_inc(vs_done, 1)
                for n in range(UU, UQ):
                    m = n - UU
                    i = m // 2
                    dve.wait_ge(mixed, m + 1)
                    out = staging(dve, n)
                    nc.vector.scalar_tensor_tensor(out.rearrange("p (c t) -> p c t", c=4), psT[m % 2][:, :].rearrange("p (c t) -> p c t", c=4),
                                                   sgain[:, i:i + 1], bsp[:, i:i + 1, :].to_broadcast([P, 4, P]),
                                                   ALU.mult, ALU.add).then_inc(ob_a, 1)
                    dve.wait_ge(ob_a, m + 1)
                    dve.wait_ge(freed[0], 8 + m + 1)
                    nc.vector.tensor_tensor(out, out, rt[:, m % 2, :], ALU.mult).then_inc(staged_d, 1)
                for n in range(UQ, UG):
                    m = n - UQ
                    dve.wait_ge(vv_done, m + 1)
                    dve.wait_ge(rt_done, m + 1)
                    r, v = rt[:, m % 2, :], vv[:, m % 2, :]
                    link(nc.vector.reciprocal(r, r))
                    link(nc.vector.tensor_tensor(v, v, r, ALU.mult))
                    link(nc.vector.tensor_tensor(v, v, r, ALU.mult))
                    link(nc.vector.tensor_scalar(v, v, -0.5, 1.5, ALU.mult, ALU.add))
                    link(nc.vector.tensor_tensor(r, r, v, ALU.mult))
                    out = staging(dve, n)
                    nc.vector.scalar_tensor_tensor(out, psP[n % 4][:, :], qkgain[:, m // 8:m // 8 + 1],
                                                   rt[:, m % 2, :], ALU.mult, ALU.mult).then_inc(staged_d, 1)

            @block.tensor
            def _(pe):
                def turn(src, h, bank):
                    for k in range(4):
                        ins = nc.tensor.transpose(bank[:, k * P:(k + 1) * P], src[:, (4 * h + k) * P:(4 * h + k + 1) * P], c["ident"])
                    return ins
                for t in range(TT):
                    pe.wait_ge(hn_done, t + 1)
                    for h in range(2):
                        if t >= 1:
                            pe.wait_ge(hT_done, 2 * t - 1 + h)
                        turn(hn, h, psT[h]).then_inc(hn_turned, 1)
                pe.wait_ge(wmask, 1)
                for h in range(2):
                    pe.wait_ge(hT_done, 2 * TT)
                    turn(xt[:, 0], h, psT[h]).then_inc(wt_turned, 1)

                def bank_free(n):
                    if n >= 4:
                        m = n - 4
                        if 8 <= m < 16:
                            pe.wait_ge(staged_d, m - 8 + 1)
                        elif m < 8:
                            pe.wait_ge(freed[0], m + 1)
                        elif m < UQ:
                            pe.wait_ge(freed[0], 8 + m - UU + 1)
                        elif m < UG:
                            pe.wait_ge(staged_d, 16 + m - UQ + 1)
                        else:
                            pe.wait_ge(staged_a, m - UG + 1)

                def product(n, operands):
                    bank_free(n)
                    for i, (a, b) in enumerate(operands):
                        ins = nc.tensor.matmul(psP[n % 4][:, :], a, b, start=(i == 0), stop=(i == len(operands) - 1))
                    ins.then_inc(proj, 1)

                for chunk in range(2):
                    for t in range(TT):
                        if chunk == 0 and t == 0:
                            pe.wait_ge(hT_done, 2 * TT)
                        if t == 0:
                            pe.wait_ge(w_split, 4 * chunk + 4)
                        product(8 * chunk + t, [(hT[a][:, k, t * P:(t + 1) * P],
                                                 wS[b][:, 4 * chunk + k // 2, (k % 2) * HALF:(k % 2 + 1) * HALF])
                                                for k in range(KT) for a, b in PARTS])

                def piece(i, half):
                    n = UU + 2 * i + half
                    if half == 0:
                        pe.wait_ge(w_split, 8 + i + 1)
                    s = (8 + i) % RING
                    product(n, [(wS[a][:, s, k * P:(k + 1) * P], hT[b][:, k, half * HALF:(half + 1) * HALF])
                                for k in range(KT) for a, b in PARTS])

                def mix(m):
                    i, half = divmod(m, 2)
                    pe.wait_ge(vs_done, TT)
                    pe.wait_ge(wT_done, 2)
                    if m >= 2:
                        pe.wait_ge(ob_a, m - 1)
                    for ch in range(4):
                        for g in range(2):
                            ins = nc.tensor.matmul(psT[m % 2][g * GD:(g + 1) * GD, ch * P:(ch + 1) * P],
                                                   vs[:, 4 * half + ch, (2 * i + g) * GD:(2 * i + g + 1) * GD],
                                                   wT[:, 2 * i + g, :], start=True, stop=True)
                    ins.then_inc(mixed, 1)

                def sums(m):
                    pe.wait_ge(sq_done, m + 1)
                    if m >= 2:
                        pe.wait_ge(rt_done, m - 1)
                    nc.tensor.matmul(psS[m % 2][:, :], c["headones"], sq[:, m % 2, :], start=True, stop=True).then_inc(ssum, 1)

                for i in range(4):
                    for half in range(2):
                        piece(i, half)
                        mix(2 * i + half)
                for i in range(4, 12):
                    for half in range(2):
                        piece(i, half)
                        m = 2 * (i - 4) + half
                        if m >= 1:
                            sums(m - 1)
                sums(15)
                for i in range(12, 28):
                    for half in range(2):
                        piece(i, half)


def attention(nc, c, dr):
    with ExitStack() as ctx:
        sb = lambda name, shape, dt=F32: ctx.enter_context(nc.sbuf_tensor("b_" + name, shape, dt))
        ps = lambda name, shape: ctx.enter_context(nc.psum_tensor("b_" + name, shape, F32))
        sem = lambda name: ctx.enter_context(nc.semaphore("b_" + name))
        R = 4
        kT = sb("kT", [P, PAIRS, T])
        qT = sb("qT", [P, HEADS, T])
        v = sb("v", [P, TT, SBW])
        e = sb("e", [P, R, T])
        lb = sb("lb", [P, R, T])
        lk = sb("lk", [P, R, T])
        after = sb("after", [P, R, T + 1])
        aT = sb("aT", [P, 2, T])
        o = sb("o", [P, PAIRS, T])
        psZ = [ps(f"psZ{i}", [P, T]) for i in range(2)]
        psA = [ps(f"psA{i}", [P, HALF]) for i in range(2)]
        psO = [ps(f"psO{i}", [P, P]) for i in range(2)]
        zeroed = sem("zeroed"); qkv_in = [sem(f"qkv_in{i}") for i in range(PAIRS)]; v_in = sem("v_in")
        z_done = sem("z_done"); act_step = sem("act_step"); l_done = sem("l_done"); z_read = sem("z_read")
        dve_step = sem("dve_step"); scanned = sem("scanned"); summed = sem("summed"); expd = sem("expd"); a_done = sem("a_done")
        turned = sem("turned"); aT_done = sem("aT_done"); pv_done = sem("pv_done"); o_done = sem("o_done"); o_out = sem("o_out")

        units = [(i, qt, h) for i in range(PAIRS) for qt in range(TT) for h in range(2)]
        N = len(units)
        groups = [(u[1] + 4) // 4 for u in units]
        gsum = [sum(groups[:n]) for n in range(N + 1)]
        keys = [(u[1] + 1) * P for u in units]

        with nc.Block() as block:
            @block.sync
            def _(sp):
                sp.wait_ge(zeroed, 2)
                for i in range(PAIRS):
                    for h in range(2):
                        rows = slice(h * HD, (h + 1) * HD)
                        sp.dma_start(qT[rows, 2 * i + h, :], dr["qk"][i, rows, :]).then_inc(qkv_in[i], 16)
                    sp.dma_start(kT[:, i, :], dr["qk"][PAIRS + i]).then_inc(qkv_in[i], 16)
                    if i == 0:
                        sp.dma_start(v[:, :, :], dr["v"].rearrange("(t p) n -> p t n", p=P)).then_inc(v_in, 16)
                for i in range(PAIRS):
                    sp.wait_ge(o_done, TT * (i + 1))
                    sp.dma_start(dr["oa"][i], o[:, i, :]).then_inc(o_out, 16)
                sp.wait_ge(o_out, 16 * PAIRS)

            @block.gpsimd
            def _(pool):
                for h in range(2):
                    rows = slice((1 - h) * HD, (2 - h) * HD)
                    nc.gpsimd.memset(qT[rows, h::2, :], 0.0).then_inc(zeroed, 1)
                for n in range(N + 2):
                    if n < N:
                        r, S = n % R, keys[n]
                        pool.wait_ge(scanned, n + 1)
                        nc.gpsimd.tensor_tensor(lb[:, r, 0:S], lb[:, r, 0:S], after[:, r, 1:S + 1], ALU.add).then_inc(summed, 1)
                    if n >= 2:
                        m = n - 2
                        r, S = m % R, keys[m]
                        pool.wait_ge(expd, m + 1)
                        nc.gpsimd.tensor_tensor(lk[:, r, S - P:S], lk[:, r, S - P:S], c["causal"], ALU.mult).then_inc(a_done, 1)

            @block.scalar
            def _(act):
                link = Chain(act, act_step)
                nc.scalar.preload_act_table_set("natural_log_exp_and_others")
                for n in range(N + 5):
                    if n < N:
                        r, S = n % R, keys[n]
                        act.wait_ge(z_done, n + 1)
                        if n >= R:
                            act.wait_ge(z_read, n - R + 1)
                        link(nc.scalar.activation(e[:, r, 0:S], psZ[n % 2][:, 0:S], ACT.Abs))
                        link(nc.scalar.activation(e[:, r, 0:S], e[:, r, 0:S], ACT.Exp, scale=-1.0))
                        nc.scalar.activation(e[:, r, 0:S], e[:, r, 0:S], ACT.Ln, bias=1.0).then_inc(l_done, 1)
                    if 2 <= n < N + 2:
                        m = n - 2
                        r, S = m % R, keys[m]
                        act.wait_ge(summed, m + 1)
                        nc.scalar.activation(lk[:, r, 0:S], lb[:, r, 0:S], ACT.Exp).then_inc(expd, 1)
                    if n >= 5 and units[n - 5][2] == 1:
                        i, qt, _ = units[n - 5]
                        act.wait_ge(pv_done, n - 4)
                        nc.scalar.copy(o[:, i, qt * P:(qt + 1) * P], psO[qt % 2][:, :]).then_inc(o_done, 1)

            @block.vector
            def _(dve):
                link = Chain(dve, dve_step)
                link(nc.vector.memset(after[:, :, :], 0.0))
                for n in range(N + 3):
                    if n < N:
                        r, S = n % R, keys[n]
                        z = psZ[n % 2][:, 0:S]
                        dve.wait_ge(l_done, n + 1)
                        if n >= R:
                            dve.wait_ge(expd, n - R + 1)
                            dve.wait_ge(turned, gsum[n - R + 1])
                        link(nc.vector.scalar_tensor_tensor(lb[:, r, 0:S], z, 0.0, e[:, r, 0:S], ALU.min, ALU.subtract))
                        nc.vector.tensor_tensor(lk[:, r, 0:S], lb[:, r, 0:S], z, ALU.subtract).then_inc(z_read, 1)
                        dve.wait_ge(z_read, n + 1)
                        link(nc.vector.tensor_tensor(lk[:, r, S - P:S], lk[:, r, S - P:S], c["causal"], ALU.mult))
                        link(nc.vector.memset(after[:, r, S:S + 1], 0.0))
                        nc.vector.tensor_tensor_scan(after[:, r, 0:S][:, ::-1], c["ones"][:, 0:1].to_broadcast([P, S]),
                                                     lk[:, r, 0:S][:, ::-1], 0.0, ALU.mult, ALU.add).then_inc(scanned, 1)
                    if n >= 3:
                        m = n - 3
                        for g in range(groups[m]):
                            G = gsum[m] + g
                            dve.wait_ge(turned, G + 1)
                            if m >= 2:
                                dve.wait_ge(pv_done, m - 1)
                            w = min(HALF, keys[m] - g * HALF)
                            nc.vector.tensor_copy(aT[:, m % 2, g * HALF:g * HALF + w], psA[G % 2][:, 0:w]).then_inc(aT_done, 1)

            @block.tensor
            def _(pe):
                for n in range(N + 4):
                    if n < N:
                        i, qt, h = units[n]
                        if qt == 0 and h == 0:
                            pe.wait_ge(qkv_in[i], 48)
                        if n >= 2:
                            pe.wait_ge(z_read, n - 1)
                        for g in range(groups[n]):
                            w = min(HALF, keys[n] - g * HALF)
                            ins = nc.tensor.matmul(psZ[n % 2][:, g * HALF:g * HALF + w], qT[:, 2 * i + h, qt * P:(qt + 1) * P],
                                                   kT[:, i, g * HALF:g * HALF + w], start=True, stop=True)
                        ins.then_inc(z_done, 1)
                    if n >= 4:
                        m = n - 4
                        i, qt, h = units[m]
                        pe.wait_ge(aT_done, gsum[m + 1])
                        if m == 0:
                            pe.wait_ge(v_in, 16)
                        if h == 0 and m >= 4:
                            pe.wait_ge(o_done, m // 2 - 1)
                        for j in range(qt + 1):
                            ins = nc.tensor.matmul(psO[qt % 2][h * HD:(h + 1) * HD, :], v[:, j, (2 * i + h) * HD:(2 * i + h + 1) * HD],
                                                   aT[:, m % 2, j * P:(j + 1) * P], start=(j == 0), stop=(j == qt))
                        ins.then_inc(pv_done, 1)
                    if 3 <= n < N + 3:
                        m = n - 3
                        qt = units[m][1]
                        pe.wait_ge(a_done, m + 1)
                        for g in range(groups[m]):
                            G = gsum[m] + g
                            if G >= 2:
                                pe.wait_ge(aT_done, G - 1)
                            for j in range(4 * g, min(4 * g + 4, qt + 1)):
                                ins = nc.tensor.transpose(psA[G % 2][:, (j % 4) * P:(j % 4 + 1) * P], lk[:, m % R, j * P:(j + 1) * P], c["ident"])
                            ins.then_inc(turned, 1)


BLOCK = 128
MAXB = T * 2 // BLOCK + NE


def merge_and_route(nc, c, io, dr, keep):
    with ExitStack() as ctx:
        sb = lambda name, shape, dt=F32: ctx.enter_context(nc.sbuf_tensor("m_" + name, shape, dt))
        ps = lambda name, shape: ctx.enter_context(nc.psum_tensor("m_" + name, shape, F32))
        sem = lambda name: ctx.enter_context(nc.semaphore("m_" + name))
        RAW, UR, URAW = 3, 2, 2
        oS = [sb(f"o{i}", [P, 2 * PAIRS, T], F32R) for i in range(2)]
        mS = [sb(f"m{i}", [P, KT, T], F32R) for i in range(2)]
        uS = [sb(f"u{i}", [P, UR, D], F32R) for i in range(2)]
        raw = sb("raw", [P, RAW, D])
        uraw = sb("uraw", [P, URAW, D])
        gate = sb("gate", [P, 2, 2, HALF])
        ta = sb("ta", [P, HALF]); tb = sb("tb", [P, HALF])
        x1 = gate[:, :, :, :].rearrange("p r i n -> p r (i n)")
        h2T = uraw[:, 0, :].rearrange("p (k n) -> p k n", k=KT)
        hn = uraw[:, 1, :]
        gain = sb("gain", [P, D])
        NR = 96
        wr = sb("wr", [P, KT, NR])
        br = sb("br", [P, NG + NE])
        L = sb("L", [P, TT, NG + NE])
        ssq = sb("ssq", [P, TT]); srt = sb("srt", [P, TT]); rstd = sb("rstd", [P, TT]); tmp = sb("tmp", [P, TT])
        psP = [ps(f"psP{i}", [P, HALF]) for i in range(6)]
        psT = [ps(f"psT{i}", [P, HALF]) for i in range(2)]

        gain_in = sem("gain_in"); wr_zero = sem("wr_zero"); wr_in = sem("wr_in")
        raw_in = [sem(f"raw_in{i}") for i in range(RAW)]; uraw_in = [sem(f"uraw_in{i}") for i in range(URAW)]
        gate_in = [sem(f"gate_in{i}") for i in range(2)]; x_in = [sem(f"x_in{i}") for i in range(2)]
        u_hi = sem("u_hi"); u_split = sem("u_split")
        hi = sem("hi"); lo = sem("lo")
        up = sem("up"); dve_step = sem("dve_step"); act_step = sem("act_step"); gated = sem("gated"); m_sum = sem("m_sum"); m_hi = sem("m_hi"); m_done = sem("m_done")
        out = sem("out"); x1_done = sem("x1_done"); ssq_done = sem("ssq_done"); srt_done = sem("srt_done"); h2_done = sem("h2_done")
        turned = sem("turned"); h2T_done = sem("h2T_done"); logits = sem("logits"); L_done = sem("L_done")
        x1_out = [sem(f"x1_out{i}") for i in range(2)]; h2_out = sem("h2_out")

        G8 = [P, TT, NG]; E8 = [P, TT, EPG]; GE = [P, TT, NG, EPG]; TE = [P, TT, NE]
        w4 = sb("w4", [P, 1, NG]); w8 = sb("w8", [P, 1, EPG]); thr = sb("thr", [P, 1, TT - 1])
        tokid = sb("tokid", [P, TT], I32); filler = sb("filler", [P, MAXB + 1], I32); zrow = sb("zrow", [1, D])
        gmax = sb("gmax", [P, TT, 1]); g_oh = sb("g_oh", G8); g_tmp = sb("g_tmp", G8); g_exp = sb("g_exp", G8); g_w = sb("g_w", [P, TT])
        sel4 = sb("sel4", GE); esel = sb("esel", E8); e_tmp = sb("e_tmp", E8); pick = [sb(f"pick{i}", E8) for i in range(2)]
        emax = [sb(f"emax{i}", [P, TT, 1]) for i in range(2)]; e_exp = sb("e_exp", [P, TT]); e_sum = sb("e_sum", [P, TT])
        hot = [sb(f"hot{i}", GE) for i in range(2)]; both = sb("both", TE)
        rank = sb("rank", TE); count = sb("count", TE); off = sb("off", TE); total = sb("total", [P, NE, 1])
        over = sb("over", [P, NE, TT - 1]); nb = sb("nb", [P, NE]); cum = sb("cum", [P, NE + 1]); base = sb("base", [P, 1, NE])
        destf = sb("destf", [P, 2, TT])
        r_const = sem("r_const"); d_ready = sem("d_ready"); d_exp = sem("d_exp"); hot_done = sem("hot_done"); ranked = sem("ranked")
        dest_done = sem("dest_done"); fill_out = sem("fill_out"); slots_out = sem("slots_out")
        flat = lambda a: a[:, :, :].rearrange("p t n -> p (t n)")

        def first_of_max(link, values, out_hot, maximum, weights, tmp3):
            shape = list(values.shape)
            link(nc.vector.tensor_reduce(maximum, values, AX.X, ALU.max))
            link(nc.vector.tensor_tensor(out_hot, values, maximum.to_broadcast(shape), ALU.is_equal))
            link(nc.vector.tensor_tensor(out_hot, out_hot, weights.to_broadcast(shape), ALU.mult))
            link(nc.vector.tensor_reduce(tmp3, out_hot, AX.X, ALU.max))
            link(nc.vector.tensor_tensor(out_hot, out_hot, tmp3.to_broadcast(shape), ALU.is_equal))

        def routing(dve, link):
            dve.wait_ge(r_const, 6)
            t1 = tmp[:, :].rearrange("p (t n) -> p t n", n=1)
            LG = L[:, :, 0:NG]
            LE = L[:, :, NG:].rearrange("p t (g e) -> p t g e", g=NG)
            spread = lambda oh: oh.rearrange("p t (g n) -> p t g n", n=1).to_broadcast(GE)
            first_of_max(link, LG, g_oh[:, :, :], gmax[:, :, :], w4[:, :, :], t1)
            nc.vector.tensor_tensor(g_tmp[:, :, :], LG, gmax[:, :, :].to_broadcast(G8), ALU.subtract).then_inc(d_ready, 1)
            link(nc.vector.tensor_tensor(sel4[:, :, :, :], LE, spread(g_oh[:, :, :]), ALU.mult))
            link(nc.vector.tensor_reduce(esel[:, :, :], sel4[:, :, :, :].rearrange("p t g e -> p t e g"), AX.X, ALU.add))
            first_of_max(link, esel[:, :, :], pick[0][:, :, :], emax[0][:, :, :], w8[:, :, :], t1)
            link(nc.vector.scalar_tensor_tensor(e_tmp[:, :, :], pick[0][:, :, :], -3e38, esel[:, :, :], ALU.mult, ALU.add))
            first_of_max(link, e_tmp[:, :, :], pick[1][:, :, :], emax[1][:, :, :], w8[:, :, :], t1)
            flat1 = lambda a: a[:, :, :].rearrange("p t n -> p (t n)")
            nc.vector.tensor_tensor(e_sum[:, :], flat1(emax[1]), flat1(emax[0]), ALU.subtract).then_inc(d_ready, 1)
            for i in range(2):
                link(nc.vector.tensor_tensor(hot[i][:, :, :, :], spread(g_oh[:, :, :]),
                                             pick[i][:, :, :].rearrange("p t (n e) -> p t n e", n=1).to_broadcast(GE), ALU.mult))
            h = [a[:, :, :, :].rearrange("p t g e -> p t (g e)") for a in hot]
            nc.vector.tensor_tensor(both[:, :, :], h[0], h[1], ALU.add).then_inc(hot_done, 1)
            dve.wait_ge(d_exp, 2)
            link(nc.vector.tensor_reduce(g_w[:, :], g_exp[:, :, :], AX.X, ALU.add))
            link(nc.vector.tensor_scalar(e_sum[:, :], e_exp[:, :], 1.0, None, ALU.add))
            link(nc.vector.tensor_tensor(e_sum[:, :], e_sum[:, :], g_w[:, :], ALU.mult))
            link(nc.vector.reciprocal(keep["w"][:, 0, :], e_sum[:, :]))
            link(nc.vector.tensor_tensor(keep["w"][:, 1, :], keep["w"][:, 0, :], e_exp[:, :], ALU.mult))
            dve.wait_ge(ranked, 2)
            link(nc.vector.tensor_copy(flat(count), psP[1][:, 0:TT * NE]))
            link(nc.vector.memset(off[:, 0, :], 0.0))
            for t in range(1, TT):
                link(nc.vector.tensor_tensor(off[:, t, :], off[:, t - 1, :], count[:, t - 1, :], ALU.add))
            tot = total[:, :, :].rearrange("p e n -> p (e n)")
            link(nc.vector.tensor_tensor(tot, off[:, TT - 1, :], count[:, TT - 1, :], ALU.add))
            link(nc.vector.tensor_tensor(flat(rank), flat(off), psP[0][:, 0:TT * NE], ALU.add))
            link(nc.vector.tensor_tensor(over[:, :, :], total[:, :, :].to_broadcast([P, NE, TT - 1]), thr[:, :, :].to_broadcast([P, NE, TT - 1]), ALU.is_gt))
            link(nc.vector.tensor_reduce(nb[:, :], over[:, :, :], AX.X, ALU.add))
            link(nc.vector.tensor_scalar(nb[:, :], nb[:, :], 1.0, None, ALU.add))
            link(nc.vector.memset(cum[:, 0:1], 0.0))
            link(nc.vector.tensor_tensor_scan(cum[:, 1:NE + 1], c["ones"][:, 0:NE], nb[:, :], 0.0, ALU.mult, ALU.add))
            link(nc.vector.tensor_copy(keep["cum"][:, 0:NE + 1], cum[:, :]))
            link(nc.vector.tensor_scalar(keep["cum"][:, NE + 1:NE + 2], cum[:, NE:NE + 1], -1.0, float(MAXB), ALU.mult, ALU.add))
            link(nc.vector.tensor_scalar(base[:, 0, :], cum[:, 0:NE], float(BLOCK), None, ALU.mult))
            link(nc.vector.tensor_tensor(rank[:, :, :], rank[:, :, :], base[:, :, :].to_broadcast(TE), ALU.add))
            for i in range(2):
                link(nc.vector.tensor_tensor(off[:, :, :], h[i], rank[:, :, :], ALU.mult))
                link(nc.vector.tensor_reduce(destf[:, i, :], off[:, :, :], AX.X, ALU.add))
            nc.vector.tensor_copy(keep["dest"][:, :, :], destf[:, :, :]).then_inc(dest_done, 1)

        def rank_products(pe):
            pe.wait_ge(hot_done, 1)
            pe.wait_ge(x1_done, 2 * TT)
            nc.tensor.matmul(psP[0][:, 0:TT * NE], c["below"], flat(both), start=True, stop=True).then_inc(ranked, 1)
            nc.tensor.matmul(psP[1][:, 0:TT * NE], c["ones"], flat(both), start=True, stop=True).then_inc(ranked, 1)

        def routing_exps(act):
            act.wait_ge(d_ready, 2)
            nc.scalar.activation(g_exp[:, :, :], g_tmp[:, :, :], ACT.Exp).then_inc(d_exp, 1)
            nc.scalar.activation(e_exp[:, :], e_sum[:, :], ACT.Exp).then_inc(d_exp, 1)

        def routing_constants():
            iota = lambda out, pattern, base, mult: nc.gpsimd.iota(out, pattern, base=base, channel_multiplier=mult,
                                                                   allow_small_or_imprecise_dtypes=True).then_inc(r_const, 1)
            iota(w4[:, 0, :], [[-1, NG]], NG, 0)
            iota(w8[:, 0, :], [[-1, EPG]], EPG, 0)
            iota(thr[:, 0, :], [[BLOCK, TT - 1]], BLOCK, 0)
            iota(tokid[:, :], [[P, TT]], 0, 1)
            iota(filler[:, :], [[0, MAXB + 1]], T, 0)
            nc.gpsimd.memset(zrow[:, :], 0.0).then_inc(r_const, 1)

        def scatter_tokens(pool):
            pool.wait_ge(r_const, 6)
            pool.dma_start(dr["slots"].rearrange("(p b) n -> p (b n)", p=P), filler[:, :]).then_inc(fill_out, 16)
            pool.dma_start(dr["h2"][T:T + 1, :], zrow[:, :]).then_inc(fill_out, 16)
            pool.wait_ge(fill_out, 32)
            pool.wait_ge(dest_done, 1)
            for i in range(2):
                for t in range(TT):
                    nc.gpsimd.indirect_dma_start(out=dr["slots"], out_offset=bass.IndirectOffsetOnAxis(ap=keep["dest"][:, i, t:t + 1], axis=0),
                                                 in_=tokid[:, t:t + 1], in_offset=None).then_inc(slots_out, 16)
            pool.wait_ge(slots_out, 16 * 2 * TT)

        w_up = [io["w_up_a"][0], io["w_up_b"][0]]
        w_out = io["w_out"][0]
        stream = [dr["oa"][i] for i in range(PAIRS)] + [dr["ob"][i] for i in range(PAIRS)]
        stream += [w_out[2 * j * P:(2 * j + 2) * P, n * HALF:(n + 1) * HALF].rearrange("(k p) n -> p k n", p=P)
                   for n in range(2) for j in range(4)]

        with nc.Block() as block:
            @block.sync
            def _(sp):
                def load_raw(g):
                    if g >= RAW:
                        sp.wait_ge(lo, g - RAW + 1)
                    dst = raw[:, g % RAW] if g < 8 else raw[:, g % RAW].rearrange("p (k n) -> p k n", k=2)
                    sp.dma_start(dst, stream[g]).then_inc(raw_in[g % RAW], 16)

                def load_up(f):
                    if f >= URAW:
                        sp.wait_ge(u_split, f - URAW + 1)
                    for i in range(2):
                        sp.dma_start(uraw[:, f % URAW, i * HALF:(i + 1) * HALF].rearrange("p (k n) -> p k n", k=4),
                                     w_up[i][:, f * P:(f + 1) * P].rearrange("(k p) n -> p k n", p=P)).then_inc(uraw_in[f % URAW], 16)

                def load_gates(f, half):
                    n = 2 * f + half
                    if n >= 2:
                        sp.wait_ge(gated, n - 1)
                    for i in range(2):
                        sp.dma_start(gate[:, n % 2, i], dr["gates"][KT * i + f, :, half * HALF:(half + 1) * HALF]).then_inc(gate_in[n % 2], 16)

                load_up(0)
                load_up(1)
                for g in range(8):
                    load_raw(g)
                sp.dma_start(gain[:, :], io["norm_ffn"].to_broadcast([P, D])).then_inc(gain_in, 16)
                sp.wait_ge(wr_zero, 1)
                with nc.allow_non_contiguous_dma(reason="router columns, 144 bytes a row"):
                    sp.dma_start(wr[:, :, 0:NG], io["w_group_router"][0].rearrange("(k p) n -> p k n", p=P)).then_inc(wr_in, 16)
                    sp.dma_start(wr[:, :, NG:NG + NE], io["w_expert_router"][0].rearrange("(k p) n -> p k n", p=P)).then_inc(wr_in, 16)
                sp.dma_start(br[:, 0:NG], io["b_group_router"].to_broadcast([P, NG])).then_inc(wr_in, 16)
                sp.dma_start(br[:, NG:], io["b_expert_router"].to_broadcast([P, NE])).then_inc(wr_in, 16)
                for f in range(KT):
                    for half in range(2):
                        load_gates(f, half)
                    if f >= 1 and f + 1 < KT:
                        load_up(f + 1)
                for g in range(8, 16):
                    load_raw(g)
                sp.wait_ge(gated, 2 * KT)
                for t in range(TT):
                    if t >= 2:
                        sp.wait_ge(x1_out[t % 2], 16 * (t // 2))
                        sp.wait_ge(h2_done, t - 1)
                    sp.dma_start(x1[:, t % 2], io["x"][0, t * P:(t + 1) * P, :]).then_inc(x_in[t % 2], 16)
                    for m in ([t - 1] if t < TT - 1 else [t - 1, t]):
                        if m >= 0:
                            sp.wait_ge(x1_done, 2 * m + 2)
                            sp.dma_start(dr["x1"][m * P:(m + 1) * P, :], x1[:, m % 2]).then_inc(x1_out[m % 2], 16)
                            sp.wait_ge(h2_done, m + 1)
                            sp.dma_start(dr["h2"][m * P:(m + 1) * P, :], hn).then_inc(h2_out, 16)
                for i in range(2):
                    sp.wait_ge(x1_out[i], 16 * TT // 2)
                sp.wait_ge(h2_out, 16 * TT)

            @block.gpsimd
            def _(pool):
                nc.gpsimd.memset(wr[:, :, :], 0.0).then_inc(wr_zero, 1)
                routing_constants()
                for f in range(KT):
                    pool.wait_ge(uraw_in[f % URAW], 32 * (f // URAW + 1))
                    if f >= UR:
                        pool.wait_ge(up, 4 * (f - UR + 1))
                    r = uraw[:, f % URAW, :]
                    h, l = (w[:, f % UR, :] for w in uS)
                    nc.gpsimd.tensor_tensor(h, r, c["ones"][:, 0:1].to_broadcast([P, D]), ALU.mult).then_inc(u_hi, 1)
                    pool.wait_ge(u_hi, f + 1)
                    nc.gpsimd.tensor_tensor(l, r, h.bitcast(F32), ALU.subtract).then_inc(u_split, 1)
                scatter_tokens(pool)

            @block.scalar
            def _(act):
                link = Chain(act, act_step)

                def high(g):
                    act.wait_ge(raw_in[g % RAW], 16 * (g // RAW + 1))
                    if g == 8:
                        act.wait_ge(up, 4 * KT)
                    nc.scalar.copy(oS[0][:, g % 8, :], raw[:, g % RAW, :]).then_inc(hi, 1)
                for g in range(8):
                    high(g)
                for n in range(2 * KT):
                    f, half = divmod(n, 2)
                    act.wait_ge(m_sum, n + 1)
                    nc.scalar.copy(mS[0][:, f, half * HALF:(half + 1) * HALF], ta[:, :]).then_inc(m_hi, 1)
                for g in range(8, 16):
                    high(g)
                act.wait_ge(u_split, KT)
                for t in range(TT):
                    act.wait_ge(x1_done, 2 * t + 2)
                    if t >= 1:
                        act.wait_ge(turned, 2 * t)
                        act.wait_ge(h2_out, 16 * t)
                    nc.scalar.activation(hn, x1[:, t % 2], ACT.Square, accum_out=ssq[:, t:t + 1]).then_inc(ssq_done, 1)
                    act.wait_ge(ssq_done, t + 1)
                    nc.scalar.activation(srt[:, t:t + 1], ssq[:, t:t + 1], ACT.Sqrt, bias=c["eps"], scale=1.0 / D).then_inc(srt_done, 1)
                    for h in range(2):
                        act.wait_ge(turned, 2 * t + h + 1)
                        if t >= 1:
                            act.wait_ge(logits, t)
                        nc.scalar.copy(h2T[:, 4 * h:4 * h + 4, :], psT[h][:, :].rearrange("p (k n) -> p k n", k=4)).then_inc(h2T_done, 1)
                routing_exps(act)

            @block.vector
            def _(dve):
                link = Chain(dve, dve_step)

                def low(g):
                    dve.wait_ge(hi, g + 1)
                    nc.vector.tensor_tensor(oS[1][:, g % 8, :], raw[:, g % RAW, :], oS[0][:, g % 8, :].bitcast(F32), ALU.subtract).then_inc(lo, 1)
                for g in range(8):
                    low(g)
                for n in range(2 * KT):
                    f, half = divmod(n, 2)
                    dve.wait_ge(gate_in[n % 2], 32 * (n // 2 + 1))
                    dve.wait_ge(up, 2 * n + 2)
                    if n >= 1:
                        dve.wait_ge(m_hi, n)
                    link(nc.vector.tensor_tensor(ta[:, :], psP[(2 * n) % 4][:, :], gate[:, n % 2, 0], ALU.mult))
                    nc.vector.tensor_tensor(tb[:, :], psP[(2 * n + 1) % 4][:, :], gate[:, n % 2, 1], ALU.mult).then_inc(gated, 1)
                    dve.wait_ge(gated, n + 1)
                    nc.vector.tensor_tensor(ta[:, :], ta[:, :], tb[:, :], ALU.add).then_inc(m_sum, 1)
                    dve.wait_ge(m_sum, n + 1)
                    dve.wait_ge(m_hi, n + 1)
                    cols = slice(half * HALF, (half + 1) * HALF)
                    nc.vector.tensor_tensor(mS[1][:, f, cols], ta[:, :], mS[0][:, f, cols].bitcast(F32), ALU.subtract).then_inc(m_done, 1)
                    dve.wait_ge(m_done, n + 1)
                for g in range(8, 16):
                    low(g)
                dve.wait_ge(gain_in, 16)
                dve.wait_ge(wr_in, 64)
                for t in range(TT):
                    dve.wait_ge(x_in[t % 2], 16 * (t // 2 + 1))
                    for n in range(2):
                        u = 2 * t + n
                        dve.wait_ge(out, u + 1)
                        v = x1[:, t % 2, n * HALF:(n + 1) * HALF]
                        nc.vector.tensor_tensor(v, v, psP[u % 4][:, :], ALU.add).then_inc(x1_done, 1)
                    dve.wait_ge(x1_done, 2 * t + 2)
                    dve.wait_ge(srt_done, t + 1)
                    refined_rstd(nc, link, rstd[:, t:t + 1], ssq[:, t:t + 1], srt[:, t:t + 1], tmp[:, 0:1], D)
                    nc.vector.scalar_tensor_tensor(hn, x1[:, t % 2], rstd[:, t:t + 1], gain[:, :], ALU.mult, ALU.mult).then_inc(h2_done, 1)
                    if t >= 1:
                        dve.wait_ge(logits, t)
                        nc.vector.tensor_tensor(L[:, t - 1, :], psP[4 + (t - 1) % 2][:, 0:NG + NE], br[:, :], ALU.add).then_inc(L_done, 1)
                dve.wait_ge(logits, TT)
                nc.vector.tensor_tensor(L[:, TT - 1, :], psP[4 + (TT - 1) % 2][:, 0:NG + NE], br[:, :], ALU.add).then_inc(L_done, 1)
                dve.wait_ge(L_done, TT)
                routing(dve, link)

            @block.tensor
            def _(pe):
                for n in range(2 * KT):
                    f, half = divmod(n, 2)
                    if n == 0:
                        pe.wait_ge(lo, 8)
                    pe.wait_ge(u_split, f + 1)
                    for i in range(2):
                        if n >= 2:
                            pe.wait_ge(gated, n - 1)
                        steps = [(k, a, b) for k in range(4) for a, b in PARTS]
                        for j, (k, a, b) in enumerate(steps):
                            ins = nc.tensor.matmul(psP[(2 * n + i) % 4][:, :], uS[a][:, f % UR, i * HALF + k * P:i * HALF + (k + 1) * P],
                                                   oS[b][:, 4 * i + k, half * HALF:(half + 1) * HALF], start=(j == 0), stop=(j == len(steps) - 1))
                        ins.then_inc(up, 1)

                def route(t):
                    pe.wait_ge(h2T_done, 2 * t + 2)
                    if t == 0:
                        pe.wait_ge(wr_in, 64)
                    if t >= 2:
                        pe.wait_ge(L_done, t - 1)
                    for k in range(KT):
                        ins = nc.tensor.matmul(psP[4 + t % 2][:, 0:NR], h2T[:, k, :], wr[:, k, :], start=(k == 0), stop=(k == KT - 1))
                    ins.then_inc(logits, 1)

                def turn(t):
                    pe.wait_ge(h2_done, t + 1)
                    for h in range(2):
                        if t >= 1:
                            pe.wait_ge(h2T_done, 2 * t - 1 + h)
                        for k in range(4):
                            ins = nc.tensor.transpose(psT[h][:, k * P:(k + 1) * P], hn[:, (4 * h + k) * P:(4 * h + k + 1) * P], c["ident"])
                        ins.then_inc(turned, 1)

                pe.wait_ge(m_done, 2 * KT)
                for t in range(TT):
                    for n in range(2):
                        u = 2 * t + n
                        if t == 0:
                            pe.wait_ge(lo, 8 + 4 * (n + 1))
                        if u >= 4:
                            pe.wait_ge(x1_done, u - 3)
                        steps = [(k, a, b) for k in range(KT) for a, b in PARTS]
                        for j, (k, a, b) in enumerate(steps):
                            ins = nc.tensor.matmul(psP[u % 4][:, :], mS[a][:, k, t * P:(t + 1) * P],
                                                   oS[b][:, 4 * n + k // 2, (k % 2) * HALF:(k % 2 + 1) * HALF],
                                                   start=(j == 0), stop=(j == len(steps) - 1))
                        ins.then_inc(out, 1)
                    if t >= 1:
                        turn(t - 1)
                        if t >= 2:
                            route(t - 2)
                turn(TT - 1)
                route(TT - 2)
                route(TT - 1)
                rank_products(pe)


def experts(nc, c, io, dr, keep):
    with ExitStack() as ctx:
        sb = lambda name, shape, dt=F32: ctx.enter_context(nc.sbuf_tensor("e_" + name, shape, dt))
        ps = lambda name, shape: ctx.enter_context(nc.psum_tensor("e_" + name, shape, F32))
        sem = lambda name: ctx.enter_context(nc.semaphore("e_" + name))
        FK = FF // P
        QF = FF // 2
        w1 = [sb(f"w1_{s}", [P, KT, 2 * FF]) for s in range(2)]
        w2 = [sb(f"w2_{s}", [P, FK, D]) for s in range(2)]
        idx = sb("idx", [P, 1], I32)
        xg = sb("xg", [P, D])
        xT = sb("xT", [P, KT, P])
        sil = sb("sil", [P, 2, QF])
        hid = sb("hid", [P, 2, QF])
        hT = sb("hT", [P, FK, P])
        y = sb("y", [P, D])
        psX = [ps(f"psX{i}", [P, HALF]) for i in range(2)]
        psG = [ps(f"psG{i}", [P, HALF]) for i in range(2)]
        psH = ps("psH", [P, HALF])
        psY = [ps(f"psY{i}", [P, HALF]) for i in range(2)]
        w1_in = [[sem(f"w1_in{s}{j}") for j in range(2)] for s in range(2)]
        w2_in = [sem(f"w2_in{s}") for s in range(2)]
        idx_in = sem("idx_in"); held = sem("held"); xg_in = sem("xg_in"); y_out = sem("y_out")
        x_turned = sem("x_turned"); xT_done = sem("xT_done"); ga = sem("ga"); gb = sem("gb")
        silu = sem("silu"); h_done = sem("h_done"); h_turned = sem("h_turned"); hT_done = sem("hT_done")
        y_done = sem("y_done"); y_copied = sem("y_copied")
        rest_out = sem("rest_out")
        nothing = sb("nothing", [P, 1])
        zeros = sb("zeros", [P, D])

        def blocks(eng, e):
            return eng.value_load(keep["cum"][0:1, bass.ds(e, 1)], min_val=0, max_val=MAXB)

        with nc.Block() as block:
            @block.sync
            def _(sp):
                def load(e, s, before):
                    if before is not None:
                        sp.wait_ge(gb, before)
                    for j in range(2):
                        sp.dma_start(w1[s][:, 4 * j:4 * j + 4, :], io["w_expert_in"][0, bass.ds(e, 1), 4 * j * P:(4 * j + 4) * P, :]
                                     .rearrange("o (k p) n -> p (o k) n", p=P)).then_inc(w1_in[s][j], 16)
                    if before is not None:
                        sp.wait_ge(y_done, before)
                    sp.dma_start(w2[s][:, :, :], io["w_expert_out"][0, bass.ds(e, 1)].rearrange("o (k p) n -> p (o k) n", p=P)).then_inc(w2_in[s], 16)
                for s in range(2):
                    load(s, s, None)
                with sp.Fori(1, NE // 2) as i:
                    for s in range(2):
                        load(2 * i + s, s, blocks(sp, 2 * i + s - 1))
                rest = sp.value_load(keep["cum"][0:1, NE + 1:NE + 2], min_val=1, max_val=MAXB)
                sp.wait_ge(h_done, 2)
                with sp.Fori(0, rest) as g:
                    sp.dma_start(dr["ys"][bass.ds((MAXB - 1) * BLOCK - g * BLOCK, BLOCK), :], zeros[:, :]).then_inc(rest_out, 16)
                sp.wait_ge(rest_out, 16 * rest)
                sp.sem_inc(held, 1)

            @block.gpsimd
            def _(pool):
                n = blocks(pool, NE)
                with pool.Fori(0, n + 1) as g:
                    pool.dma_start(idx[:, :], dr["slots"][bass.ds(g * BLOCK, BLOCK), :]).then_inc(idx_in, 16)
                    pool.wait_ge(idx_in, 16 * (g + 1))
                    pool.wait_ge(x_turned, g + 1)
                    pool.sem_inc(held, 1)
                    nc.gpsimd.indirect_dma_start(out=xg[:, :], out_offset=None, in_=dr["h2"],
                                                 in_offset=bass.IndirectOffsetOnAxis(ap=idx[:, 0:1], axis=0)).then_inc(xg_in, 16)
                    pool.wait_ge(xg_in, 16 * (g + 1))

            @block.scalar
            def _(act):
                n = blocks(act, NE)

                def copy_x(g):
                    act.wait_ge(x_turned, g + 2)
                    for h in range(2):
                        nc.scalar.copy(xT[:, 4 * h:4 * h + 4, :], psX[h][:, :].rearrange("p (k n) -> p k n", k=4)).then_inc(xT_done, 1)
                copy_x(0)
                with act.Fori(0, n) as g:
                    for i, done in enumerate((ga, gb)):
                        act.wait_ge(done, g + 1)
                        act.wait_ge(h_done, 2 * g + i + 1)
                        nc.scalar.activation(sil[:, i, :], psG[i][:, 0:QF], ACT.Silu).then_inc(silu, 1)
                    copy_x(g + 1)
                    act.wait_ge(y_copied, g + 2)
                    act.dma_start(dr["ys"][bass.ds(g * BLOCK, BLOCK), :], y[:, :]).then_inc(y_out, 16)
                act.wait_ge(y_out, 16 * n + 16)
                act.sem_inc(held, 1)

            @block.vector
            def _(dve):
                n = blocks(dve, NE)
                nc.vector.memset(zeros[:, :], 0.0).then_inc(h_done, 2)
                dve.wait_ge(h_done, 2)
                nc.vector.memset(nothing[:, :], 0.0).then_inc(y_copied, 1)
                dve.wait_ge(y_copied, 1)
                nc.vector.memset(nothing[:, :], 0.0).then_inc(y_out, 16)
                dve.wait_ge(y_out, 16)
                nc.vector.memset(nothing[:, :], 0.0).then_inc(x_turned, 1)
                with dve.Fori(0, n) as g:
                    for i in range(2):
                        dve.wait_ge(silu, 2 * g + i + 1)
                        nc.vector.tensor_tensor(hid[:, i, :], sil[:, i, :], psG[i][:, QF:2 * QF], ALU.mult).then_inc(h_done, 1)
                        dve.wait_ge(h_turned, 2 * g + i + 1)
                        nc.vector.tensor_copy(hT[:, 2 * i:2 * i + 2, :], psH[:, i * 2 * P:(i + 1) * 2 * P].rearrange("p (k n) -> p k n", k=2)).then_inc(hT_done, 1)
                    dve.wait_ge(y_done, g + 1)
                    dve.wait_ge(y_out, 16 * g + 16)
                    nc.vector.tensor_copy(y[:, 0:HALF], psY[0][:, :])
                    nc.vector.tensor_copy(y[:, HALF:D], psY[1][:, :]).then_inc(y_copied, 1)

            @block.tensor
            def _(pe):
                def turn_x(g):
                    pe.wait_ge(xg_in, 16 * g + 16)
                    for k in range(KT):
                        ins = nc.tensor.transpose(psX[k // 4][:, (k % 4) * P:(k % 4 + 1) * P], xg[:, k * P:(k + 1) * P], c["ident"])
                    ins.then_inc(x_turned, 1)

                def gate_up(g, s, i, round_, done):
                    for k in range(KT):
                        if i == 0 and k % 4 == 0:
                            pe.wait_ge(w1_in[s][k // 4], 16 * round_ + 16)
                        cols = w1[s][:, k, :].rearrange("p (u h n) -> p h u n", u=2, h=2)[:, i]
                        ins = nc.tensor.matmul(psG[i][:, :].rearrange("p (u n) -> p u n", u=2), xT[:, k, :], cols, start=(k == 0), stop=(k == KT - 1))
                    ins.then_inc(done, 1)

                def turn_h(g, i):
                    pe.wait_ge(h_done, 2 * g + i + 3)
                    for k in range(2):
                        ins = nc.tensor.transpose(psH[:, (2 * i + k) * P:(2 * i + k + 1) * P], hid[:, i, k * P:(k + 1) * P], c["ident"])
                    ins.then_inc(h_turned, 1)

                def down(g, s, i, round_):
                    pe.wait_ge(hT_done, 2 * g + i + 1)
                    if i == 0:
                        pe.wait_ge(w2_in[s], 16 * round_ + 16)
                        pe.wait_ge(y_copied, g + 1)
                    for n in range(2):
                        for k in range(2 * i, 2 * i + 2):
                            ins = nc.tensor.matmul(psY[n][:, :], hT[:, k, :], w2[s][:, k, n * HALF:(n + 1) * HALF], start=(k == 0), stop=(k == FK - 1))
                    if i == 1:
                        ins.then_inc(y_done, 1)

                pe.wait_ge(x_turned, 1)
                turn_x(0)
                with pe.Fori(0, NE // 2) as round_:
                    for s in range(2):
                        first = blocks(pe, 2 * round_ + s)
                        end = blocks(pe, 2 * round_ + s + 1)
                        with pe.Fori(first, end) as g:
                            pe.wait_ge(xT_done, 2 * g + 2)
                            gate_up(g, s, 0, round_, ga)
                            gate_up(g, s, 1, round_, gb)
                            turn_h(g, 0)
                            turn_x(g + 1)
                            down(g, s, 0, round_)
                            turn_h(g, 1)
                            down(g, s, 1, round_)


def combine_and_embed(nc, c, io, dr, keep):
    with ExitStack() as ctx:
        sb = lambda name, shape, dt=F32: ctx.enter_context(nc.sbuf_tensor("p_" + name, shape, dt))
        ps = lambda name, shape: ctx.enter_context(nc.psum_tensor("p_" + name, shape, F32))
        sem = lambda name: ctx.enter_context(nc.semaphore("p_" + name))
        PK = PLE // P
        NW = KT + PK
        wS = [sb(f"w{i}", [P, NW, D], F32R) for i in range(2)]
        raw = sb("raw", [P, 2, D])
        xs = sb("xs", [P, 3, D])
        ys = sb("ys", [P, 2, 2, D])
        pt = sb("pt", [P, 2, PLE])
        hn = sb("hn", [P, D])
        sig = sb("sig", [P, D])
        gain = sb("gain", [P, D])
        hS = [sb(f"h{i}", [P, 2, KT, P], F32R) for i in range(2)]
        pS = [sb(f"pe{i}", [P, 2, PK, P], F32R) for i in range(2)]
        ssq = sb("ssq", [P, TT]); srt = sb("srt", [P, TT]); rstd = sb("rstd", [P, TT]); tmp = sb("tmp", [P, TT])
        psT = [ps(f"psT{i}", [P, HALF]) for i in range(2)]
        psQ = ps("psQ", [P, HALF])
        psG = [ps(f"psG{i}", [P, HALF]) for i in range(2)]
        psE = [ps(f"psE{i}", [P, HALF]) for i in range(2)]
        gain_in = sem("gain_in"); raw_in = [sem(f"raw_in{i}") for i in range(2)]
        x_in = [sem(f"x_in{i}") for i in range(3)]; p_in = [sem(f"p_in{i}") for i in range(2)]; y_in = [sem(f"y_in{i}") for i in range(2)]
        w_hi = sem("w_hi"); w_lo = sem("w_lo")
        dve_step = sem("dve_step"); x2_done = sem("x2_done"); ssq_done = sem("ssq_done"); srt_done = sem("srt_done"); hn_done = sem("hn_done")
        turned = sem("turned"); p_turned = sem("p_turned"); h_hi = sem("h_hi"); h_lo = sem("h_lo"); p_hi = sem("p_hi"); p_lo = sem("p_lo")
        gated = sem("gated"); embedded = sem("embedded"); sig_done = sem("sig_done"); e_done = sem("e_done"); o_done = sem("o_done")
        o_out = [sem(f"o_out{i}") for i in range(3)]
        w_gate, w_proj = io["w_ple_gate"][0], io["w_ple_proj"][0]
        rows = lambda a, t: a[t * P:(t + 1) * P, :]

        def granule(g):
            return rows(w_proj, g) if g < PK else rows(w_gate, g - PK)

        with nc.Block() as block:
            @block.sync
            def _(sp):
                sp.dma_start(gain[:, :], io["norm_ple"].to_broadcast([P, D])).then_inc(gain_in, 16)

                def load_tile(t):
                    if t >= 3:
                        sp.wait_ge(o_out[t % 3], 16 * (t // 3))
                    sp.dma_start(xs[:, t % 3], rows(dr["x1"], t)).then_inc(x_in[t % 3], 16)
                    if t >= 2:
                        sp.wait_ge(p_turned, t - 1)
                    sp.dma_start(pt[:, t % 2], rows(io["p"][0, 0], t)).then_inc(p_in[t % 2], 16)
                load_tile(0)
                load_tile(1)
                for g in range(NW):
                    if g >= 2:
                        sp.wait_ge(w_lo, g - 1)
                    sp.dma_start(raw[:, g % 2], granule(g)).then_inc(raw_in[g % 2], 16)
                load_tile(2)
                for t in range(TT):
                    sp.wait_ge(o_done, 2 * t + 2)
                    sp.dma_start(rows(io["out"][0], t), xs[:, t % 3]).then_inc(o_out[t % 3], 16)
                    if t + 3 < TT:
                        load_tile(t + 3)
                for i in range(3):
                    sp.wait_ge(o_out[i], 16 * len(range(i, TT, 3)))

            @block.gpsimd
            def _(pool):
                for t in range(TT):
                    if t >= 2:
                        pool.wait_ge(x2_done, t - 1)
                    for i in range(2):
                        nc.gpsimd.indirect_dma_start(out=ys[:, t % 2, i, :], out_offset=None, in_=dr["ys"],
                                                     in_offset=bass.IndirectOffsetOnAxis(ap=keep["dest"][:, i, t:t + 1], axis=0)).then_inc(y_in[t % 2], 16)

            @block.scalar
            def _(act):
                def square(t):
                    act.wait_ge(x2_done, t + 1)
                    if t >= 1:
                        act.wait_ge(turned, 2 * t)
                    nc.scalar.activation(hn[:, :], xs[:, t % 3], ACT.Square, accum_out=ssq[:, t:t + 1]).then_inc(ssq_done, 1)
                    act.wait_ge(ssq_done, t + 1)
                    nc.scalar.activation(srt[:, t:t + 1], ssq[:, t:t + 1], ACT.Sqrt, bias=c["eps"], scale=1.0 / D).then_inc(srt_done, 1)

                def high(t):
                    act.wait_ge(p_turned, t + 1)
                    if t >= 2:
                        act.wait_ge(embedded, 2 * t - 2)
                    nc.scalar.copy(pS[0][:, t % 2], psQ[:, 0:PK * P].rearrange("p (k n) -> p k n", k=PK)).then_inc(p_hi, 1)
                    for h in range(2):
                        act.wait_ge(turned, 2 * t + h + 1)
                        nc.scalar.copy(hS[0][:, t % 2, 4 * h:4 * h + 4, :], psT[h][:, :].rearrange("p (k n) -> p k n", k=4)).then_inc(h_hi, 1)

                def sigmoid(t):
                    for n in range(2):
                        act.wait_ge(gated, 2 * t + n + 1)
                        if t >= 1:
                            act.wait_ge(o_done, 2 * t)
                        nc.scalar.activation(sig[:, n * HALF:(n + 1) * HALF], psG[n][:, :], ACT.Sigmoid).then_inc(sig_done, 1)
                for g in range(NW):
                    act.wait_ge(raw_in[g % 2], 16 * (g // 2 + 1))
                    nc.scalar.copy(wS[0][:, g, :], raw[:, g % 2]).then_inc(w_hi, 1)
                for t in range(TT + 1):
                    if t < TT:
                        square(t)
                        high(t)
                    if t >= 1:
                        sigmoid(t - 1)

            @block.vector
            def _(dve):
                link = Chain(dve, dve_step)
                dve.wait_ge(gain_in, 16)

                def sum_experts(t):
                    dve.wait_ge(y_in[t % 2], 32 * (t // 2 + 1))
                    dve.wait_ge(x_in[t % 3], 16 * (t // 3 + 1))
                    x = xs[:, t % 3]
                    link(nc.vector.scalar_tensor_tensor(x, ys[:, t % 2, 0, :], keep["w"][:, 0, t:t + 1], x, ALU.mult, ALU.add))
                    nc.vector.scalar_tensor_tensor(x, ys[:, t % 2, 1, :], keep["w"][:, 1, t:t + 1], x, ALU.mult, ALU.add).then_inc(x2_done, 1)

                def norm(t):
                    dve.wait_ge(x2_done, t + 1)
                    dve.wait_ge(srt_done, t + 1)
                    refined_rstd(nc, link, rstd[:, t:t + 1], ssq[:, t:t + 1], srt[:, t:t + 1], tmp[:, 0:1], D)
                    nc.vector.scalar_tensor_tensor(hn[:, :], xs[:, t % 3], rstd[:, t:t + 1], gain[:, :], ALU.mult, ALU.mult).then_inc(hn_done, 1)

                def low(t):
                    dve.wait_ge(p_hi, t + 1)
                    nc.vector.tensor_tensor(pS[1][:, t % 2], psQ[:, 0:PK * P].rearrange("p (k n) -> p k n", k=PK),
                                            pS[0][:, t % 2].bitcast(F32), ALU.subtract).then_inc(p_lo, 1)
                    for h in range(2):
                        dve.wait_ge(h_hi, 2 * t + h + 1)
                        nc.vector.tensor_tensor(hS[1][:, t % 2, 4 * h:4 * h + 4, :], psT[h][:, :].rearrange("p (k n) -> p k n", k=4),
                                                hS[0][:, t % 2, 4 * h:4 * h + 4, :].bitcast(F32), ALU.subtract).then_inc(h_lo, 1)

                def finish(t):
                    for n in range(2):
                        cols = slice(n * HALF, (n + 1) * HALF)
                        dve.wait_ge(sig_done, 2 * t + n + 1)
                        dve.wait_ge(embedded, 2 * t + n + 1)
                        nc.vector.tensor_tensor(sig[:, cols], sig[:, cols], psE[n][:, :], ALU.mult).then_inc(e_done, 1)
                        dve.wait_ge(e_done, 2 * t + n + 1)
                        nc.vector.tensor_tensor(xs[:, t % 3, cols], xs[:, t % 3, cols], sig[:, cols], ALU.add).then_inc(o_done, 1)

                for g in range(NW):
                    dve.wait_ge(w_hi, g + 1)
                    nc.vector.tensor_tensor(wS[1][:, g, :], raw[:, g % 2], wS[0][:, g, :].bitcast(F32), ALU.subtract).then_inc(w_lo, 1)
                sum_experts(0)
                for t in range(TT + 1):
                    if t < TT:
                        norm(t)
                        if t + 1 < TT:
                            sum_experts(t + 1)
                        low(t)
                    if t >= 1:
                        finish(t - 1)

            @block.tensor
            def _(pe):
                def turn(t):
                    pe.wait_ge(p_in[t % 2], 16 * (t // 2 + 1))
                    if t >= 1:
                        pe.wait_ge(p_lo, t)
                    for k in range(PK):
                        ins = nc.tensor.transpose(psQ[:, k * P:(k + 1) * P], pt[:, t % 2, k * P:(k + 1) * P], c["ident"])
                    ins.then_inc(p_turned, 1)
                    pe.wait_ge(hn_done, t + 1)
                    for h in range(2):
                        if t >= 1:
                            pe.wait_ge(h_lo, 2 * t - 1 + h)
                        for k in range(4):
                            ins = nc.tensor.transpose(psT[h][:, k * P:(k + 1) * P], hn[:, (4 * h + k) * P:(4 * h + k + 1) * P], c["ident"])
                        ins.then_inc(turned, 1)

                def product(t, bank, n, parts, weights, kts, g0, done):
                    steps = [(k, a, b) for k in range(kts) for a, b in PARTS]
                    for j, (k, a, b) in enumerate(steps):
                        ins = nc.tensor.matmul(bank[:, :], parts[a][:, t % 2, k, :], weights[b][:, g0 + k, n * HALF:(n + 1) * HALF],
                                               start=(j == 0), stop=(j == len(steps) - 1))
                    ins.then_inc(done, 1)
                turn(0)
                for t in range(TT):
                    pe.wait_ge(p_lo, t + 1)
                    for n in range(2):
                        if t == 0:
                            pe.wait_ge(w_lo, PK)
                        else:
                            pe.wait_ge(e_done, 2 * t - 1 + n)
                        product(t, psE[n], n, pS, wS, PK, 0, embedded)
                    if t + 1 < TT:
                        turn(t + 1)
                    pe.wait_ge(h_lo, 2 * t + 2)
                    for n in range(2):
                        if t == 0:
                            pe.wait_ge(w_lo, NW)
                        else:
                            pe.wait_ge(sig_done, 2 * t - 1 + n)
                        product(t, psG[n], n, hS, wS, KT, PK, gated)


INPUTS = ["x", "p", "norm_mix", "w_in", "q_norm", "k_norm", "sgu_norm", "w_spatial", "b_spatial", "w_up_a", "w_up_b",
          "w_out", "norm_ffn", "w_group_router", "b_group_router", "w_expert_router", "b_expert_router",
          "w_expert_in", "w_expert_out", "norm_ple", "w_ple_gate", "w_ple_proj"]


def trunk_layer(nc, io):
    with ExitStack() as ctx:
        scratch = lambda name, shape, dt=F32: nc.dram_tensor("d_" + name, shape, dt, kind="Internal").ap()
        sb = lambda name, shape, dt=F32: ctx.enter_context(nc.sbuf_tensor("k_" + name, shape, dt))
        dr = {
            "qk": scratch("qk", [2 * PAIRS, P, T]),
            "v": scratch("v", [T, SBW]),
            "ob": scratch("ob", [PAIRS, P, T]),
            "gates": scratch("gates", [2 * KT, P, T]),
            "oa": scratch("oa", [PAIRS, P, T]),
            "x1": scratch("x1", [T, D]),
            "h2": scratch("h2", [T + 1, D]),
            "slots": scratch("slots", [BLOCK * (MAXB + 1), 1], I32),
            "ys": scratch("ys", [BLOCK * MAXB, D]),
        }
        keep = {"w": sb("w", [P, 2, TT]), "dest": sb("dest", [P, 2, TT], I32), "cum": sb("cum", [P, NE + 2], I32)}
        c = constants(nc, ctx)
        mix_projection(nc, c, io, dr)
        attention(nc, c, dr)
        merge_and_route(nc, c, io, dr, keep)
        experts(nc, c, io, dr, keep)
        combine_and_embed(nc, c, io, dr, keep)


def kernel(**inputs):
    import numpy as np
    import concourse.bacc as bacc
    from concourse.bass_utils import run_bass_kernel_spmd

    nc = bacc.Bacc("TRN2", target_bir_lowering=False, num_devices=1)
    arrays = {name: np.ascontiguousarray(inputs[name]) for name in INPUTS}
    io = {name: nc.dram_tensor(name, a.shape, mybir.dt.from_np(a.dtype), kind="ExternalInput").ap() for name, a in arrays.items()}
    io["out"] = nc.dram_tensor("out", [1, T, D], F32, kind="ExternalOutput").ap()
    trunk_layer(nc, io)
    r = run_bass_kernel_spmd(nc, [arrays], core_ids=[0])
    return r.results[0]["out"]
```

```python
from contextlib import ExitStack

import concourse.bass as bass
from concourse import mybir

F32 = mybir.dt.float32
F32R = mybir.dt.float32r
I32 = mybir.dt.int32
U32 = mybir.dt.uint32
ALU = mybir.AluOpType
ACT = mybir.ActivationFunctionType
AX = mybir.AxisListType

P = 128
D = 1024
T = 1024
KT = D // P
TT = T // P
HALF = 512
HEADS, HD = 8, 64
PAIRS = HEADS // 2
SBW = HEADS * HD
GROUPS, GD = 8, 64
NG, EPG = 4, 8
NE = NG * EPG
FF = 512
PLE = 256
EPS = 1e-6
PARTS = ((0, 0), (0, 1), (1, 0))


class Chain:

    def __init__(self, eng, sem):
        self.eng, self.sem, self.n = eng, sem, 0

    def __call__(self, ins):
        self.n += 1
        ins.then_inc(self.sem, 1)
        self.eng.wait_ge(self.sem, self.n)


def constants(nc, ctx):
    sb = lambda name, shape, dt=F32: ctx.enter_context(nc.sbuf_tensor("c_" + name, shape, dt))
    ident = sb("ident", [P, P])
    headones = sb("headones", [P, P])
    ones = sb("ones", [P, P])
    below = sb("below", [P, P])
    causal = sb("causal", [P, P])
    eps = sb("eps", [P, 1])
    with nc.semaphore("c_set") as c_set, nc.semaphore("c_sel") as c_sel, nc.Block() as block:
        @block.gpsimd
        def _(pool):
            nc.gpsimd.memset(ident[:, :], 0.0).then_inc(c_set, 1)
            nc.gpsimd.memset(headones[:, :], 1.0).then_inc(c_set, 1)
            nc.gpsimd.memset(ones[:, :], 1.0).then_inc(c_set, 1)
            nc.gpsimd.memset(eps[:, :], EPS).then_inc(c_set, 1)
            pool.wait_ge(c_set, 4)
            nc.gpsimd.affine_select(out=ident[:, :], in_=ident[:, :], compare_op=ALU.not_equal, fill=1.0, base=0,
                                    pattern=[[-1, P]], channel_multiplier=1).then_inc(c_sel, 1)
            nc.gpsimd.affine_select(out=below[:, :], in_=ones[:, :], compare_op=ALU.is_gt, fill=0.0, base=0,
                                    pattern=[[1, P]], channel_multiplier=-1).then_inc(c_sel, 1)
            nc.gpsimd.affine_select(out=causal[:, :], in_=ones[:, :], compare_op=ALU.is_gt, fill=0.0, base=0,
                                    pattern=[[-1, P]], channel_multiplier=1).then_inc(c_sel, 1)
            nc.gpsimd.affine_select(out=headones[:, 0:HD], in_=headones[:, 0:HD], compare_op=ALU.is_ge, fill=0.0,
                                    base=HD - 1, pattern=[[0, HD]], channel_multiplier=-1).then_inc(c_sel, 1)
            nc.gpsimd.affine_select(out=headones[:, HD:P], in_=headones[:, HD:P], compare_op=ALU.is_ge, fill=0.0,
                                    base=-HD, pattern=[[0, HD]], channel_multiplier=1).then_inc(c_sel, 1)
            pool.wait_ge(c_sel, 5)
    return {"ident": ident[:, :], "headones": headones[:, :], "ones": ones[:, :], "below": below[:, :],
            "causal": causal[:, :], "eps": eps[:, 0:1]}


def refined_rstd(nc, link, out, sumsq, root, tmp, width):
    link(nc.vector.tensor_scalar(tmp, sumsq, 1.0 / width, EPS, ALU.mult, ALU.add))
    link(nc.vector.reciprocal(out, root))
    link(nc.vector.tensor_tensor(tmp, tmp, out, ALU.mult))
    link(nc.vector.tensor_tensor(tmp, tmp, out, ALU.mult))
    link(nc.vector.tensor_scalar(tmp, tmp, -0.5, 1.5, ALU.mult, ALU.add))
    link(nc.vector.tensor_tensor(out, out, tmp, ALU.mult))


def mix_projection(nc, c, io, dr):
    with ExitStack() as ctx:
        sb = lambda name, shape, dt=F32: ctx.enter_context(nc.sbuf_tensor("a_" + name, shape, dt))
        ps = lambda name, shape: ctx.enter_context(nc.psum_tensor("a_" + name, shape, F32))
        sems = []

        @ctx.callback
        def free():
            nc.clear_and_free_semaphores(sems)
            nc.all_engine_barrier()

        def sem(name):
            sems.append(nc.alloc_semaphore("a_" + name))
            return sems[-1]
        XR, RAW, RING, ST = 2, 4, 8, 3
        hT = [sb(f"hT{i}", [P, KT, T], F32R) for i in range(2)]
        wS = [sb(f"w{i}", [P, RING, D], F32R) for i in range(2)]
        raw = sb("raw", [P, RAW, D])
        xt = sb("xt", [P, XR, D])
        hn = sb("hn", [P, D])
        gain = sb("gain", [P, D])
        vs = sb("vs", [P, TT, SBW])
        wT = sb("wT", [P, GROUPS, P])
        bsp = sb("bsp", [P, PAIRS, P])
        sgain = sb("sgain", [P, PAIRS])
        qkgain = sb("qkgain", [P, 2])
        st = sb("st", [P, ST, HALF])
        sq = sb("sq", [P, 2, HALF])
        rt = sb("rt", [P, 2, HALF])
        vv = sb("vv", [P, 2, HALF])
        tmp = sb("tmp", [P, TT])
        ssq = sb("ssq", [P, TT]); srt = sb("srt", [P, TT]); rstd = sb("rstd", [P, TT])
        vss = sb("vss", [P, TT]); vsr = sb("vsr", [P, TT]); vrs = sb("vrs", [P, TT])
        psP = [ps(f"psP{i}", [P, HALF]) for i in range(4)]
        psT = [ps(f"psT{i}", [P, HALF]) for i in range(2)]
        psS = [ps(f"psS{i}", [P, HALF]) for i in range(2)]

        x_in = [sem(f"x_in{i}") for i in range(XR)]; consts_in = sem("consts_in"); wsp_in = sem("wsp_in")
        raw_in = [sem(f"raw_in{i}") for i in range(RAW)]
        w_split = sem("w_split"); w_hi = sem("w_hi")
        ssq_done = sem("ssq_done"); srt_done = sem("srt_done"); dve_step = sem("dve_step")
        hn_done = sem("hn_done"); hn_turned = sem("hn_turned"); hi_done = sem("hi_done"); hT_done = sem("hT_done")
        wmask = sem("wmask"); wt_turned = sem("wt_turned"); wT_done = sem("wT_done")
        proj = sem("proj"); freed = [sem("freed_act"), sem("freed_dve")]
        vs_gelu = sem("vs_gelu"); vs_sq = sem("vs_sq"); vs_rt = sem("vs_rt"); vs_done = sem("vs_done")
        mixed = sem("mixed"); u_gelu = sem("u_gelu"); ob_a = sem("ob_a")
        sq_done = sem("sq_done"); ssum = sem("ssum"); rt_done = sem("rt_done"); vv_done = sem("vv_done")
        staged_a = sem("staged_a"); staged_d = sem("staged_d")
        stored = [sem(f"stored{i}") for i in range(ST)]

        w_in = io["w_in"][0]
        QCOL, KCOL, VCOL, UCOL, VSCOL, GCOL = 0, SBW, 2 * SBW, 3 * SBW, 4 * SBW, 5 * SBW
        granules = [w_in[2 * j * P:(2 * j + 2) * P, col:col + HALF].rearrange("(k p) n -> p k n", p=P)
                    for col in (VSCOL, VCOL) for j in range(4)]
        fcols = [UCOL + P * i for i in range(4)] + [P * i for i in range(8)] + [GCOL + P * i for i in range(16)]
        granules += [w_in[:, col:col + P].rearrange("(k p) n -> p k n", p=P) for col in fcols]
        NGR = len(granules)
        UU, UQ, UG = 16, 24, 40
        NU = UG + 32

        def unit_done_needs(g):
            return 8 * (g // 4 + 1) if g < 8 else 16 + 2 * (g - 8 + 1)

        def unit_owner(n):
            if n < 8 or UU <= n < UQ or n >= UG:
                return 0
            return 1

        def frees_before(n):
            m = n - 4
            who = unit_owner(m)
            return who, sum(unit_owner(i) == who for i in range(m + 1))

        def destination(n):
            if 8 <= n < 16:
                return dr["v"][(n - 8) * P:(n - 7) * P, :]
            i, half = divmod(n - UU, 2)
            cols = slice(half * HALF, (half + 1) * HALF)
            if n < UQ:
                return dr["ob"][i, :, cols]
            if n < UG:
                return dr["qk"][i - 4, :, cols]
            return dr["gates"][i - 12, :, cols]
        stores = list(range(8, NU))

        with nc.Block() as block:
            @block.sync
            def _(sp):
                for i in range(XR):
                    sp.dma_start(xt[:, i], io["x"][0, i * P:(i + 1) * P, :]).then_inc(x_in[i], 16)
                sp.dma_start(gain[:, :], io["norm_mix"].to_broadcast([P, D])).then_inc(consts_in, 16)
                for g in range(RAW):
                    sp.dma_start(raw[:, g].rearrange("p (k n) -> p k n", n=granules[g].shape[-1]), granules[g]).then_inc(raw_in[g], 16)
                with nc.allow_non_contiguous_dma(reason="gains, a few hundred words"):
                    sp.dma_start(sgain[:, :], io["sgu_norm"][0].rearrange("(a p) -> p a", p=P)).then_inc(consts_in, 16)
                    for i, name in enumerate(("q_norm", "k_norm")):
                        for h in range(2):
                            sp.dma_start(qkgain[h * HD:(h + 1) * HD, i:i + 1],
                                         io[name].rearrange("a p -> p a")).then_inc(consts_in, 16)
                for g in range(GROUPS):
                    sp.dma_start(bsp[(g % 2) * GD:(g % 2 + 1) * GD, g // 2, :],
                                 io["b_spatial"][0, g:g + 1, :].to_broadcast([GD, P])).then_inc(consts_in, 16)
                for i in range(XR, TT):
                    sp.wait_ge(ssq_done, i - XR + 1)
                    sp.wait_ge(hn_done, i - XR + 1)
                    sp.dma_start(xt[:, i % XR], io["x"][0, i * P:(i + 1) * P, :]).then_inc(x_in[i % XR], 16)
                sp.wait_ge(ssq_done, TT)
                sp.wait_ge(hn_done, TT)
                sp.dma_start(xt[:, 0].rearrange("p (g s) -> p g s", g=GROUPS),
                             io["w_spatial"][0].rearrange("g t s -> t g s")).then_inc(wsp_in, 16)
                for g in range(RAW, NGR):
                    sp.wait_ge(w_split, g - RAW + 1)
                    sp.dma_start(raw[:, g % RAW].rearrange("p (k n) -> p k n", n=granules[g].shape[-1]),
                                 granules[g]).then_inc(raw_in[g % RAW], 16)

            @block.gpsimd
            def _(pool):
                for g in range(NGR):
                    if g == 6:
                        pool.wait_ge(wsp_in, 16)
                        v = xt[:, 0].rearrange("p (g s) -> p g s", g=GROUPS)
                        nc.gpsimd.affine_select(out=v, in_=v, compare_op=ALU.is_ge, fill=0.0, base=0,
                                                pattern=[[0, GROUPS], [-1, P]], channel_multiplier=1).then_inc(wmask, 1)
                    pool.wait_ge(raw_in[g % RAW], 16 * (g // RAW + 1))
                    if g >= RING:
                        pool.wait_ge(proj, unit_done_needs(g - RING))
                    r = raw[:, g % RAW, :]
                    hi, lo = (w[:, g % RING, :] for w in wS)
                    nc.gpsimd.tensor_tensor(hi, r, c["ones"][:, 0:1].to_broadcast([P, D]), ALU.mult).then_inc(w_hi, 1)
                    pool.wait_ge(w_hi, g + 1)
                    nc.gpsimd.tensor_tensor(lo, r, hi.bitcast(F32), ALU.subtract).then_inc(w_split, 1)

            def staging(eng, n):
                i = stores.index(n)
                if i >= ST:
                    eng.wait_ge(stored[i % ST], 16 * (i // ST))
                return st[:, i % ST, :]

            @block.scalar
            def _(act):
                def store(n):
                    i = stores.index(n)
                    act.wait_ge(staged_a if n >= UG else staged_d, n - UG + 1 if n >= UG else i + 1)
                    act.dma_start(destination(n), st[:, i % ST]).then_inc(stored[i % ST], 16)

                for t in range(TT):
                    act.wait_ge(x_in[t % XR], 16 * (t // XR + 1))
                    if t >= 1:
                        act.wait_ge(hn_done, t)
                        act.wait_ge(hn_turned, 2 * t)
                    nc.scalar.activation(hn[:, :], xt[:, t % XR], ACT.Square, accum_out=ssq[:, t:t + 1]).then_inc(ssq_done, 1)
                    act.wait_ge(ssq_done, t + 1)
                    nc.scalar.activation(srt[:, t:t + 1], ssq[:, t:t + 1], ACT.Sqrt, bias=c["eps"], scale=1.0 / D).then_inc(srt_done, 1)
                    for h in range(2):
                        act.wait_ge(hn_turned, 2 * t + h + 1)
                        nc.scalar.copy(hT[0][:, 4 * h:4 * h + 4, t * P:(t + 1) * P],
                                       psT[h][:, :].rearrange("p (k n) -> p k n", k=4)).then_inc(hi_done, 1)
                for h in range(2):
                    act.wait_ge(wt_turned, h + 1)
                    nc.scalar.copy(wT[:, 4 * h:4 * h + 4, :], psT[h][:, :].rearrange("p (k n) -> p k n", k=4)).then_inc(wT_done, 1)
                for t in range(TT):
                    act.wait_ge(proj, t + 1)
                    nc.scalar.activation(vs[:, t, :], psP[t % 4][:, :], ACT.Gelu_apprx_tanh).then_inc(freed[0], 1)
                    act.wait_ge(freed[0], t + 1)
                    if t == 0:
                        act.wait_ge(hn_turned, 2 * TT)
                    else:
                        act.wait_ge(vs_sq, t)
                    nc.scalar.activation(hn[:, 0:HALF], vs[:, t, :], ACT.Square, accum_out=vss[:, t:t + 1]).then_inc(vs_sq, 1)
                act.wait_ge(vs_sq, TT)
                nc.scalar.activation(vsr[:, :], vss[:, :], ACT.Sqrt, bias=c["eps"], scale=1.0 / SBW).then_inc(vs_rt, 1)
                for n in range(8, UU):
                    store(n)
                for n in range(UU, UQ):
                    act.wait_ge(proj, n + 1)
                    m = n - UU
                    if m >= 2:
                        act.wait_ge(staged_d, 8 + m - 1)
                    nc.scalar.activation(rt[:, m % 2, :], psP[n % 4][:, :], ACT.Gelu_apprx_tanh).then_inc(freed[0], 1)
                    if m >= 1:
                        store(n - 1)
                for n in range(UQ, UG):
                    m = n - UQ
                    act.wait_ge(proj, n + 1)
                    if m >= 2:
                        act.wait_ge(ssum, m - 1)
                    nc.scalar.activation(sq[:, m % 2, :], psP[n % 4][:, :], ACT.Square).then_inc(sq_done, 1)
                    act.wait_ge(ssum, m + 1)
                    act.wait_ge(staged_d, 16 + m - 1 if m >= 2 else 16)
                    nc.scalar.activation(vv[:, m % 2, :], psS[m % 2][:, :], ACT.Identity, bias=c["eps"], scale=1.0 / HD).then_inc(vv_done, 1)
                    nc.scalar.activation(rt[:, m % 2, :], psS[m % 2][:, :], ACT.Sqrt, bias=c["eps"], scale=1.0 / HD).then_inc(rt_done, 1)
                    store(n - 1)
                store(UG - 1)
                for n in range(UG, NU):
                    act.wait_ge(proj, n + 1)
                    out = staging(act, n)
                    nc.scalar.activation(out, psP[n % 4][:, :], ACT.Sigmoid).then_inc(staged_a, 1)
                    store(n)
                for i in range(ST):
                    act.wait_ge(stored[i], 16 * len(range(i, len(stores), ST)))

            @block.vector
            def _(dve):
                link = Chain(dve, dve_step)
                dve.wait_ge(consts_in, 16 * (1 + 1 + 4 + GROUPS))
                link(nc.vector.tensor_scalar(qkgain[:, 0:1], qkgain[:, 0:1], HD ** -0.5, None, ALU.mult))
                for t in range(TT):
                    dve.wait_ge(srt_done, t + 1)
                    refined_rstd(nc, link, rstd[:, t:t + 1], ssq[:, t:t + 1], srt[:, t:t + 1], tmp[:, 0:1], D)
                    nc.vector.scalar_tensor_tensor(hn[:, :], xt[:, t % XR], rstd[:, t:t + 1], gain[:, :],
                                                   ALU.mult, ALU.mult).then_inc(hn_done, 1)
                    for h in range(2):
                        dve.wait_ge(hi_done, 2 * t + h + 1)
                        cols = slice(t * P, (t + 1) * P)
                        nc.vector.tensor_tensor(hT[1][:, 4 * h:4 * h + 4, cols], psT[h][:, :].rearrange("p (k n) -> p k n", k=4),
                                                hT[0][:, 4 * h:4 * h + 4, cols].bitcast(F32), ALU.subtract).then_inc(hT_done, 1)
                for n in range(8, 16):
                    dve.wait_ge(proj, n + 1)
                    out = staging(dve, n)
                    nc.vector.tensor_copy(out, psP[n % 4][:, :]).then_inc(staged_d, 1)
                    if n == 11:
                        dve.wait_ge(vs_rt, 1)
                        refined_rstd(nc, link, vrs[:, :], vss[:, :], vsr[:, :], tmp[:, :], SBW)
                        for t in range(TT):
                            nc.vector.tensor_scalar(vs[:, t, :], vs[:, t, :], vrs[:, t:t + 1], None, ALU.mult).then_inc(vs_done, 1)
                for n in range(UU, UQ):
                    m = n - UU
                    i = m // 2
                    dve.wait_ge(mixed, m + 1)
                    out = staging(dve, n)
                    nc.vector.scalar_tensor_tensor(out.rearrange("p (c t) -> p c t", c=4), psT[m % 2][:, :].rearrange("p (c t) -> p c t", c=4),
                                                   sgain[:, i:i + 1], bsp[:, i:i + 1, :].to_broadcast([P, 4, P]),
                                                   ALU.mult, ALU.add).then_inc(ob_a, 1)
                    dve.wait_ge(ob_a, m + 1)
                    dve.wait_ge(freed[0], 8 + m + 1)
                    nc.vector.tensor_tensor(out, out, rt[:, m % 2, :], ALU.mult).then_inc(staged_d, 1)
                for n in range(UQ, UG):
                    m = n - UQ
                    dve.wait_ge(vv_done, m + 1)
                    dve.wait_ge(rt_done, m + 1)
                    r, v = rt[:, m % 2, :], vv[:, m % 2, :]
                    link(nc.vector.reciprocal(r, r))
                    link(nc.vector.tensor_tensor(v, v, r, ALU.mult))
                    link(nc.vector.tensor_tensor(v, v, r, ALU.mult))
                    link(nc.vector.tensor_scalar(v, v, -0.5, 1.5, ALU.mult, ALU.add))
                    link(nc.vector.tensor_tensor(r, r, v, ALU.mult))
                    out = staging(dve, n)
                    nc.vector.scalar_tensor_tensor(out, psP[n % 4][:, :], qkgain[:, m // 8:m // 8 + 1],
                                                   rt[:, m % 2, :], ALU.mult, ALU.mult).then_inc(staged_d, 1)

            @block.tensor
            def _(pe):
                def turn(src, h, bank):
                    for k in range(4):
                        ins = nc.tensor.transpose(bank[:, k * P:(k + 1) * P], src[:, (4 * h + k) * P:(4 * h + k + 1) * P], c["ident"])
                    return ins
                for t in range(TT):
                    pe.wait_ge(hn_done, t + 1)
                    for h in range(2):
                        if t >= 1:
                            pe.wait_ge(hT_done, 2 * t - 1 + h)
                        turn(hn, h, psT[h]).then_inc(hn_turned, 1)
                pe.wait_ge(wmask, 1)
                for h in range(2):
                    pe.wait_ge(hT_done, 2 * TT)
                    turn(xt[:, 0], h, psT[h]).then_inc(wt_turned, 1)

                def bank_free(n):
                    if n >= 4:
                        m = n - 4
                        if 8 <= m < 16:
                            pe.wait_ge(staged_d, m - 8 + 1)
                        elif m < 8:
                            pe.wait_ge(freed[0], m + 1)
                        elif m < UQ:
                            pe.wait_ge(freed[0], 8 + m - UU + 1)
                        elif m < UG:
                            pe.wait_ge(staged_d, 16 + m - UQ + 1)
                        else:
                            pe.wait_ge(staged_a, m - UG + 1)

                def product(n, operands):
                    bank_free(n)
                    for i, (a, b) in enumerate(operands):
                        ins = nc.tensor.matmul(psP[n % 4][:, :], a, b, start=(i == 0), stop=(i == len(operands) - 1))
                    ins.then_inc(proj, 1)

                for chunk in range(2):
                    for t in range(TT):
                        if chunk == 0 and t == 0:
                            pe.wait_ge(hT_done, 2 * TT)
                        if t == 0:
                            pe.wait_ge(w_split, 4 * chunk + 4)
                        product(8 * chunk + t, [(hT[a][:, k, t * P:(t + 1) * P],
                                                 wS[b][:, 4 * chunk + k // 2, (k % 2) * HALF:(k % 2 + 1) * HALF])
                                                for k in range(KT) for a, b in PARTS])

                def piece(i, half):
                    n = UU + 2 * i + half
                    if half == 0:
                        pe.wait_ge(w_split, 8 + i + 1)
                    s = (8 + i) % RING
                    product(n, [(wS[a][:, s, k * P:(k + 1) * P], hT[b][:, k, half * HALF:(half + 1) * HALF])
                                for k in range(KT) for a, b in PARTS])

                def mix(m):
                    i, half = divmod(m, 2)
                    pe.wait_ge(vs_done, TT)
                    pe.wait_ge(wT_done, 2)
                    if m >= 2:
                        pe.wait_ge(ob_a, m - 1)
                    for ch in range(4):
                        for g in range(2):
                            ins = nc.tensor.matmul(psT[m % 2][g * GD:(g + 1) * GD, ch * P:(ch + 1) * P],
                                                   vs[:, 4 * half + ch, (2 * i + g) * GD:(2 * i + g + 1) * GD],
                                                   wT[:, 2 * i + g, :], start=True, stop=True)
                    ins.then_inc(mixed, 1)

                def sums(m):
                    pe.wait_ge(sq_done, m + 1)
                    if m >= 2:
                        pe.wait_ge(rt_done, m - 1)
                    nc.tensor.matmul(psS[m % 2][:, :], c["headones"], sq[:, m % 2, :], start=True, stop=True).then_inc(ssum, 1)

                for i in range(4):
                    for half in range(2):
                        piece(i, half)
                        mix(2 * i + half)
                for i in range(4, 12):
                    for half in range(2):
                        piece(i, half)
                        m = 2 * (i - 4) + half
                        if m >= 1:
                            sums(m - 1)
                sums(15)
                for i in range(12, 28):
                    for half in range(2):
                        piece(i, half)


def attention(nc, c, dr):
    with ExitStack() as ctx:
        sb = lambda name, shape, dt=F32: ctx.enter_context(nc.sbuf_tensor("b_" + name, shape, dt))
        ps = lambda name, shape: ctx.enter_context(nc.psum_tensor("b_" + name, shape, F32))
        sem = lambda name: ctx.enter_context(nc.semaphore("b_" + name))
        RZ, RE, RL, RK, RA, RT = 3, 3, 4, 5, 2, 3
        LB, SCAN, SUM, EXP, TURN, PV = 1, 2, 2, 3, 4, 6
        hide = sb("hide", [P, P])
        kT = sb("kT", [P, PAIRS, T])
        qT = sb("qT", [P, HEADS, T])
        v = sb("v", [P, TT, SBW])
        z = sb("z", [P, RZ, T])
        e = sb("e", [P, RE, T])
        lb = sb("lb", [P, RL, T])
        lk = sb("lk", [P, RK, T])
        after = sb("after", [P, RA, T + 1])
        aT = sb("aT", [P, RT, T])
        o = sb("o", [P, PAIRS, T])
        psZ = [ps(f"psZ{i}", [P, T]) for i in range(2)]
        psA = [ps(f"psA{i}", [P, HALF]) for i in range(2)]
        psO = [ps(f"psO{i}", [P, P]) for i in range(2)]
        zeros = sb("zeros", [P, 1, D])
        zeroed = sem("zeroed"); qkv_in = [sem(f"qkv_in{i}") for i in range(2)]
        z_done = sem("z_done"); z_copied = sem("z_copied"); act_step = sem("act_step"); l_done = sem("l_done")
        dve_step = sem("dve_step"); lb_done = sem("lb_done"); lk_done = [sem(f"lk_done{i}") for i in range(2)]; scanned = sem("scanned")
        summed = sem("summed"); expd = sem("expd");
        turned = sem("turned"); aT_done = [sem(f"aT_done{i}") for i in range(2)]
        pv_done = sem("pv_done"); o_done = sem("o_done"); o_out = sem("o_out")

        units = [(i, qt, h) for qt in reversed(range(TT)) for i in range(PAIRS) for h in range(2)]
        N = len(units)
        keys = [(u[1] + 1) * P for u in units]
        groups = [(u[1] + 4) // 4 for u in units]
        gsum = [sum(groups[:n]) for n in range(N + 1)]

        SHARE = 3
        by_vector = lambda m: m % SHARE == SHARE - 1
        lk_counts = lambda m: (lk_done[1], m // SHARE + 1) if by_vector(m) else (lk_done[0], m - m // SHARE + 1)

        def keep_log(eng, ns, m):
            S = keys[m]
            eng.wait_ge(lb_done, m + 1)
            if m >= RK:
                eng.wait_ge(turned, gsum[m - RK + 1])
            ns.tensor_tensor(lk[:, m % RK, 0:S], lb[:, m % RL, 0:S], z[:, m % RZ, 0:S], ALU.subtract).then_inc(lk_counts(m)[0], 1)

        def copy_turned(eng, copy, m, which):
            for g in range(groups[m]):
                G = gsum[m] + g
                if G % 2 == which:
                    eng.wait_ge(turned, G + 1)
                    if m >= RT:
                        eng.wait_ge(pv_done, m - RT + 1)
                    w = min(HALF, keys[m] - g * HALF)
                    copy(aT[:, m % RT, g * HALF:g * HALF + w], psA[which][:, 0:w]).then_inc(aT_done[which], 1)

        with nc.Block() as block:
            @block.sync
            def _(sp):
                sp.wait_ge(zeroed, 3)
                for i in range(PAIRS):
                    arrived = qkv_in[min(i, 1)]
                    for h in range(2):
                        rows = slice(h * HD, (h + 1) * HD)
                        sp.dma_start(qT[rows, 2 * i + h, :], dr["qk"][i, rows, :]).then_inc(arrived, 16)
                    sp.dma_start(kT[:, i, :], dr["qk"][PAIRS + i]).then_inc(arrived, 16)
                sp.dma_start(v[:, :, :], dr["v"].rearrange("(t p) n -> p t n", p=P)).then_inc(qkv_in[1], 16)
                sp.dma_start(dr["ys"][NE * BLOCK:, :].rearrange("(b p) n -> p b n", p=P),
                             zeros[:, :, :].to_broadcast([P, MAXB - NE, D])).then_inc(o_out, 16)
                for j in range(TT):
                    cols = slice((TT - 1 - j) * P, (TT - j) * P)
                    sp.wait_ge(o_done, PAIRS * (j + 1))
                    sp.dma_start(dr["oa"].rearrange("i p t -> p i t")[:, :, cols], o[:, :, cols]).then_inc(o_out, 16)
                sp.wait_ge(o_out, 16 * TT + 16)

            @block.gpsimd
            def _(pool):
                nc.gpsimd.memset(zeros[:, :, :], 0.0).then_inc(zeroed, 1)
                pool.wait_ge(zeroed, 1)
                for h in range(2):
                    rows = slice((1 - h) * HD, (2 - h) * HD)
                    nc.gpsimd.memset(qT[rows, h::2, :], 0.0).then_inc(zeroed, 1)
                for n in range(N + SUM):
                    if 0 <= n - LB < N and not by_vector(n - LB):
                        keep_log(pool, nc.gpsimd, n - LB)
                    m = n - SUM
                    if m >= 0:
                        S = keys[m]
                        pool.wait_ge(scanned, m + 1)
                        nc.gpsimd.tensor_tensor(lb[:, m % RL, 0:S], lb[:, m % RL, 0:S], after[:, m % RA, 1:S + 1], ALU.add).then_inc(summed, 1)

            @block.scalar
            def _(act):
                link = Chain(act, act_step)
                nc.scalar.preload_act_table_set("natural_log_exp_and_others")
                for n in range(N + TURN):
                    if n < N:
                        x = e[:, n % RE, 0:keys[n]]
                        act.wait_ge(z_copied, n + 1)
                        if n >= RE:
                            act.wait_ge(lb_done, n - RE + 1)
                        link(nc.scalar.activation(x, z[:, n % RZ, 0:keys[n]], ACT.Abs))
                        link(nc.scalar.activation(x, x, ACT.Exp, scale=-1.0))
                        nc.scalar.activation(x, x, ACT.Ln, bias=1.0).then_inc(l_done, 1)
                    m = n - EXP
                    if 0 <= m < N:
                        act.wait_ge(summed, m + 1)
                        nc.scalar.activation(lk[:, m % RK, 0:keys[m]], lb[:, m % RL, 0:keys[m]], ACT.Exp).then_inc(expd, 1)
                    if n >= TURN:
                        copy_turned(act, nc.scalar.copy, n - TURN, 1)

            @block.vector
            def _(dve):
                link = Chain(dve, dve_step)
                link(nc.vector.memset(after[:, :, :], 0.0))
                link(nc.vector.tensor_scalar(hide[:, :], c["causal"], 1e30, -1e30, ALU.mult, ALU.add))
                for n in range(N + PV + 1):
                    if n < N:
                        S = keys[n]
                        dve.wait_ge(z_done, n + 1)
                        if n >= RZ:
                            dve.wait_ge(*lk_counts(n - RZ))
                        if S > P:
                            nc.vector.tensor_copy(z[:, n % RZ, 0:S - P], psZ[n % 2][:, 0:S - P])
                        nc.vector.tensor_tensor(z[:, n % RZ, S - P:S], psZ[n % 2][:, S - P:S], hide[:, :], ALU.add).then_inc(z_copied, 1)
                    m = n - LB
                    if 0 <= m < N:
                        S = keys[m]
                        dve.wait_ge(l_done, m + 1)
                        if m >= RL:
                            dve.wait_ge(expd, m - RL + 1)
                        nc.vector.scalar_tensor_tensor(lb[:, m % RL, 0:S], z[:, m % RZ, 0:S], 0.0, e[:, m % RE, 0:S],
                                                       ALU.min, ALU.subtract).then_inc(lb_done, 1)
                        if by_vector(m):
                            keep_log(dve, nc.vector, m)
                    m = n - SCAN
                    if 0 <= m < N:
                        S = keys[m]
                        dve.wait_ge(*lk_counts(m))
                        if m >= RA:
                            dve.wait_ge(summed, m - RA + 1)
                        link(nc.vector.memset(after[:, m % RA, S:S + 1], 0.0))
                        nc.vector.tensor_tensor_scan(after[:, m % RA, 0:S][:, ::-1], c["ones"][:, 0:1].to_broadcast([P, S]),
                                                     lk[:, m % RK, 0:S][:, ::-1], 0.0, ALU.mult, ALU.add).then_inc(scanned, 1)
                    if 0 <= n - TURN < N:
                        copy_turned(dve, nc.vector.tensor_copy, n - TURN, 0)
                    m = n - PV - 1
                    if m >= 0 and units[m][2] == 1:
                        i, qt, _ = units[m]
                        dve.wait_ge(pv_done, m + 1)
                        nc.vector.tensor_copy(o[:, i, qt * P:(qt + 1) * P], psO[m // 2 % 2][:, :]).then_inc(o_done, 1)

            @block.tensor
            def _(pe):
                for n in range(N + PV):
                    if n < N:
                        i, qt, h = units[n]
                        if n == 0:
                            pe.wait_ge(qkv_in[0], 48)
                        if n == 2:
                            pe.wait_ge(qkv_in[1], 48 * (PAIRS - 1) + 16)
                        if n >= 2:
                            pe.wait_ge(z_copied, n - 1)
                        for g in range(groups[n]):
                            w = min(HALF, keys[n] - g * HALF)
                            ins = nc.tensor.matmul(psZ[n % 2][:, g * HALF:g * HALF + w], qT[:, 2 * i + h, qt * P:(qt + 1) * P],
                                                   kT[:, i, g * HALF:g * HALF + w], start=True, stop=True)
                        ins.then_inc(z_done, 1)
                    m = n - PV
                    if m >= 0:
                        i, qt, h = units[m]
                        for G in range(gsum[m], gsum[m + 1]):
                            pe.wait_ge(aT_done[G % 2], G // 2 + 1)
                        if h == 0 and m >= 4:
                            pe.wait_ge(o_done, m // 2 - 1)
                        for j in range(qt + 1):
                            ins = nc.tensor.matmul(psO[m // 2 % 2][h * HD:(h + 1) * HD, :], v[:, j, (2 * i + h) * HD:(2 * i + h + 1) * HD],
                                                   aT[:, m % RT, j * P:(j + 1) * P], start=(j == 0), stop=(j == qt))
                        ins.then_inc(pv_done, 1)
                    m = n - TURN
                    if 0 <= m < N:
                        qt = units[m][1]
                        pe.wait_ge(expd, m + 1)
                        for g in range(groups[m]):
                            G = gsum[m] + g
                            if G >= 2:
                                pe.wait_ge(aT_done[G % 2], G // 2)
                            for j in range(4 * g, min(4 * g + 4, qt + 1)):
                                ins = nc.tensor.transpose(psA[G % 2][:, (j % 4) * P:(j % 4 + 1) * P], lk[:, m % RK, j * P:(j + 1) * P], c["ident"])
                            ins.then_inc(turned, 1)


BLOCK = 128
MAXB = T * 2 // BLOCK + NE


def merge_and_route(nc, c, io, dr, keep):
    with ExitStack() as ctx:
        sb = lambda name, shape, dt=F32: ctx.enter_context(nc.sbuf_tensor("m_" + name, shape, dt))
        ps = lambda name, shape: ctx.enter_context(nc.psum_tensor("m_" + name, shape, F32))
        sem = lambda name: ctx.enter_context(nc.semaphore("m_" + name))
        RAW, UR, URAW = 3, 2, 2
        oS = [sb(f"o{i}", [P, 2 * PAIRS, T], F32R) for i in range(2)]
        mS = [sb(f"m{i}", [P, KT, T], F32R) for i in range(2)]
        uS = [sb(f"u{i}", [P, UR, D], F32R) for i in range(2)]
        raw = sb("raw", [P, RAW, D])
        uraw = sb("uraw", [P, URAW, D])
        gate = sb("gate", [P, 2, 2, HALF])
        ta = sb("ta", [P, HALF]); tb = sb("tb", [P, HALF])
        x1 = gate[:, :, :, :].rearrange("p r i n -> p r (i n)")
        h2T = uraw[:, 0, :].rearrange("p (k n) -> p k n", k=KT)
        hn = uraw[:, 1, :]
        gain = sb("gain", [P, D])
        NR = 96
        wr = sb("wr", [P, KT, NR])
        br = sb("br", [P, NG + NE])
        L = sb("L", [P, TT, NG + NE])
        ssq = sb("ssq", [P, TT]); srt = sb("srt", [P, TT]); rstd = sb("rstd", [P, TT]); tmp = sb("tmp", [P, TT])
        psP = [ps(f"psP{i}", [P, HALF]) for i in range(6)]
        psT = [ps(f"psT{i}", [P, HALF]) for i in range(2)]

        gain_in = sem("gain_in"); wr_zero = sem("wr_zero"); wr_in = sem("wr_in")
        raw_in = [sem(f"raw_in{i}") for i in range(RAW)]; uraw_in = [sem(f"uraw_in{i}") for i in range(URAW)]
        gate_in = [sem(f"gate_in{i}") for i in range(2)]; x_in = [sem(f"x_in{i}") for i in range(2)]
        u_hi = sem("u_hi"); u_split = sem("u_split")
        hi = sem("hi"); lo = sem("lo")
        up = sem("up"); dve_step = sem("dve_step"); act_step = sem("act_step"); gated = sem("gated"); m_sum = sem("m_sum"); m_hi = sem("m_hi"); m_done = sem("m_done")
        out = sem("out"); x1_done = sem("x1_done"); ssq_done = sem("ssq_done"); srt_done = sem("srt_done"); h2_done = sem("h2_done")
        turned = sem("turned"); h2T_done = sem("h2T_done"); logits = sem("logits"); L_done = sem("L_done")
        x1_out = [sem(f"x1_out{i}") for i in range(2)]; h2_out = sem("h2_out")

        G8 = [P, TT, NG]; E8 = [P, TT, EPG]; GE = [P, TT, NG, EPG]; TE = [P, TT, NE]
        w4 = sb("w4", [P, 1, NG]); w8 = sb("w8", [P, 1, EPG]); thr = sb("thr", [P, 1, TT - 1])
        tokid = sb("tokid", [P, TT], I32); filler = sb("filler", [P, MAXB + 2], I32); zrow = sb("zrow", [1, D])
        gmax = sb("gmax", [P, TT, 1]); g_oh = sb("g_oh", G8); g_tmp = sb("g_tmp", G8); g_exp = sb("g_exp", G8); g_w = sb("g_w", [P, TT])
        sel4 = sb("sel4", GE); esel = sb("esel", E8); e_tmp = sb("e_tmp", E8); pick = [sb(f"pick{i}", E8) for i in range(2)]
        emax = [sb(f"emax{i}", [P, TT, 1]) for i in range(2)]; e_exp = sb("e_exp", [P, TT]); e_sum = sb("e_sum", [P, TT])
        hot = [sb(f"hot{i}", GE) for i in range(2)]; both = sb("both", TE)
        rank = sb("rank", TE); count = sb("count", TE); off = sb("off", TE); total = sb("total", [P, NE, 1])
        over = sb("over", [P, NE, TT - 1]); nb = sb("nb", [P, NE]); cum = sb("cum", [P, NE + 1]); base = sb("base", [P, 1, NE])
        destf = sb("destf", [P, 2, TT])
        r_const = sem("r_const"); d_ready = sem("d_ready"); d_exp = sem("d_exp"); hot_done = sem("hot_done"); ranked = sem("ranked")
        dest_done = sem("dest_done"); fill_out = sem("fill_out"); slots_out = sem("slots_out")
        flat = lambda a: a[:, :, :].rearrange("p t n -> p (t n)")

        def first_of_max(link, values, out_hot, maximum, weights, tmp3):
            shape = list(values.shape)
            link(nc.vector.tensor_reduce(maximum, values, AX.X, ALU.max))
            link(nc.vector.tensor_tensor(out_hot, values, maximum.to_broadcast(shape), ALU.is_equal))
            link(nc.vector.tensor_tensor(out_hot, out_hot, weights.to_broadcast(shape), ALU.mult))
            link(nc.vector.tensor_reduce(tmp3, out_hot, AX.X, ALU.max))
            link(nc.vector.tensor_tensor(out_hot, out_hot, tmp3.to_broadcast(shape), ALU.is_equal))

        def routing(dve, link):
            dve.wait_ge(r_const, 6)
            t1 = tmp[:, :].rearrange("p (t n) -> p t n", n=1)
            LG = L[:, :, 0:NG]
            LE = L[:, :, NG:].rearrange("p t (g e) -> p t g e", g=NG)
            spread = lambda oh: oh.rearrange("p t (g n) -> p t g n", n=1).to_broadcast(GE)
            first_of_max(link, LG, g_oh[:, :, :], gmax[:, :, :], w4[:, :, :], t1)
            nc.vector.tensor_tensor(g_tmp[:, :, :], LG, gmax[:, :, :].to_broadcast(G8), ALU.subtract).then_inc(d_ready, 1)
            link(nc.vector.tensor_tensor(sel4[:, :, :, :], LE, spread(g_oh[:, :, :]), ALU.mult))
            link(nc.vector.tensor_reduce(esel[:, :, :], sel4[:, :, :, :].rearrange("p t g e -> p t e g"), AX.X, ALU.add))
            first_of_max(link, esel[:, :, :], pick[0][:, :, :], emax[0][:, :, :], w8[:, :, :], t1)
            link(nc.vector.scalar_tensor_tensor(e_tmp[:, :, :], pick[0][:, :, :], -3e38, esel[:, :, :], ALU.mult, ALU.add))
            first_of_max(link, e_tmp[:, :, :], pick[1][:, :, :], emax[1][:, :, :], w8[:, :, :], t1)
            flat1 = lambda a: a[:, :, :].rearrange("p t n -> p (t n)")
            nc.vector.tensor_tensor(e_sum[:, :], flat1(emax[1]), flat1(emax[0]), ALU.subtract).then_inc(d_ready, 1)
            for i in range(2):
                link(nc.vector.tensor_tensor(hot[i][:, :, :, :], spread(g_oh[:, :, :]),
                                             pick[i][:, :, :].rearrange("p t (n e) -> p t n e", n=1).to_broadcast(GE), ALU.mult))
            h = [a[:, :, :, :].rearrange("p t g e -> p t (g e)") for a in hot]
            nc.vector.tensor_tensor(both[:, :, :], h[0], h[1], ALU.add).then_inc(hot_done, 1)
            dve.wait_ge(d_exp, 2)
            link(nc.vector.tensor_reduce(g_w[:, :], g_exp[:, :, :], AX.X, ALU.add))
            link(nc.vector.tensor_scalar(e_sum[:, :], e_exp[:, :], 1.0, None, ALU.add))
            link(nc.vector.tensor_tensor(e_sum[:, :], e_sum[:, :], g_w[:, :], ALU.mult))
            link(nc.vector.reciprocal(keep["w"][:, 0, :], e_sum[:, :]))
            link(nc.vector.tensor_tensor(keep["w"][:, 1, :], keep["w"][:, 0, :], e_exp[:, :], ALU.mult))
            dve.wait_ge(ranked, 2)
            link(nc.vector.tensor_copy(flat(count), psP[1][:, 0:TT * NE]))
            link(nc.vector.memset(off[:, 0, :], 0.0))
            for t in range(1, TT):
                link(nc.vector.tensor_tensor(off[:, t, :], off[:, t - 1, :], count[:, t - 1, :], ALU.add))
            tot = total[:, :, :].rearrange("p e n -> p (e n)")
            link(nc.vector.tensor_tensor(tot, off[:, TT - 1, :], count[:, TT - 1, :], ALU.add))
            link(nc.vector.tensor_tensor(flat(rank), flat(off), psP[0][:, 0:TT * NE], ALU.add))
            link(nc.vector.tensor_tensor(over[:, :, :], total[:, :, :].to_broadcast([P, NE, TT - 1]), thr[:, :, :].to_broadcast([P, NE, TT - 1]), ALU.is_gt))
            link(nc.vector.tensor_reduce(nb[:, :], over[:, :, :], AX.X, ALU.add))
            link(nc.vector.tensor_scalar(nb[:, :], nb[:, :], 1.0, None, ALU.add))
            link(nc.vector.memset(cum[:, 0:1], 0.0))
            link(nc.vector.tensor_tensor_scan(cum[:, 1:NE + 1], c["ones"][:, 0:NE], nb[:, :], 0.0, ALU.mult, ALU.add))
            link(nc.vector.tensor_copy(keep["cum"][:, :], cum[:, :]))
            link(nc.vector.tensor_scalar(keep["last"][:, :], cum[:, 1:NE + 1], -1.0, None, ALU.add))
            link(nc.vector.tensor_scalar(base[:, 0, :], cum[:, 0:NE], float(BLOCK), None, ALU.mult))
            link(nc.vector.tensor_tensor(rank[:, :, :], rank[:, :, :], base[:, :, :].to_broadcast(TE), ALU.add))
            for i in range(2):
                link(nc.vector.tensor_tensor(off[:, :, :], h[i], rank[:, :, :], ALU.mult))
                link(nc.vector.tensor_reduce(destf[:, i, :], off[:, :, :], AX.X, ALU.add))
            nc.vector.tensor_copy(keep["dest"][:, :, :], destf[:, :, :]).then_inc(dest_done, 1)

        def rank_products(pe):
            pe.wait_ge(hot_done, 1)
            pe.wait_ge(x1_done, 2 * TT)
            nc.tensor.matmul(psP[0][:, 0:TT * NE], c["below"], flat(both), start=True, stop=True).then_inc(ranked, 1)
            nc.tensor.matmul(psP[1][:, 0:TT * NE], c["ones"], flat(both), start=True, stop=True).then_inc(ranked, 1)

        def routing_exps(act):
            act.wait_ge(d_ready, 2)
            nc.scalar.activation(g_exp[:, :, :], g_tmp[:, :, :], ACT.Exp).then_inc(d_exp, 1)
            nc.scalar.activation(e_exp[:, :], e_sum[:, :], ACT.Exp).then_inc(d_exp, 1)

        def routing_constants():
            iota = lambda out, pattern, base, mult: nc.gpsimd.iota(out, pattern, base=base, channel_multiplier=mult,
                                                                   allow_small_or_imprecise_dtypes=True).then_inc(r_const, 1)
            iota(w4[:, 0, :], [[-1, NG]], NG, 0)
            iota(w8[:, 0, :], [[-1, EPG]], EPG, 0)
            iota(thr[:, 0, :], [[BLOCK, TT - 1]], BLOCK, 0)
            iota(tokid[:, :], [[P, TT]], 0, 1)
            iota(filler[:, :], [[0, MAXB + 2]], T, 0)
            nc.gpsimd.memset(zrow[:, :], 0.0).then_inc(r_const, 1)

        def scatter_tokens(pool):
            pool.wait_ge(r_const, 6)
            pool.dma_start(dr["slots"].rearrange("(p b) n -> p (b n)", p=P), filler[:, :]).then_inc(fill_out, 16)
            pool.dma_start(dr["h2"][T:T + 1, :], zrow[:, :]).then_inc(fill_out, 16)
            pool.wait_ge(fill_out, 32)
            pool.wait_ge(dest_done, 1)
            for i in range(2):
                for t in range(TT):
                    nc.gpsimd.indirect_dma_start(out=dr["slots"], out_offset=bass.IndirectOffsetOnAxis(ap=keep["dest"][:, i, t:t + 1], axis=0),
                                                 in_=tokid[:, t:t + 1], in_offset=None).then_inc(slots_out, 16)
            pool.wait_ge(slots_out, 16 * 2 * TT)

        w_up = [io["w_up_a"][0], io["w_up_b"][0]]
        w_out = io["w_out"][0]
        stream = [dr["oa"][i] for i in range(PAIRS)] + [dr["ob"][i] for i in range(PAIRS)]
        stream += [w_out[2 * j * P:(2 * j + 2) * P, n * HALF:(n + 1) * HALF].rearrange("(k p) n -> p k n", p=P)
                   for n in range(2) for j in range(4)]

        with nc.Block() as block:
            @block.sync
            def _(sp):
                def load_raw(g):
                    if g >= RAW:
                        sp.wait_ge(lo, g - RAW + 1)
                    dst = raw[:, g % RAW] if g < 8 else raw[:, g % RAW].rearrange("p (k n) -> p k n", k=2)
                    sp.dma_start(dst, stream[g]).then_inc(raw_in[g % RAW], 16)

                def load_up(f):
                    if f >= URAW:
                        sp.wait_ge(u_split, f - URAW + 1)
                    for i in range(2):
                        sp.dma_start(uraw[:, f % URAW, i * HALF:(i + 1) * HALF].rearrange("p (k n) -> p k n", k=4),
                                     w_up[i][:, f * P:(f + 1) * P].rearrange("(k p) n -> p k n", p=P)).then_inc(uraw_in[f % URAW], 16)

                def load_gates(f, half):
                    n = 2 * f + half
                    if n >= 2:
                        sp.wait_ge(gated, n - 1)
                    for i in range(2):
                        sp.dma_start(gate[:, n % 2, i], dr["gates"][KT * i + f, :, half * HALF:(half + 1) * HALF]).then_inc(gate_in[n % 2], 16)

                load_up(0)
                load_up(1)
                for g in range(8):
                    load_raw(g)
                sp.dma_start(gain[:, :], io["norm_ffn"].to_broadcast([P, D])).then_inc(gain_in, 16)
                sp.wait_ge(wr_zero, 1)
                with nc.allow_non_contiguous_dma(reason="router columns, 144 bytes a row"):
                    sp.dma_start(wr[:, :, 0:NG], io["w_group_router"][0].rearrange("(k p) n -> p k n", p=P)).then_inc(wr_in, 16)
                    sp.dma_start(wr[:, :, NG:NG + NE], io["w_expert_router"][0].rearrange("(k p) n -> p k n", p=P)).then_inc(wr_in, 16)
                sp.dma_start(br[:, 0:NG], io["b_group_router"].to_broadcast([P, NG])).then_inc(wr_in, 16)
                sp.dma_start(br[:, NG:], io["b_expert_router"].to_broadcast([P, NE])).then_inc(wr_in, 16)
                for f in range(KT):
                    for half in range(2):
                        load_gates(f, half)
                    if f >= 1 and f + 1 < KT:
                        load_up(f + 1)
                for g in range(8, 16):
                    load_raw(g)
                sp.wait_ge(gated, 2 * KT)
                for t in range(TT):
                    if t >= 2:
                        sp.wait_ge(x1_out[t % 2], 16 * (t // 2))
                        sp.wait_ge(h2_done, t - 1)
                    sp.dma_start(x1[:, t % 2], io["x"][0, t * P:(t + 1) * P, :]).then_inc(x_in[t % 2], 16)
                    for m in ([t - 1] if t < TT - 1 else [t - 1, t]):
                        if m >= 0:
                            sp.wait_ge(x1_done, 2 * m + 2)
                            sp.dma_start(dr["x1"][m * P:(m + 1) * P, :], x1[:, m % 2]).then_inc(x1_out[m % 2], 16)
                            sp.wait_ge(h2_done, m + 1)
                            sp.dma_start(dr["h2"][m * P:(m + 1) * P, :], hn).then_inc(h2_out, 16)
                for i in range(2):
                    sp.wait_ge(x1_out[i], 16 * TT // 2)
                sp.wait_ge(h2_out, 16 * TT)

            @block.gpsimd
            def _(pool):
                nc.gpsimd.memset(wr[:, :, :], 0.0).then_inc(wr_zero, 1)
                routing_constants()
                for f in range(KT):
                    pool.wait_ge(uraw_in[f % URAW], 32 * (f // URAW + 1))
                    if f >= UR:
                        pool.wait_ge(up, 4 * (f - UR + 1))
                    r = uraw[:, f % URAW, :]
                    h, l = (w[:, f % UR, :] for w in uS)
                    nc.gpsimd.tensor_tensor(h, r, c["ones"][:, 0:1].to_broadcast([P, D]), ALU.mult).then_inc(u_hi, 1)
                    pool.wait_ge(u_hi, f + 1)
                    nc.gpsimd.tensor_tensor(l, r, h.bitcast(F32), ALU.subtract).then_inc(u_split, 1)
                scatter_tokens(pool)

            @block.scalar
            def _(act):
                link = Chain(act, act_step)

                def high(g):
                    act.wait_ge(raw_in[g % RAW], 16 * (g // RAW + 1))
                    if g == 8:
                        act.wait_ge(up, 4 * KT)
                    nc.scalar.copy(oS[0][:, g % 8, :], raw[:, g % RAW, :]).then_inc(hi, 1)
                for g in range(8):
                    high(g)
                for n in range(2 * KT):
                    f, half = divmod(n, 2)
                    act.wait_ge(m_sum, n + 1)
                    nc.scalar.copy(mS[0][:, f, half * HALF:(half + 1) * HALF], ta[:, :]).then_inc(m_hi, 1)
                for g in range(8, 16):
                    high(g)
                act.wait_ge(u_split, KT)
                for t in range(TT):
                    act.wait_ge(x1_done, 2 * t + 2)
                    if t >= 1:
                        act.wait_ge(turned, 2 * t)
                        act.wait_ge(h2_out, 16 * t)
                    nc.scalar.activation(hn, x1[:, t % 2], ACT.Square, accum_out=ssq[:, t:t + 1]).then_inc(ssq_done, 1)
                    act.wait_ge(ssq_done, t + 1)
                    nc.scalar.activation(srt[:, t:t + 1], ssq[:, t:t + 1], ACT.Sqrt, bias=c["eps"], scale=1.0 / D).then_inc(srt_done, 1)
                    for h in range(2):
                        act.wait_ge(turned, 2 * t + h + 1)
                        if t >= 1:
                            act.wait_ge(logits, t)
                        nc.scalar.copy(h2T[:, 4 * h:4 * h + 4, :], psT[h][:, :].rearrange("p (k n) -> p k n", k=4)).then_inc(h2T_done, 1)
                routing_exps(act)

            @block.vector
            def _(dve):
                link = Chain(dve, dve_step)

                def low(g):
                    dve.wait_ge(hi, g + 1)
                    nc.vector.tensor_tensor(oS[1][:, g % 8, :], raw[:, g % RAW, :], oS[0][:, g % 8, :].bitcast(F32), ALU.subtract).then_inc(lo, 1)
                for g in range(8):
                    low(g)
                for n in range(2 * KT):
                    f, half = divmod(n, 2)
                    dve.wait_ge(gate_in[n % 2], 32 * (n // 2 + 1))
                    dve.wait_ge(up, 2 * n + 2)
                    if n >= 1:
                        dve.wait_ge(m_hi, n)
                    link(nc.vector.tensor_tensor(ta[:, :], psP[(2 * n) % 4][:, :], gate[:, n % 2, 0], ALU.mult))
                    nc.vector.tensor_tensor(tb[:, :], psP[(2 * n + 1) % 4][:, :], gate[:, n % 2, 1], ALU.mult).then_inc(gated, 1)
                    dve.wait_ge(gated, n + 1)
                    nc.vector.tensor_tensor(ta[:, :], ta[:, :], tb[:, :], ALU.add).then_inc(m_sum, 1)
                    dve.wait_ge(m_sum, n + 1)
                    dve.wait_ge(m_hi, n + 1)
                    cols = slice(half * HALF, (half + 1) * HALF)
                    nc.vector.tensor_tensor(mS[1][:, f, cols], ta[:, :], mS[0][:, f, cols].bitcast(F32), ALU.subtract).then_inc(m_done, 1)
                    dve.wait_ge(m_done, n + 1)
                for g in range(8, 16):
                    low(g)
                dve.wait_ge(gain_in, 16)
                dve.wait_ge(wr_in, 64)
                for t in range(TT):
                    dve.wait_ge(x_in[t % 2], 16 * (t // 2 + 1))
                    for n in range(2):
                        u = 2 * t + n
                        dve.wait_ge(out, u + 1)
                        v = x1[:, t % 2, n * HALF:(n + 1) * HALF]
                        nc.vector.tensor_tensor(v, v, psP[u % 4][:, :], ALU.add).then_inc(x1_done, 1)
                    dve.wait_ge(x1_done, 2 * t + 2)
                    dve.wait_ge(srt_done, t + 1)
                    refined_rstd(nc, link, rstd[:, t:t + 1], ssq[:, t:t + 1], srt[:, t:t + 1], tmp[:, 0:1], D)
                    nc.vector.scalar_tensor_tensor(hn, x1[:, t % 2], rstd[:, t:t + 1], gain[:, :], ALU.mult, ALU.mult).then_inc(h2_done, 1)
                    if t >= 1:
                        dve.wait_ge(logits, t)
                        nc.vector.tensor_tensor(L[:, t - 1, :], psP[4 + (t - 1) % 2][:, 0:NG + NE], br[:, :], ALU.add).then_inc(L_done, 1)
                dve.wait_ge(logits, TT)
                nc.vector.tensor_tensor(L[:, TT - 1, :], psP[4 + (TT - 1) % 2][:, 0:NG + NE], br[:, :], ALU.add).then_inc(L_done, 1)
                dve.wait_ge(L_done, TT)
                routing(dve, link)

            @block.tensor
            def _(pe):
                for n in range(2 * KT):
                    f, half = divmod(n, 2)
                    if n == 0:
                        pe.wait_ge(lo, 8)
                    pe.wait_ge(u_split, f + 1)
                    for i in range(2):
                        if n >= 2:
                            pe.wait_ge(gated, n - 1)
                        steps = [(k, a, b) for k in range(4) for a, b in PARTS]
                        for j, (k, a, b) in enumerate(steps):
                            ins = nc.tensor.matmul(psP[(2 * n + i) % 4][:, :], uS[a][:, f % UR, i * HALF + k * P:i * HALF + (k + 1) * P],
                                                   oS[b][:, 4 * i + k, half * HALF:(half + 1) * HALF], start=(j == 0), stop=(j == len(steps) - 1))
                        ins.then_inc(up, 1)

                def route(t):
                    pe.wait_ge(h2T_done, 2 * t + 2)
                    if t == 0:
                        pe.wait_ge(wr_in, 64)
                    if t >= 2:
                        pe.wait_ge(L_done, t - 1)
                    for k in range(KT):
                        ins = nc.tensor.matmul(psP[4 + t % 2][:, 0:NR], h2T[:, k, :], wr[:, k, :], start=(k == 0), stop=(k == KT - 1))
                    ins.then_inc(logits, 1)

                def turn(t):
                    pe.wait_ge(h2_done, t + 1)
                    for h in range(2):
                        if t >= 1:
                            pe.wait_ge(h2T_done, 2 * t - 1 + h)
                        for k in range(4):
                            ins = nc.tensor.transpose(psT[h][:, k * P:(k + 1) * P], hn[:, (4 * h + k) * P:(4 * h + k + 1) * P], c["ident"])
                        ins.then_inc(turned, 1)

                pe.wait_ge(m_done, 2 * KT)
                for t in range(TT):
                    for n in range(2):
                        u = 2 * t + n
                        if t == 0:
                            pe.wait_ge(lo, 8 + 4 * (n + 1))
                        if u >= 4:
                            pe.wait_ge(x1_done, u - 3)
                        steps = [(k, a, b) for k in range(KT) for a, b in PARTS]
                        for j, (k, a, b) in enumerate(steps):
                            ins = nc.tensor.matmul(psP[u % 4][:, :], mS[a][:, k, t * P:(t + 1) * P],
                                                   oS[b][:, 4 * n + k // 2, (k % 2) * HALF:(k % 2 + 1) * HALF],
                                                   start=(j == 0), stop=(j == len(steps) - 1))
                        ins.then_inc(out, 1)
                    if t >= 1:
                        turn(t - 1)
                        if t >= 2:
                            route(t - 2)
                turn(TT - 1)
                route(TT - 2)
                route(TT - 1)
                rank_products(pe)


def experts(nc, c, io, dr, keep):
    with ExitStack() as ctx:
        sb = lambda name, shape, dt=F32: ctx.enter_context(nc.sbuf_tensor("e_" + name, shape, dt))
        ps = lambda name, shape: ctx.enter_context(nc.psum_tensor("e_" + name, shape, F32))
        sem = lambda name: ctx.enter_context(nc.semaphore("e_" + name))
        FK = FF // P
        NGR = KT + FK
        EARLY = 6
        AHEAD = 2
        PAIR = 2
        raw = sb("raw", [P, NGR, D])
        wS = [sb(f"w{i}", [P, NGR, D], F32R) for i in range(2)]
        idx = sb("idx", [P, 1], I32)
        xg = sb("xg", [P, D])
        xS = [sb(f"x{i}", [P, KT, P], F32R) for i in range(2)]
        sil = sb("sil", [P, FF])
        hid = sb("hid", [P, FF])
        hS = [sb(f"h{i}", [P, FK, P], F32R) for i in range(2)]
        y = sb("y", [P, D])
        nothing = sb("nothing", [P, 1])
        psX = [ps(f"psX{i}", [P, HALF]) for i in range(2)]
        psG = ps("psG", [P, FF])
        psU = ps("psU", [P, FF])
        psH = [ps(f"psH{i}", [P, 2 * P]) for i in range(2)]
        psY = [ps(f"psY{i}", [P, HALF]) for i in range(2)]
        raw_in = [sem(f"raw_in{i}") for i in range(NGR // PAIR)]
        w_hi = sem("w_hi"); w_lo = [sem(f"w_lo{i}") for i in range(2)]; used = sem("used")
        idx_in = sem("idx_in"); held = sem("held"); xg_in = sem("xg_in"); y_out = sem("y_out");
        x_turned = sem("x_turned"); x_hi = sem("x_hi"); x_lo = sem("x_lo"); gate_done = sem("gate_done")
        silu = sem("silu"); h_done = sem("h_done"); h_turned = sem("h_turned"); h_hi = sem("h_hi"); h_lo = sem("h_lo")
        y_copied = sem("y_copied")
        by_vector = [j for j in range(NGR) if j % 3 != 2]
        by_pool = [j for j in range(NGR) if j % 3 == 2]

        def parts_ready(eng, q, j):
            i, maker = (1, by_pool) if j in by_pool else (0, by_vector)
            eng.wait_ge(w_lo[i], len(maker) * q + (maker.index(j) + 1))

        def blocks(eng, e):
            return eng.value_load(keep["cum"][0:1, bass.ds(e, 1)], min_val=0, max_val=MAXB - 1)

        def all_but_last(eng, first, last, body):
            with eng.If(last > first):
                with eng.Fori(first, last) as g:
                    body(g)

        def last_block(eng, e):
            return eng.value_load(keep["last"][0:1, bass.ds(e, 1)], min_val=0, max_val=MAXB - 2)

        with nc.Block() as block:
            @block.sync
            def _(sp):
                def load(e, after_lows_of):
                    for j in range(0, NGR, PAIR):
                        if after_lows_of is not None:
                            if j + PAIR - 1 in by_pool or j in by_pool:
                                parts_ready(sp, after_lows_of, j)
                                sp.sem_inc(held, 1)
                            parts_ready(sp, after_lows_of, j + PAIR - 1)
                        source, k = (io["w_expert_in"], j) if j < KT else (io["w_expert_out"], j - KT)
                        sp.dma_start(raw[:, j:j + PAIR, :], source[0, bass.ds(e, 1), k * P:(k + PAIR) * P, :]
                                     .rearrange("o (k p) n -> p (o k) n", p=P)).then_inc(raw_in[j // PAIR], 16)

                def put_y(g):
                    sp.wait_ge(y_copied, g + 2)
                    sp.dma_start(dr["ys"][bass.ds(g * BLOCK, BLOCK), :], y[:, :]).then_inc(y_out, 16)
                load(0, None)
                load(1, 0)
                with sp.Fori(0, NE - 2) as q:
                    first, last = blocks(sp, q), last_block(sp, q)
                    all_but_last(sp, first, last, put_y)
                    load(q + 2, q + 1)
                    put_y(last)
                n = blocks(sp, NE)
                before_last = blocks(sp, NE - 2)
                with sp.Fori(before_last, n) as g:
                    put_y(g)
                sp.wait_ge(y_out, 16 * n + 16)
                sp.sem_inc(held, 1)

            @block.gpsimd
            def _(pool):
                def load_idx(g):
                    pool.dma_start(idx[:, :], dr["slots"][bass.ds(g * BLOCK, BLOCK), :]).then_inc(idx_in, 16)

                def gather(g):
                    pool.wait_ge(idx_in, 16 * (g + 1))
                    pool.wait_ge(x_turned, g + 1)
                    pool.sem_inc(held, 1)
                    nc.gpsimd.indirect_dma_start(out=xg[:, :], out_offset=None, in_=dr["h2"],
                                                 in_offset=bass.IndirectOffsetOnAxis(ap=idx[:, 0:1], axis=0)).then_inc(xg_in, 16)

                def gathered(g):
                    pool.wait_ge(xg_in, 16 * (g + 1))
                    load_idx(g + 1)

                def plain(g):
                    gather(g + 2)
                    gathered(g + 2)

                def lows(q, js):
                    for j in js:
                        pool.wait_ge(w_hi, NGR * q + j + 1)
                        nc.gpsimd.tensor_tensor(wS[1][:, j], raw[:, j], wS[0][:, j].bitcast(F32), ALU.subtract).then_inc(w_lo[1], 1)
                load_idx(0)
                gather(0)
                gathered(0)
                lows(0, by_pool)
                gather(1)
                gathered(1)
                with pool.Fori(0, NE - 1) as q:
                    first, last = blocks(pool, q), last_block(pool, q)
                    all_but_last(pool, first, last, plain)
                    lows(q + 1, by_pool[:2])
                    gather(last + 2)
                    lows(q + 1, by_pool[2:])
                    gathered(last + 2)
                with pool.Fori(blocks(pool, NE - 1), blocks(pool, NE)) as g:
                    plain(g)
                pool.wait_ge(idx_in, 16 * blocks(pool, NE) + 48)
                pool.sem_inc(held, 1)

            @block.scalar
            def _(act):
                def highs(q, js, before):
                    for j in js:
                        act.wait_ge(raw_in[j // PAIR], 16 * q + 16)
                        if before is not None:
                            act.wait_ge(used, before + (j + 1))
                        nc.scalar.copy(wS[0][:, j], raw[:, j]).then_inc(w_hi, 1)

                def high_x(g):
                    for h in range(2):
                        act.wait_ge(x_turned, g + 2)
                        nc.scalar.copy(xS[0][:, 4 * h:4 * h + 4, :], psX[h][:, :].rearrange("p (k n) -> p k n", k=4)).then_inc(x_hi, 1)

                def hidden(g):
                    for i in range(2):
                        cols = slice(i * 2 * P, (i + 1) * 2 * P)
                        act.wait_ge(gate_done, g + 1)
                        nc.scalar.activation(sil[:, cols], psG[:, cols], ACT.Silu).then_inc(silu, 1)
                    for i in range(2):
                        act.wait_ge(h_turned, 2 * g + i + 1)
                        nc.scalar.copy(hS[0][:, 2 * i:2 * i + 2, :], psH[i][:, :].rearrange("p (k n) -> p k n", k=2)).then_inc(h_hi, 1)

                def plain(g):
                    hidden(g)
                    high_x(g + 1)
                nc.scalar.preload_act_table_set("silu_and_others")
                highs(0, range(NGR), None)
                high_x(0)
                with act.Fori(0, NE - 1) as q:
                    first, last = blocks(act, q), last_block(act, q)
                    all_but_last(act, first, last, plain)
                    before = NGR * last + NGR
                    highs(q + 1, range(0, EARLY), before)
                    plain(last)
                    highs(q + 1, range(EARLY, NGR), before)
                with act.Fori(blocks(act, NE - 1), blocks(act, NE)) as g:
                    plain(g)

            @block.vector
            def _(dve):
                def lows(q, js):
                    for j in js:
                        if j in by_vector:
                            dve.wait_ge(w_hi, NGR * q + j + 1)
                            nc.vector.tensor_tensor(wS[1][:, j], raw[:, j], wS[0][:, j].bitcast(F32), ALU.subtract).then_inc(w_lo[0], 1)

                def low_x(g):
                    for h in range(2):
                        dve.wait_ge(x_hi, 2 * g + h + 1)
                        nc.vector.tensor_tensor(xS[1][:, 4 * h:4 * h + 4, :], psX[h][:, :].rearrange("p (k n) -> p k n", k=4),
                                                xS[0][:, 4 * h:4 * h + 4, :].bitcast(F32), ALU.subtract).then_inc(x_lo, 1)

                def hidden(g):
                    dve.wait_ge(used, NGR * g + (NGR + KT))
                    for i in range(2):
                        cols = slice(i * 2 * P, (i + 1) * 2 * P)
                        dve.wait_ge(silu, 2 * g + i + 1)
                        nc.vector.tensor_tensor(hid[:, cols], sil[:, cols], psU[:, cols], ALU.mult).then_inc(h_done, 1)
                    for i in range(2):
                        dve.wait_ge(h_hi, 2 * g + i + 1)
                        nc.vector.tensor_tensor(hS[1][:, 2 * i:2 * i + 2, :], psH[i][:, :].rearrange("p (k n) -> p k n", k=2),
                                                hS[0][:, 2 * i:2 * i + 2, :].bitcast(F32), ALU.subtract).then_inc(h_lo, 1)

                def take_y(g):
                    dve.wait_ge(used, NGR * g + 2 * NGR)
                    dve.wait_ge(y_out, 16 * g + 16)
                    nc.vector.tensor_copy(y[:, 0:HALF], psY[0][:, :])
                    nc.vector.tensor_copy(y[:, HALF:D], psY[1][:, :]).then_inc(y_copied, 1)

                def plain(g):
                    hidden(g)
                    low_x(g + 1)
                    take_y(g)
                for signal, count in ((h_done, 2), (y_copied, 1), (y_out, 16), (used, NGR), (x_turned, 1)):
                    nc.vector.memset(nothing[:, :], 0.0).then_inc(signal, count)
                    if signal is not x_turned:
                        dve.wait_ge(signal, count)
                lows(0, range(NGR))
                low_x(0)
                with dve.Fori(0, NE - 1) as q:
                    first, last = blocks(dve, q), last_block(dve, q)
                    all_but_last(dve, first, last, plain)
                    lows(q + 1, range(0, EARLY))
                    hidden(last)
                    low_x(last + 1)
                    lows(q + 1, range(EARLY, NGR))
                    take_y(last)
                with dve.Fori(blocks(dve, NE - 1), blocks(dve, NE)) as g:
                    plain(g)

            @block.tensor
            def _(pe):
                def turn_x(g):
                    pe.wait_ge(xg_in, 16 * g + 16)
                    for k in range(KT):
                        ins = nc.tensor.transpose(psX[k // 4][:, (k % 4) * P:(k % 4 + 1) * P], xg[:, k * P:(k + 1) * P], c["ident"])
                    ins.then_inc(x_turned, 1)

                def gate(k):
                    for a, b in PARTS:
                        ins = nc.tensor.matmul(psG[:, :], xS[a][:, k, :], wS[b][:, k, 0:FF], start=(k == 0 and (a, b) == PARTS[0]),
                                               stop=(k == KT - 1 and (a, b) == PARTS[-1]))
                    return ins

                def up(k):
                    for a, b in PARTS:
                        ins = nc.tensor.matmul(psU[:, :], xS[a][:, k, :], wS[b][:, k, FF:2 * FF], start=(k == 0 and (a, b) == PARTS[0]),
                                               stop=(k == KT - 1 and (a, b) == PARTS[-1]))
                    ins.then_inc(used, 1)
                    return ins

                def gate_up(q, g):
                    pe.wait_ge(x_lo, 2 * g + 2)
                    for k in range(KT):
                        parts_ready(pe, q, k)
                        ins = gate(k)
                        if k < KT - AHEAD:
                            up(k)
                    ins.then_inc(gate_done, 1)
                    for k in range(KT - AHEAD, KT):
                        ins = up(k)
                    return ins

                def turn_h(g):
                    for i in range(2):
                        pe.wait_ge(h_done, 2 * g + i + 3)
                        for k in range(2 * i, 2 * i + 2):
                            ins = nc.tensor.transpose(psH[i][:, k % 2 * P:(k % 2 + 1) * P], hid[:, k * P:(k + 1) * P], c["ident"])
                        ins.then_inc(h_turned, 1)

                def down(q, g):
                    pe.wait_ge(y_copied, g + 1)
                    for k in range(FK):
                        if k % 2 == 0:
                            pe.wait_ge(h_lo, 2 * g + k // 2 + 1)
                        parts_ready(pe, q, KT + k)
                        for n in range(2):
                            for a, b in PARTS:
                                ins = nc.tensor.matmul(psY[n][:, :], hS[a][:, k, :], wS[b][:, KT + k, n * HALF:(n + 1) * HALF],
                                                       start=(k == 0 and (a, b) == PARTS[0]), stop=(k == FK - 1 and (a, b) == PARTS[-1]))
                        ins.then_inc(used, 1)

                pe.wait_ge(x_turned, 1)
                turn_x(0)
                with pe.Fori(0, NE) as q:
                    with pe.Fori(blocks(pe, q), blocks(pe, q + 1)) as g:
                        gate_up(q, g)
                        turn_x(g + 1)
                        turn_h(g)
                        down(q, g)


def combine_and_embed(nc, c, io, dr, keep):
    with ExitStack() as ctx:
        sb = lambda name, shape, dt=F32: ctx.enter_context(nc.sbuf_tensor("p_" + name, shape, dt))
        ps = lambda name, shape: ctx.enter_context(nc.psum_tensor("p_" + name, shape, F32))
        sem = lambda name: ctx.enter_context(nc.semaphore("p_" + name))
        PK = PLE // P
        NW = KT + PK
        wS = [sb(f"w{i}", [P, NW, D], F32R) for i in range(2)]
        raw = sb("raw", [P, 2, D])
        xs = sb("xs", [P, 3, D])
        ys = sb("ys", [P, 2, 2, D])
        pt = sb("pt", [P, 2, PLE])
        hn = sb("hn", [P, D])
        sig = sb("sig", [P, D])
        gain = sb("gain", [P, D])
        hS = [sb(f"h{i}", [P, 2, KT, P], F32R) for i in range(2)]
        pS = [sb(f"pe{i}", [P, 2, PK, P], F32R) for i in range(2)]
        ssq = sb("ssq", [P, TT]); srt = sb("srt", [P, TT]); rstd = sb("rstd", [P, TT]); tmp = sb("tmp", [P, TT])
        psT = [ps(f"psT{i}", [P, HALF]) for i in range(2)]
        psQ = ps("psQ", [P, HALF])
        psG = [ps(f"psG{i}", [P, HALF]) for i in range(2)]
        psE = [ps(f"psE{i}", [P, HALF]) for i in range(2)]
        gain_in = sem("gain_in"); raw_in = [sem(f"raw_in{i}") for i in range(2)]
        x_in = [sem(f"x_in{i}") for i in range(3)]; p_in = [sem(f"p_in{i}") for i in range(2)]; y_in = [sem(f"y_in{i}") for i in range(2)]
        w_hi = sem("w_hi"); w_lo = sem("w_lo")
        dve_step = sem("dve_step"); x2_done = sem("x2_done"); ssq_done = sem("ssq_done"); srt_done = sem("srt_done"); hn_done = sem("hn_done")
        turned = sem("turned"); p_turned = sem("p_turned"); h_hi = sem("h_hi"); h_lo = sem("h_lo"); p_hi = sem("p_hi"); p_lo = sem("p_lo")
        gated = sem("gated"); embedded = sem("embedded"); sig_done = sem("sig_done"); e_done = sem("e_done"); o_done = sem("o_done")
        o_out = [sem(f"o_out{i}") for i in range(3)]
        w_gate, w_proj = io["w_ple_gate"][0], io["w_ple_proj"][0]
        rows = lambda a, t: a[t * P:(t + 1) * P, :]

        def granule(g):
            return rows(w_proj, g) if g < PK else rows(w_gate, g - PK)

        with nc.Block() as block:
            @block.sync
            def _(sp):
                sp.dma_start(gain[:, :], io["norm_ple"].to_broadcast([P, D])).then_inc(gain_in, 16)

                def load_tile(t):
                    if t >= 3:
                        sp.wait_ge(o_out[t % 3], 16 * (t // 3))
                    sp.dma_start(xs[:, t % 3], rows(dr["x1"], t)).then_inc(x_in[t % 3], 16)
                    if t >= 2:
                        sp.wait_ge(p_turned, t - 1)
                    sp.dma_start(pt[:, t % 2], rows(io["p"][0, 0], t)).then_inc(p_in[t % 2], 16)
                load_tile(0)
                load_tile(1)
                for g in range(NW):
                    if g >= 2:
                        sp.wait_ge(w_lo, g - 1)
                    sp.dma_start(raw[:, g % 2], granule(g)).then_inc(raw_in[g % 2], 16)
                load_tile(2)
                for t in range(TT):
                    sp.wait_ge(o_done, 2 * t + 2)
                    sp.dma_start(rows(io["out"][0], t), xs[:, t % 3]).then_inc(o_out[t % 3], 16)
                    if t + 3 < TT:
                        load_tile(t + 3)
                for i in range(3):
                    sp.wait_ge(o_out[i], 16 * len(range(i, TT, 3)))

            @block.gpsimd
            def _(pool):
                for t in range(TT):
                    if t >= 2:
                        pool.wait_ge(x2_done, t - 1)
                    for i in range(2):
                        nc.gpsimd.indirect_dma_start(out=ys[:, t % 2, i, :], out_offset=None, in_=dr["ys"],
                                                     in_offset=bass.IndirectOffsetOnAxis(ap=keep["dest"][:, i, t:t + 1], axis=0)).then_inc(y_in[t % 2], 16)

            @block.scalar
            def _(act):
                def square(t):
                    act.wait_ge(x2_done, t + 1)
                    if t >= 1:
                        act.wait_ge(turned, 2 * t)
                    nc.scalar.activation(hn[:, :], xs[:, t % 3], ACT.Square, accum_out=ssq[:, t:t + 1]).then_inc(ssq_done, 1)
                    act.wait_ge(ssq_done, t + 1)
                    nc.scalar.activation(srt[:, t:t + 1], ssq[:, t:t + 1], ACT.Sqrt, bias=c["eps"], scale=1.0 / D).then_inc(srt_done, 1)

                def high(t):
                    act.wait_ge(p_turned, t + 1)
                    if t >= 2:
                        act.wait_ge(embedded, 2 * t - 2)
                    nc.scalar.copy(pS[0][:, t % 2], psQ[:, 0:PK * P].rearrange("p (k n) -> p k n", k=PK)).then_inc(p_hi, 1)
                    for h in range(2):
                        act.wait_ge(turned, 2 * t + h + 1)
                        nc.scalar.copy(hS[0][:, t % 2, 4 * h:4 * h + 4, :], psT[h][:, :].rearrange("p (k n) -> p k n", k=4)).then_inc(h_hi, 1)

                def sigmoid(t):
                    for n in range(2):
                        act.wait_ge(gated, 2 * t + n + 1)
                        if t >= 1:
                            act.wait_ge(o_done, 2 * t)
                        nc.scalar.activation(sig[:, n * HALF:(n + 1) * HALF], psG[n][:, :], ACT.Sigmoid).then_inc(sig_done, 1)
                for g in range(NW):
                    act.wait_ge(raw_in[g % 2], 16 * (g // 2 + 1))
                    nc.scalar.copy(wS[0][:, g, :], raw[:, g % 2]).then_inc(w_hi, 1)
                for t in range(TT + 1):
                    if t < TT:
                        square(t)
                        high(t)
                    if t >= 1:
                        sigmoid(t - 1)

            @block.vector
            def _(dve):
                link = Chain(dve, dve_step)
                dve.wait_ge(gain_in, 16)

                def sum_experts(t):
                    dve.wait_ge(y_in[t % 2], 32 * (t // 2 + 1))
                    dve.wait_ge(x_in[t % 3], 16 * (t // 3 + 1))
                    x = xs[:, t % 3]
                    link(nc.vector.scalar_tensor_tensor(x, ys[:, t % 2, 0, :], keep["w"][:, 0, t:t + 1], x, ALU.mult, ALU.add))
                    nc.vector.scalar_tensor_tensor(x, ys[:, t % 2, 1, :], keep["w"][:, 1, t:t + 1], x, ALU.mult, ALU.add).then_inc(x2_done, 1)

                def norm(t):
                    dve.wait_ge(x2_done, t + 1)
                    dve.wait_ge(srt_done, t + 1)
                    refined_rstd(nc, link, rstd[:, t:t + 1], ssq[:, t:t + 1], srt[:, t:t + 1], tmp[:, 0:1], D)
                    nc.vector.scalar_tensor_tensor(hn[:, :], xs[:, t % 3], rstd[:, t:t + 1], gain[:, :], ALU.mult, ALU.mult).then_inc(hn_done, 1)

                def low(t):
                    dve.wait_ge(p_hi, t + 1)
                    nc.vector.tensor_tensor(pS[1][:, t % 2], psQ[:, 0:PK * P].rearrange("p (k n) -> p k n", k=PK),
                                            pS[0][:, t % 2].bitcast(F32), ALU.subtract).then_inc(p_lo, 1)
                    for h in range(2):
                        dve.wait_ge(h_hi, 2 * t + h + 1)
                        nc.vector.tensor_tensor(hS[1][:, t % 2, 4 * h:4 * h + 4, :], psT[h][:, :].rearrange("p (k n) -> p k n", k=4),
                                                hS[0][:, t % 2, 4 * h:4 * h + 4, :].bitcast(F32), ALU.subtract).then_inc(h_lo, 1)

                def finish(t):
                    for n in range(2):
                        cols = slice(n * HALF, (n + 1) * HALF)
                        dve.wait_ge(sig_done, 2 * t + n + 1)
                        dve.wait_ge(embedded, 2 * t + n + 1)
                        nc.vector.tensor_tensor(sig[:, cols], sig[:, cols], psE[n][:, :], ALU.mult).then_inc(e_done, 1)
                        dve.wait_ge(e_done, 2 * t + n + 1)
                        nc.vector.tensor_tensor(xs[:, t % 3, cols], xs[:, t % 3, cols], sig[:, cols], ALU.add).then_inc(o_done, 1)

                for g in range(NW):
                    dve.wait_ge(w_hi, g + 1)
                    nc.vector.tensor_tensor(wS[1][:, g, :], raw[:, g % 2], wS[0][:, g, :].bitcast(F32), ALU.subtract).then_inc(w_lo, 1)
                sum_experts(0)
                for t in range(TT + 1):
                    if t < TT:
                        norm(t)
                        if t + 1 < TT:
                            sum_experts(t + 1)
                        low(t)
                    if t >= 1:
                        finish(t - 1)

            @block.tensor
            def _(pe):
                def turn(t):
                    pe.wait_ge(p_in[t % 2], 16 * (t // 2 + 1))
                    if t >= 1:
                        pe.wait_ge(p_lo, t)
                    for k in range(PK):
                        ins = nc.tensor.transpose(psQ[:, k * P:(k + 1) * P], pt[:, t % 2, k * P:(k + 1) * P], c["ident"])
                    ins.then_inc(p_turned, 1)
                    pe.wait_ge(hn_done, t + 1)
                    for h in range(2):
                        if t >= 1:
                            pe.wait_ge(h_lo, 2 * t - 1 + h)
                        for k in range(4):
                            ins = nc.tensor.transpose(psT[h][:, k * P:(k + 1) * P], hn[:, (4 * h + k) * P:(4 * h + k + 1) * P], c["ident"])
                        ins.then_inc(turned, 1)

                def product(t, bank, n, parts, weights, kts, g0, done):
                    steps = [(k, a, b) for k in range(kts) for a, b in PARTS]
                    for j, (k, a, b) in enumerate(steps):
                        ins = nc.tensor.matmul(bank[:, :], parts[a][:, t % 2, k, :], weights[b][:, g0 + k, n * HALF:(n + 1) * HALF],
                                               start=(j == 0), stop=(j == len(steps) - 1))
                    ins.then_inc(done, 1)
                turn(0)
                for t in range(TT):
                    pe.wait_ge(p_lo, t + 1)
                    for n in range(2):
                        if t == 0:
                            pe.wait_ge(w_lo, PK)
                        else:
                            pe.wait_ge(e_done, 2 * t - 1 + n)
                        product(t, psE[n], n, pS, wS, PK, 0, embedded)
                    if t + 1 < TT:
                        turn(t + 1)
                    pe.wait_ge(h_lo, 2 * t + 2)
                    for n in range(2):
                        if t == 0:
                            pe.wait_ge(w_lo, NW)
                        else:
                            pe.wait_ge(sig_done, 2 * t - 1 + n)
                        product(t, psG[n], n, hS, wS, KT, PK, gated)


INPUTS = ["x", "p", "norm_mix", "w_in", "q_norm", "k_norm", "sgu_norm", "w_spatial", "b_spatial", "w_up_a", "w_up_b",
          "w_out", "norm_ffn", "w_group_router", "b_group_router", "w_expert_router", "b_expert_router",
          "w_expert_in", "w_expert_out", "norm_ple", "w_ple_gate", "w_ple_proj"]


def trunk_layer(nc, io):
    with ExitStack() as ctx:
        scratch = lambda name, shape, dt=F32: nc.dram_tensor("d_" + name, shape, dt, kind="Internal").ap()
        sb = lambda name, shape, dt=F32: ctx.enter_context(nc.sbuf_tensor("k_" + name, shape, dt))
        dr = {
            "qk": scratch("qk", [2 * PAIRS, P, T]),
            "v": scratch("v", [T, SBW]),
            "ob": scratch("ob", [PAIRS, P, T]),
            "gates": scratch("gates", [2 * KT, P, T]),
            "oa": scratch("oa", [PAIRS, P, T]),
            "x1": scratch("x1", [T, D]),
            "h2": scratch("h2", [T + 1, D]),
            "slots": scratch("slots", [BLOCK * (MAXB + 2), 1], I32),
            "ys": scratch("ys", [BLOCK * MAXB, D]),
        }
        keep = {"w": sb("w", [P, 2, TT]), "dest": sb("dest", [P, 2, TT], I32), "last": sb("last", [P, NE], I32), "cum": sb("cum", [P, NE + 1], I32)}
        c = constants(nc, ctx)
        mix_projection(nc, c, io, dr)
        attention(nc, c, dr)
        merge_and_route(nc, c, io, dr, keep)
        experts(nc, c, io, dr, keep)
        combine_and_embed(nc, c, io, dr, keep)


def kernel(**inputs):
    import numpy as np
    import concourse.bacc as bacc
    from concourse.bass_utils import run_bass_kernel_spmd

    nc = bacc.Bacc("TRN2", target_bir_lowering=False, num_devices=1)
    arrays = {name: np.ascontiguousarray(inputs[name]) for name in INPUTS}
    io = {name: nc.dram_tensor(name, a.shape, mybir.dt.from_np(a.dtype), kind="ExternalInput").ap() for name, a in arrays.items()}
    io["out"] = nc.dram_tensor("out", [1, T, D], F32, kind="ExternalOutput").ap()
    trunk_layer(nc, io)
    r = run_bass_kernel_spmd(nc, [arrays], core_ids=[0])
    return r.results[0]["out"]
```

```python
from contextlib import ExitStack

import concourse.bass as bass
from concourse import mybir

F32 = mybir.dt.float32
F32R = mybir.dt.float32r
I32 = mybir.dt.int32
ALU = mybir.AluOpType
ACT = mybir.ActivationFunctionType
AX = mybir.AxisListType

P = 128
D = 1024
T = 1024
KT = D // P
TT = T // P
HALF = 512
HEADS, HD = 8, 64
PAIRS = HEADS // 2
SBW = HEADS * HD
GROUPS, GD = 8, 64
NG, EPG = 4, 8
NE = NG * EPG
FF = 512
PLE = 256
EPS = 1e-6
PARTS = ((0, 0), (0, 1), (1, 0))


class Chain:

    def __init__(self, eng, sem):
        self.eng, self.sem, self.n = eng, sem, 0

    def __call__(self, ins):
        self.n += 1
        ins.then_inc(self.sem, 1)
        self.eng.wait_ge(self.sem, self.n)


def constants(nc, ctx):
    sb = lambda name, shape, dt=F32: ctx.enter_context(nc.sbuf_tensor("c_" + name, shape, dt))
    ident = sb("ident", [P, P])
    headones = sb("headones", [P, P])
    ones = sb("ones", [P, P])
    below = sb("below", [P, P])
    causal = sb("causal", [P, P])
    eps = sb("eps", [P, 1])
    with nc.semaphore("c_set") as c_set, nc.semaphore("c_sel") as c_sel, nc.Block() as block:
        @block.gpsimd
        def _(pool):
            nc.gpsimd.memset(ident[:, :], 0.0).then_inc(c_set, 1)
            nc.gpsimd.memset(headones[:, :], 1.0).then_inc(c_set, 1)
            nc.gpsimd.memset(ones[:, :], 1.0).then_inc(c_set, 1)
            nc.gpsimd.memset(eps[:, :], EPS).then_inc(c_set, 1)
            pool.wait_ge(c_set, 4)
            nc.gpsimd.affine_select(out=ident[:, :], in_=ident[:, :], compare_op=ALU.not_equal, fill=1.0, base=0,
                                    pattern=[[-1, P]], channel_multiplier=1).then_inc(c_sel, 1)
            nc.gpsimd.affine_select(out=below[:, :], in_=ones[:, :], compare_op=ALU.is_gt, fill=0.0, base=0,
                                    pattern=[[1, P]], channel_multiplier=-1).then_inc(c_sel, 1)
            nc.gpsimd.affine_select(out=causal[:, :], in_=ones[:, :], compare_op=ALU.is_gt, fill=0.0, base=0,
                                    pattern=[[-1, P]], channel_multiplier=1).then_inc(c_sel, 1)
            nc.gpsimd.affine_select(out=headones[:, 0:HD], in_=headones[:, 0:HD], compare_op=ALU.is_ge, fill=0.0,
                                    base=HD - 1, pattern=[[0, HD]], channel_multiplier=-1).then_inc(c_sel, 1)
            nc.gpsimd.affine_select(out=headones[:, HD:P], in_=headones[:, HD:P], compare_op=ALU.is_ge, fill=0.0,
                                    base=-HD, pattern=[[0, HD]], channel_multiplier=1).then_inc(c_sel, 1)
            pool.wait_ge(c_sel, 5)
    return {"ident": ident[:, :], "headones": headones[:, :], "ones": ones[:, :], "below": below[:, :],
            "causal": causal[:, :], "eps": eps[:, 0:1]}


def refined_rstd(nc, link, out, sumsq, root, tmp, width):
    link(nc.vector.tensor_scalar(tmp, sumsq, 1.0 / width, EPS, ALU.mult, ALU.add))
    link(nc.vector.reciprocal(out, root))
    link(nc.vector.tensor_tensor(tmp, tmp, out, ALU.mult))
    link(nc.vector.tensor_tensor(tmp, tmp, out, ALU.mult))
    link(nc.vector.tensor_scalar(tmp, tmp, -0.5, 1.5, ALU.mult, ALU.add))
    link(nc.vector.tensor_tensor(out, out, tmp, ALU.mult))


def mix_projection(nc, c, io, dr):
    with ExitStack() as ctx:
        sb = lambda name, shape, dt=F32: ctx.enter_context(nc.sbuf_tensor("a_" + name, shape, dt))
        ps = lambda name, shape: ctx.enter_context(nc.psum_tensor("a_" + name, shape, F32))
        sems = []

        @ctx.callback
        def free():
            nc.clear_and_free_semaphores(sems)
            nc.all_engine_barrier()

        def sem(name):
            sems.append(nc.alloc_semaphore("a_" + name))
            return sems[-1]
        XR, RAW, RING, ST = 2, 4, 8, 3
        hT = [sb(f"hT{i}", [P, KT, T], F32R) for i in range(2)]
        wS = [sb(f"w{i}", [P, RING, D], F32R) for i in range(2)]
        raw = sb("raw", [P, RAW, D])
        xt = sb("xt", [P, XR, D])
        hn = sb("hn", [P, 2, D])
        gain = sb("gain", [P, D])
        vs = sb("vs", [P, TT, SBW])
        wT = sb("wT", [P, GROUPS, P])
        bsp = sb("bsp", [P, PAIRS, P])
        sgain = sb("sgain", [P, PAIRS])
        qkgain = sb("qkgain", [P, 2])
        st = sb("st", [P, ST, HALF])
        sq = sb("sq", [P, 2, HALF])
        rt = sb("rt", [P, 2, HALF])
        vv = sb("vv", [P, 2, HALF])
        tmp = sb("tmp", [P, TT])
        ssq = sb("ssq", [P, TT]); srt = sb("srt", [P, TT]); rstd = sb("rstd", [P, TT])
        vss = sb("vss", [P, TT]); vsr = sb("vsr", [P, TT]); vrs = sb("vrs", [P, TT])
        psP = [ps(f"psP{i}", [P, HALF]) for i in range(4)]
        psT = [ps(f"psT{i}", [P, HALF]) for i in range(2)]
        psS = [ps(f"psS{i}", [P, HALF]) for i in range(2)]

        x_in = [sem(f"x_in{i}") for i in range(XR)]; gain_in = sem("gain_in"); consts_in = sem("consts_in"); wsp_in = sem("wsp_in")
        raw_in = [sem(f"raw_in{i}") for i in range(RAW)]
        w_split = [sem("w_split_pool"), sem("w_split_dve")]; w_hi = [sem("w_hi_pool"), sem("w_hi_act")]
        ssq_done = sem("ssq_done"); srt_done = sem("srt_done"); dve_step = sem("dve_step")
        hn_done = sem("hn_done"); hn_turned = sem("hn_turned"); hi_done = sem("hi_done"); hT_done = sem("hT_done")
        wmask = sem("wmask"); wt_turned = sem("wt_turned"); wT_done = sem("wT_done")
        proj = sem("proj"); freed = [sem("freed_act"), sem("freed_dve")]
        vs_sq = sem("vs_sq"); vs_rt = sem("vs_rt"); vs_done = sem("vs_done")
        mixed = sem("mixed"); ob_a = sem("ob_a")
        sq_done = sem("sq_done"); ssum = sem("ssum"); rt_done = sem("rt_done"); log_done = sem("log_done"); vv_done = sem("vv_done")
        staged_a = sem("staged_a"); staged_d = sem("staged_d")
        stored = [sem(f"stored{i}") for i in range(ST)]

        w_in = io["w_in"][0]
        QCOL, KCOL, VCOL, UCOL, VSCOL, GCOL = 0, SBW, 2 * SBW, 3 * SBW, 4 * SBW, 5 * SBW
        granules = [w_in[2 * j * P:(2 * j + 2) * P, col:col + HALF].rearrange("(k p) n -> p k n", p=P)
                    for col in (VSCOL, VCOL) for j in range(4)]
        fcols = [UCOL + P * i for i in range(4)] + [P * i for i in range(8)] + [GCOL + P * i for i in range(16)]
        granules += [w_in[:, col:col + P].rearrange("(k p) n -> p k n", p=P) for col in fcols]
        NGR = len(granules)
        UU, UQ, UG = 16, 24, 40
        NU = UG + 32

        def unit_done_needs(g):
            return 8 * (g // 4 + 1) if g < 8 else 16 + 2 * (g - 8 + 1)

        HELPED = (0, 2)

        def split_count(g):
            if g in HELPED:
                return 1, HELPED.index(g) + 1
            return 0, g + 1 - sum(h < g for h in HELPED)

        def split_ready(eng, g):
            who, count = split_count(g)
            eng.wait_ge(w_split[who], count)

        def destination(n):
            if 8 <= n < 16:
                return dr["v"][(n - 8) * P:(n - 7) * P, :]
            i, half = divmod(n - UU, 2)
            cols = slice(half * HALF, (half + 1) * HALF)
            if n < UQ:
                return dr["ob"][i, :, cols]
            if n < UG:
                return dr["qk"][i - 4, :, cols]
            return dr["gates"][i - 12, :, cols]
        stores = list(range(8, NU))

        with nc.Block() as block:
            @block.sync
            def _(sp):
                for i in range(XR):
                    sp.dma_start(xt[:, i], io["x"][0, i * P:(i + 1) * P, :]).then_inc(x_in[i], 16)
                sp.dma_start(gain[:, :], io["norm_mix"].to_broadcast([P, D])).then_inc(gain_in, 16)

                def load_granule(g):
                    if g >= RAW:
                        split_ready(sp, g - RAW)
                    sp.dma_start(raw[:, g % RAW].rearrange("p (k n) -> p k n", n=granules[g].shape[-1]),
                                 granules[g]).then_inc(raw_in[g % RAW], 16)
                for g in range(RAW):
                    load_granule(g)
                with nc.allow_non_contiguous_dma(reason="gains, a few hundred words"):
                    sp.dma_start(sgain[:, :], io["sgu_norm"][0].rearrange("(a p) -> p a", p=P)).then_inc(consts_in, 16)
                    for i, name in enumerate(("q_norm", "k_norm")):
                        for h in range(2):
                            sp.dma_start(qkgain[h * HD:(h + 1) * HD, i:i + 1],
                                         io[name].rearrange("a p -> p a")).then_inc(consts_in, 16)
                for g in range(GROUPS):
                    sp.dma_start(bsp[(g % 2) * GD:(g % 2 + 1) * GD, g // 2, :],
                                 io["b_spatial"][0, g:g + 1, :].to_broadcast([GD, P])).then_inc(consts_in, 16)
                for i in range(XR, TT):
                    sp.wait_ge(ssq_done, i - XR + 1)
                    sp.wait_ge(hn_done, i - XR + 1)
                    sp.dma_start(xt[:, i % XR], io["x"][0, i * P:(i + 1) * P, :]).then_inc(x_in[i % XR], 16)
                    if i < XR + RING - RAW:
                        load_granule(RAW + i - XR)
                sp.wait_ge(ssq_done, TT)
                sp.wait_ge(hn_done, TT)
                sp.dma_start(xt[:, 0].rearrange("p (g s) -> p g s", g=GROUPS),
                             io["w_spatial"][0].rearrange("g t s -> t g s")).then_inc(wsp_in, 16)
                for g in range(RING, NGR):
                    load_granule(g)

            @block.gpsimd
            def _(pool):
                for g in range(NGR):
                    if g == 8:
                        pool.wait_ge(wsp_in, 16)
                        v = xt[:, 0].rearrange("p (g s) -> p g s", g=GROUPS)
                        nc.gpsimd.affine_select(out=v, in_=v, compare_op=ALU.is_ge, fill=0.0, base=0,
                                                pattern=[[0, GROUPS], [-1, P]], channel_multiplier=1).then_inc(wmask, 1)
                    if g in HELPED:
                        continue
                    pool.wait_ge(raw_in[g % RAW], 16 * (g // RAW + 1))
                    if g >= RING:
                        pool.wait_ge(proj, unit_done_needs(g - RING))
                    r = raw[:, g % RAW, :]
                    hi, lo = (w[:, g % RING, :] for w in wS)
                    nc.gpsimd.tensor_tensor(hi, r, c["ones"][:, 0:1].to_broadcast([P, D]), ALU.mult).then_inc(w_hi[0], 1)
                    pool.wait_ge(w_hi[0], split_count(g)[1])
                    nc.gpsimd.tensor_tensor(lo, r, hi.bitcast(F32), ALU.subtract).then_inc(w_split[0], 1)

            def staging(eng, n):
                i = stores.index(n)
                if i >= ST:
                    eng.wait_ge(stored[i % ST], 16 * (i // ST))
                return st[:, i % ST, :]

            @block.scalar
            def _(act):
                def store(n):
                    i = stores.index(n)
                    act.wait_ge(staged_a if n >= UG else staged_d, n - UG + 1 if n >= UG else i + 1)
                    act.dma_start(destination(n), st[:, i % ST]).then_inc(stored[i % ST], 16)

                def square(t):
                    act.wait_ge(x_in[t % XR], 16 * (t // XR + 1))
                    if t >= 1:
                        act.wait_ge(ssq_done, t)
                    nc.scalar.activation(sq[:, :, :].rearrange("p i n -> p (i n)"), xt[:, t % XR], ACT.Square, accum_out=ssq[:, t:t + 1]).then_inc(ssq_done, 1)
                    act.wait_ge(ssq_done, t + 1)
                    nc.scalar.activation(srt[:, t:t + 1], ssq[:, t:t + 1], ACT.Sqrt, bias=c["eps"], scale=1.0 / D).then_inc(srt_done, 1)

                def gelu_vs(t):
                    act.wait_ge(proj, t + 1)
                    nc.scalar.activation(vs[:, t, :], psP[t % 4][:, :], ACT.Gelu_apprx_tanh).then_inc(freed[0], 1)

                def square_vs(t):
                    act.wait_ge(freed[0], t + 1)
                    if t >= 1:
                        act.wait_ge(vs_sq, t)
                    nc.scalar.activation(vv[:, 0, :], vs[:, t, :], ACT.Square, accum_out=vss[:, t:t + 1]).then_inc(vs_sq, 1)

                square(0)
                for g in HELPED:
                    act.wait_ge(raw_in[g], 16)
                    nc.scalar.copy(wS[0][:, g, :], raw[:, g, :]).then_inc(w_hi[1], 1)
                for t in range(TT + 1):
                    if t + 1 < TT:
                        square(t + 1)
                    if t < TT:
                        for h in range(2):
                            act.wait_ge(hn_turned, 2 * t + h + 1)
                            nc.scalar.copy(hT[0][:, 4 * h:4 * h + 4, t * P:(t + 1) * P],
                                           psT[h][:, :].rearrange("p (k n) -> p k n", k=4)).then_inc(hi_done, 1)
                    if t >= 1:
                        gelu_vs(t - 1)
                for h in range(2):
                    act.wait_ge(wt_turned, h + 1)
                    nc.scalar.copy(wT[:, 4 * h:4 * h + 4, :], psT[h][:, :].rearrange("p (k n) -> p k n", k=4)).then_inc(wT_done, 1)
                for t in range(TT):
                    square_vs(t)
                act.wait_ge(vs_sq, TT)
                nc.scalar.activation(vsr[:, :], vss[:, :], ACT.Sqrt, bias=c["eps"], scale=1.0 / SBW).then_inc(vs_rt, 1)
                for n in range(8, UU):
                    store(n)
                for n in range(UU, UQ):
                    act.wait_ge(proj, n + 1)
                    m = n - UU
                    if m >= 2:
                        act.wait_ge(staged_d, 8 + m - 1)
                    nc.scalar.activation(rt[:, m % 2, :], psP[n % 4][:, :], ACT.Gelu_apprx_tanh).then_inc(freed[0], 1)
                    if m >= 1:
                        store(n - 1)
                nc.scalar.preload_act_table_set("natural_log_exp_and_others")
                for n in range(UQ, UG):
                    m = n - UQ
                    act.wait_ge(proj, n + 1)
                    if m >= 2:
                        act.wait_ge(ssum, m - 1)
                    nc.scalar.activation(sq[:, m % 2, :], psP[n % 4][:, :], ACT.Square).then_inc(sq_done, 1)
                    act.wait_ge(ssum, m + 1)
                    act.wait_ge(staged_d, 16 + m - 1 if m >= 2 else 16)
                    nc.scalar.activation(vv[:, m % 2, :], psS[m % 2][:, :], ACT.Identity, bias=c["eps"], scale=1.0 / HD).then_inc(vv_done, 1)
                    nc.scalar.activation(rt[:, m % 2, :], psS[m % 2][:, :], ACT.Ln, bias=c["eps"], scale=1.0 / HD).then_inc(log_done, 1)
                    act.wait_ge(log_done, m + 1)
                    nc.scalar.activation(rt[:, m % 2, :], rt[:, m % 2, :], ACT.Exp, scale=-0.5).then_inc(rt_done, 1)
                    store(n - 1)
                store(UG - 1)
                for n in range(UG, NU):
                    act.wait_ge(proj, n + 1)
                    out = staging(act, n)
                    nc.scalar.activation(out, psP[n % 4][:, :], ACT.Sigmoid).then_inc(staged_a, 1)
                    store(n)
                for i in range(ST):
                    act.wait_ge(stored[i], 16 * len(range(i, len(stores), ST)))

            @block.vector
            def _(dve):
                link = Chain(dve, dve_step)
                dve.wait_ge(gain_in, 16)
                def norm(t):
                    dve.wait_ge(srt_done, t + 1)
                    refined_rstd(nc, link, rstd[:, t:t + 1], ssq[:, t:t + 1], srt[:, t:t + 1], tmp[:, 0:1], D)
                    if t >= 2:
                        dve.wait_ge(hn_turned, 2 * t - 2)
                    nc.vector.scalar_tensor_tensor(hn[:, t % 2, :], xt[:, t % XR], rstd[:, t:t + 1], gain[:, :],
                                                   ALU.mult, ALU.mult).then_inc(hn_done, 1)

                norm(0)
                for g in HELPED:
                    dve.wait_ge(w_hi[1], split_count(g)[1])
                    nc.vector.tensor_tensor(wS[1][:, g, :], raw[:, g, :], wS[0][:, g, :].bitcast(F32), ALU.subtract).then_inc(w_split[1], 1)
                for t in range(TT):
                    if t + 1 < TT:
                        norm(t + 1)
                    for h in range(2):
                        dve.wait_ge(hi_done, 2 * t + h + 1)
                        cols = slice(t * P, (t + 1) * P)
                        nc.vector.tensor_tensor(hT[1][:, 4 * h:4 * h + 4, cols], psT[h][:, :].rearrange("p (k n) -> p k n", k=4),
                                                hT[0][:, 4 * h:4 * h + 4, cols].bitcast(F32), ALU.subtract).then_inc(hT_done, 1)
                for n in range(8, 16):
                    dve.wait_ge(proj, n + 1)
                    out = staging(dve, n)
                    nc.vector.tensor_copy(out, psP[n % 4][:, :]).then_inc(staged_d, 1)
                    if n == 11:
                        dve.wait_ge(vs_rt, 1)
                        refined_rstd(nc, link, vrs[:, :], vss[:, :], vsr[:, :], tmp[:, :], SBW)
                        for t in range(TT):
                            nc.vector.tensor_scalar(vs[:, t, :], vs[:, t, :], vrs[:, t:t + 1], None, ALU.mult).then_inc(vs_done, 1)
                dve.wait_ge(consts_in, 16 * (1 + 4 + GROUPS))
                link(nc.vector.tensor_scalar(qkgain[:, 0:1], qkgain[:, 0:1], HD ** -0.5, None, ALU.mult))
                for n in range(UU, UQ):
                    m = n - UU
                    i = m // 2
                    dve.wait_ge(mixed, m + 1)
                    out = staging(dve, n)
                    nc.vector.scalar_tensor_tensor(out.rearrange("p (c t) -> p c t", c=4), psT[m % 2][:, :].rearrange("p (c t) -> p c t", c=4),
                                                   sgain[:, i:i + 1], bsp[:, i:i + 1, :].to_broadcast([P, 4, P]),
                                                   ALU.mult, ALU.add).then_inc(ob_a, 1)
                    dve.wait_ge(ob_a, m + 1)
                    dve.wait_ge(freed[0], 8 + m + 1)
                    nc.vector.tensor_tensor(out, out, rt[:, m % 2, :], ALU.mult).then_inc(staged_d, 1)
                for n in range(UQ, UG):
                    m = n - UQ
                    dve.wait_ge(vv_done, m + 1)
                    dve.wait_ge(rt_done, m + 1)
                    r, v = rt[:, m % 2, :], vv[:, m % 2, :]
                    link(nc.vector.tensor_tensor(v, v, r, ALU.mult))
                    link(nc.vector.tensor_tensor(v, v, r, ALU.mult))
                    link(nc.vector.tensor_scalar(v, v, -0.5, 1.5, ALU.mult, ALU.add))
                    link(nc.vector.tensor_tensor(r, r, v, ALU.mult))
                    out = staging(dve, n)
                    nc.vector.scalar_tensor_tensor(out, psP[n % 4][:, :], qkgain[:, m // 8:m // 8 + 1],
                                                   rt[:, m % 2, :], ALU.mult, ALU.mult).then_inc(staged_d, 1)

            @block.tensor
            def _(pe):
                def turn(src, h, bank):
                    for k in range(4):
                        ins = nc.tensor.transpose(bank[:, k * P:(k + 1) * P], src[:, (4 * h + k) * P:(4 * h + k + 1) * P], c["ident"])
                    return ins

                def turn_hn(t):
                    pe.wait_ge(hn_done, t + 1)
                    for h in range(2):
                        if t >= 1:
                            pe.wait_ge(hT_done, 2 * t - 1 + h)
                        turn(hn[:, t % 2], h, psT[h]).then_inc(hn_turned, 1)

                def turn_spatial():
                    pe.wait_ge(wmask, 1)
                    for h in range(2):
                        turn(xt[:, 0], h, psT[h]).then_inc(wt_turned, 1)

                def bank_free(n):
                    if n >= 4:
                        m = n - 4
                        if 8 <= m < 16:
                            pe.wait_ge(staged_d, m - 8 + 1)
                        elif m < 8:
                            pe.wait_ge(freed[0], m + 1)
                        elif m < UQ:
                            pe.wait_ge(freed[0], 8 + m - UU + 1)
                        elif m < UG:
                            pe.wait_ge(staged_d, 16 + m - UQ + 1)
                        else:
                            pe.wait_ge(staged_a, m - UG + 1)

                def product(n, operands):
                    bank_free(n)
                    for i, (a, b) in enumerate(operands):
                        ins = nc.tensor.matmul(psP[n % 4][:, :], a, b, start=(i == 0), stop=(i == len(operands) - 1))
                    ins.then_inc(proj, 1)

                turn_hn(0)
                for chunk in range(2):
                    for t in range(TT):
                        if chunk == 0:
                            if t + 1 < TT:
                                turn_hn(t + 1)
                            pe.wait_ge(hT_done, 2 * t + 2)
                        elif t == 0:
                            turn_spatial()
                        if t == 0:
                            split_ready(pe, 4 * chunk + 2)
                            split_ready(pe, 4 * chunk + 3)
                        product(8 * chunk + t, [(hT[a][:, k, t * P:(t + 1) * P],
                                                 wS[b][:, 4 * chunk + k // 2, (k % 2) * HALF:(k % 2 + 1) * HALF])
                                                for k in range(KT) for a, b in PARTS])

                def piece(i, half):
                    n = UU + 2 * i + half
                    if half == 0:
                        split_ready(pe, 8 + i)
                    s = (8 + i) % RING
                    product(n, [(wS[a][:, s, k * P:(k + 1) * P], hT[b][:, k, half * HALF:(half + 1) * HALF])
                                for k in range(KT) for a, b in PARTS])

                def mix(m):
                    i, half = divmod(m, 2)
                    pe.wait_ge(vs_done, TT)
                    pe.wait_ge(wT_done, 2)
                    if m >= 2:
                        pe.wait_ge(ob_a, m - 1)
                    for ch in range(4):
                        for g in range(2):
                            ins = nc.tensor.matmul(psT[m % 2][g * GD:(g + 1) * GD, ch * P:(ch + 1) * P],
                                                   vs[:, 4 * half + ch, (2 * i + g) * GD:(2 * i + g + 1) * GD],
                                                   wT[:, 2 * i + g, :], start=True, stop=True)
                    ins.then_inc(mixed, 1)

                def sums(m):
                    pe.wait_ge(sq_done, m + 1)
                    if m >= 2:
                        pe.wait_ge(rt_done, m - 1)
                    nc.tensor.matmul(psS[m % 2][:, :], c["headones"], sq[:, m % 2, :], start=True, stop=True).then_inc(ssum, 1)

                for i in range(4):
                    for half in range(2):
                        piece(i, half)
                        mix(2 * i + half)
                for i in range(4, 12):
                    for half in range(2):
                        piece(i, half)
                        m = 2 * (i - 4) + half
                        if m >= 1:
                            sums(m - 1)
                for i in range(12, 28):
                    for half in range(2):
                        piece(i, half)
                        if i == 12 and half == 0:
                            sums(15)


def attention(nc, c, io, dr, keep):
    with ExitStack() as ctx:
        sb = lambda name, shape, dt=F32: ctx.enter_context(nc.sbuf_tensor("b_" + name, shape, dt))
        ps = lambda name, shape: ctx.enter_context(nc.psum_tensor("b_" + name, shape, F32))
        sem = lambda name: ctx.enter_context(nc.semaphore("b_" + name))
        RZ, RE, RL, RK, RA, RT = 3, 3, 5, 6, 2, 3
        LB, SCAN, SUM, EXP, TURN, PV = 1, 2, 2, 3, 5, 7
        hide = sb("hide", [P, P])
        kT = sb("kT", [P, PAIRS, T])
        qT = sb("qT", [P, HEADS, T])
        v = sb("v", [P, TT, SBW])
        z = sb("z", [P, RZ, T])
        e = sb("e", [P, RE, T])
        lb = sb("lb", [P, RL, T])
        lk = sb("lk", [P, RK, T])
        after = sb("after", [P, RA, T + 1])
        aT = sb("aT", [P, RT, T])
        o = keep["stream"][:, 0:PAIRS]
        psZ = [ps(f"psZ{i}", [P, T]) for i in range(2)]
        psA = [ps(f"psA{i}", [P, HALF]) for i in range(2)]
        psO = [ps(f"psO{i}", [P, P]) for i in range(2)]
        zeros = sb("zeros", [P, 1, D])
        zeroed = sem("zeroed"); qk_in = [sem(f"qk_in{i}") for i in range(PAIRS)]; v_in = sem("v_in")
        z_done = sem("z_done"); z_copied = sem("z_copied"); act_step = sem("act_step"); l_done = sem("l_done")
        dve_step = sem("dve_step"); lb_done = sem("lb_done"); lk_done = [sem(f"lk_done{i}") for i in range(2)]; scanned = sem("scanned")
        summed = sem("summed"); expd = sem("expd");
        turned = sem("turned"); aT_done = [sem(f"aT_done{i}") for i in range(2)]
        pv_done = sem("pv_done"); o_done = sem("o_done"); zeros_out = sem("zeros_out"); v_zero = sem("v_zero")

        units = [(i, qt, h) for qt in reversed(range(TT)) for i in range(PAIRS) for h in range(2)]
        N = len(units)
        keys = [(u[1] + 1) * P for u in units]
        groups = [(u[1] + 4) // 4 for u in units]
        gsum = [sum(groups[:n]) for n in range(N + 1)]

        SHARE = 5
        by_vector = lambda m: m % SHARE == SHARE - 1
        lk_counts = lambda m: (lk_done[1], m // SHARE + 1) if by_vector(m) else (lk_done[0], m - m // SHARE + 1)

        def keep_log(eng, ns, m):
            S = keys[m]
            eng.wait_ge(lb_done, m + 1)
            if m >= RK:
                eng.wait_ge(turned, gsum[m - RK + 1])
            ns.tensor_tensor(lk[:, m % RK, 0:S], lb[:, m % RL, 0:S], z[:, m % RZ, 0:S], ALU.subtract).then_inc(lk_counts(m)[0], 1)

        def copy_turned(eng, copy, m, which):
            for g in range(groups[m]):
                G = gsum[m] + g
                if G % 2 == which:
                    eng.wait_ge(turned, G + 1)
                    if m >= RT:
                        eng.wait_ge(pv_done, m - RT + 1)
                    w = min(HALF, keys[m] - g * HALF)
                    copy(aT[:, m % RT, g * HALF:g * HALF + w], psA[which][:, 0:w]).then_inc(aT_done[which], 1)

        with nc.Block() as block:
            @block.sync
            def _(sp):
                for i in range(PAIRS):
                    for h in range(2):
                        rows = slice(h * HD, (h + 1) * HD)
                        sp.dma_start(qT[rows, 2 * i + h, :], dr["qk"][i, rows, :]).then_inc(qk_in[i], 16)
                    sp.dma_start(kT[:, i, :], dr["qk"][PAIRS + i]).then_inc(qk_in[i], 16)
                sp.dma_start(v[:, :, :], dr["v"].rearrange("(t p) n -> p t n", p=P)).then_inc(v_in, 16)
                for i in range(PAIRS):
                    sp.dma_start(keep["stream"][:, OB_SLOTS[i]], dr["ob"][i]).then_inc(keep["ob_in"], 16)
                for f in range(2):
                    load_up(sp, io, keep, f)
                for n in range(2):
                    load_gates(sp, dr, keep, n)
                sp.wait_ge(zeroed, 2)
                sp.dma_start(dr["ys"][NE * BLOCK:, :].rearrange("(b p) n -> p b n", p=P),
                             zeros[:, :, :].to_broadcast([P, MAXB - NE, D])).then_inc(zeros_out, 16)
                sp.wait_ge(zeros_out, 16)

            @block.gpsimd
            def _(pool):
                nc.gpsimd.memset(qT[HD:P, 0::2, :], 0.0).then_inc(zeroed, 1)
                pool.wait_ge(zeroed, 1)
                nc.gpsimd.memset(zeros[:, :, :], 0.0).then_inc(zeroed, 1)
                for n in range(N + SUM):
                    if 0 <= n - LB < N and not by_vector(n - LB):
                        keep_log(pool, nc.gpsimd, n - LB)
                    m = n - SUM
                    if m >= 0:
                        S = keys[m]
                        pool.wait_ge(scanned, m + 1)
                        nc.gpsimd.tensor_tensor(lb[:, m % RL, 0:S], lb[:, m % RL, 0:S], after[:, m % RA, 1:S + 1], ALU.add).then_inc(summed, 1)

            @block.scalar
            def _(act):
                link = Chain(act, act_step)
                nc.scalar.preload_act_table_set("natural_log_exp_and_others")
                for n in range(N + TURN):
                    if n < N:
                        x = e[:, n % RE, 0:keys[n]]
                        act.wait_ge(z_copied, n + 1)
                        if n >= RE:
                            act.wait_ge(lb_done, n - RE + 1)
                        link(nc.scalar.activation(x, z[:, n % RZ, 0:keys[n]], ACT.Abs))
                        link(nc.scalar.activation(x, x, ACT.Exp, scale=-1.0))
                        nc.scalar.activation(x, x, ACT.Ln, bias=1.0).then_inc(l_done, 1)
                    m = n - EXP
                    if 0 <= m < N:
                        act.wait_ge(summed, m + 1)
                        nc.scalar.activation(lk[:, m % RK, 0:keys[m]], lb[:, m % RL, 0:keys[m]], ACT.Exp).then_inc(expd, 1)
                    if n >= TURN:
                        copy_turned(act, nc.scalar.copy, n - TURN, 1)

            @block.vector
            def _(dve):
                link = Chain(dve, dve_step)
                nc.vector.memset(qT[0:HD, 1::2, :], 0.0).then_inc(v_zero, 1)
                link(nc.vector.memset(after[:, :, :], 0.0))
                link(nc.vector.tensor_scalar(hide[:, :], c["causal"], 1e30, -1e30, ALU.mult, ALU.add))
                for n in range(N + PV + 1):
                    if n < N:
                        S = keys[n]
                        dve.wait_ge(z_done, n + 1)
                        if n >= RZ:
                            dve.wait_ge(*lk_counts(n - RZ))
                        if S > P:
                            nc.vector.tensor_copy(z[:, n % RZ, 0:S - P], psZ[n % 2][:, 0:S - P])
                        nc.vector.tensor_tensor(z[:, n % RZ, S - P:S], psZ[n % 2][:, S - P:S], hide[:, :], ALU.add).then_inc(z_copied, 1)
                    m = n - LB
                    if 0 <= m < N:
                        S = keys[m]
                        dve.wait_ge(l_done, m + 1)
                        if m >= RL:
                            dve.wait_ge(expd, m - RL + 1)
                        nc.vector.scalar_tensor_tensor(lb[:, m % RL, 0:S], z[:, m % RZ, 0:S], 0.0, e[:, m % RE, 0:S],
                                                       ALU.min, ALU.subtract).then_inc(lb_done, 1)
                        if by_vector(m):
                            keep_log(dve, nc.vector, m)
                    m = n - SCAN
                    if 0 <= m < N:
                        S = keys[m]
                        dve.wait_ge(*lk_counts(m))
                        if m >= RA:
                            dve.wait_ge(summed, m - RA + 1)
                        link(nc.vector.memset(after[:, m % RA, S:S + 1], 0.0))
                        nc.vector.tensor_tensor_scan(after[:, m % RA, 0:S][:, ::-1], c["ones"][:, 0:1].to_broadcast([P, S]),
                                                     lk[:, m % RK, 0:S][:, ::-1], 0.0, ALU.mult, ALU.add).then_inc(scanned, 1)
                    if 0 <= n - TURN < N:
                        copy_turned(dve, nc.vector.tensor_copy, n - TURN, 0)
                    m = n - PV - 1
                    if m >= 0 and units[m][2] == 1:
                        i, qt, _ = units[m]
                        dve.wait_ge(pv_done, m + 1)
                        nc.vector.tensor_copy(o[:, i, qt * P:(qt + 1) * P], psO[m // 2 % 2][:, :]).then_inc(o_done, 1)

            @block.tensor
            def _(pe):
                for n in range(N + PV):
                    if n < N:
                        i, qt, h = units[n]
                        if n < 2 * PAIRS and h == 0:
                            pe.wait_ge(qk_in[i], 48)
                        if n == 0:
                            pe.wait_ge(zeroed, 1)
                            pe.wait_ge(v_zero, 1)
                        if n >= 2:
                            pe.wait_ge(z_copied, n - 1)
                        for g in range(groups[n]):
                            w = min(HALF, keys[n] - g * HALF)
                            ins = nc.tensor.matmul(psZ[n % 2][:, g * HALF:g * HALF + w], qT[:, 2 * i + h, qt * P:(qt + 1) * P],
                                                   kT[:, i, g * HALF:g * HALF + w], start=True, stop=True)
                        ins.then_inc(z_done, 1)
                    m = n - PV
                    if m >= 0:
                        i, qt, h = units[m]
                        if m == 0:
                            pe.wait_ge(v_in, 16)
                        for G in range(gsum[m], gsum[m + 1]):
                            pe.wait_ge(aT_done[G % 2], G // 2 + 1)
                        if h == 0 and m >= 4:
                            pe.wait_ge(o_done, m // 2 - 1)
                        for j in range(qt + 1):
                            ins = nc.tensor.matmul(psO[m // 2 % 2][h * HD:(h + 1) * HD, :], v[:, j, (2 * i + h) * HD:(2 * i + h + 1) * HD],
                                                   aT[:, m % RT, j * P:(j + 1) * P], start=(j == 0), stop=(j == qt))
                        ins.then_inc(pv_done, 1)
                    m = n - TURN
                    if 0 <= m < N:
                        qt = units[m][1]
                        pe.wait_ge(expd, m + 1)
                        for g in range(groups[m]):
                            G = gsum[m] + g
                            if G >= 2:
                                pe.wait_ge(aT_done[G % 2], G // 2)
                            for j in range(4 * g, min(4 * g + 4, qt + 1)):
                                ins = nc.tensor.transpose(psA[G % 2][:, (j % 4) * P:(j % 4 + 1) * P], lk[:, m % RK, j * P:(j + 1) * P], c["ident"])
                            ins.then_inc(turned, 1)


BLOCK = 128
MAXB = T * 2 // BLOCK + NE


EPAIR = 2
OB_SLOTS = (10, 11, 8, 9)


def slot(j):
    return (j + 10) % (KT + FF // P)


def load_expert_pair(sp, io, keep, e, j):
    source, k = (io["w_expert_in"], j) if j < KT else (io["w_expert_out"], j - KT)
    sp.dma_start(keep["stream"][:, slot(j):slot(j) + EPAIR, :], source[0, bass.ds(e, 1), k * P:(k + EPAIR) * P, :]
                 .rearrange("o (k p) n -> p (o k) n", p=P)).then_inc(keep["stream_in"][j // EPAIR], 16)


def load_up(sp, io, keep, f):
    for i, w in enumerate((io["w_up_a"], io["w_up_b"])):
        sp.dma_start(keep["stream"][:, 4 + f % 2, i * HALF:(i + 1) * HALF].rearrange("p (k n) -> p k n", k=4),
                     w[0, :, f * P:(f + 1) * P].rearrange("(k p) n -> p k n", p=P)).then_inc(keep["up_in"][f % 2], 16)


def load_gates(sp, dr, keep, n):
    f, half = divmod(n, 2)
    for i in range(2):
        sp.dma_start(keep["stream"][:, 6 + n % 2, i * HALF:(i + 1) * HALF],
                     dr["gates"][KT * i + f, :, half * HALF:(half + 1) * HALF]).then_inc(keep["gate_in"][n % 2], 16)


def merge_and_route(nc, c, io, dr, keep):
    with ExitStack() as ctx:
        sb = lambda name, shape, dt=F32: ctx.enter_context(nc.sbuf_tensor("m_" + name, shape, dt))
        ps = lambda name, shape: ctx.enter_context(nc.psum_tensor("m_" + name, shape, F32))
        sem = lambda name: ctx.enter_context(nc.semaphore("m_" + name))
        RAW, UR, URAW = 3, 2, 2
        oS = [sb(f"o{i}", [P, 2 * PAIRS, T], F32R) for i in range(2)]
        mS = [sb(f"m{i}", [P, KT, T], F32R) for i in range(2)]
        uS = [sb(f"u{i}", [P, UR, D], F32R) for i in range(2)]
        stream = keep["stream"]
        raw = stream[:, 0:RAW]
        uraw = stream[:, 4:4 + URAW]
        gate = stream[:, 6:8].rearrange("p r (i n) -> p r i n", i=2)
        ta, tb = stream[:, 8, 0:HALF], stream[:, 8, HALF:D]
        gain = stream[:, 9]
        x1 = stream[:, 6:8]
        h2T = uraw[:, 0, :].rearrange("p (k n) -> p k n", k=KT)
        hn = uraw[:, 1, :]
        NR = 96
        wr = sb("wr", [P, KT, NR])
        br = sb("br", [P, NG + NE])
        L = sb("L", [P, TT, NG + NE])
        ssq = sb("ssq", [P, TT]); srt = sb("srt", [P, TT]); rstd = sb("rstd", [P, TT]); tmp = sb("tmp", [P, TT])
        psP = [ps(f"psP{i}", [P, HALF]) for i in range(6)]
        psT = [ps(f"psT{i}", [P, HALF]) for i in range(2)]

        gain_in = sem("gain_in"); wr_zero = sem("wr_zero"); wr_in = sem("wr_in")
        raw_in = [sem(f"raw_in{i}") for i in range(RAW)]
        uraw_in, gate_in = keep["up_in"], keep["gate_in"]
        x_in = [sem(f"x_in{i}") for i in range(2)]
        u_hi = sem("u_hi"); u_split = sem("u_split")
        hi = sem("hi"); lo = sem("lo")
        up = sem("up"); dve_step = sem("dve_step"); act_step = sem("act_step"); gated = sem("gated"); m_sum = sem("m_sum"); m_hi = sem("m_hi"); m_done = sem("m_done")
        out = sem("out"); x1_done = sem("x1_done"); ssq_done = sem("ssq_done"); srt_done = sem("srt_done"); h2_done = sem("h2_done")
        turned = sem("turned"); h2T_done = sem("h2T_done"); logits = sem("logits"); L_done = sem("L_done")
        x1_out = [sem(f"x1_out{i}") for i in range(2)]; h2_out = sem("h2_out")

        G8 = [P, TT, NG]; E8 = [P, TT, EPG]; GE = [P, TT, NG, EPG]; TE = [P, TT, NE]
        w4 = sb("w4", [P, 1, NG]); w8 = sb("w8", [P, 1, EPG]); thr = sb("thr", [P, 1, TT - 1])
        NS = MAXB + 2
        NSP = 96
        edges = sb("edges", [P, 1, NS + 1]); places = sb("places", [P, 1, BLOCK]); tok = sb("tok", [P, TT, 1]); n_edges = sb("n_edges", [P, 2 * TT, 1])
        in_block = stream[:, 4:6].rearrange("p r n -> p (r n)")[:, 0:2 * TT * NSP].rearrange("p (u b) -> p u b", u=2 * TT)
        at_place = stream[:, 6:8].rearrange("p r (u s) -> p (r u) s", s=BLOCK)
        passed = stream[:, 9, 0:2 * TT * (NS + 1)].rearrange("p (u b) -> p u b", u=2 * TT)
        zrow = sb("zrow", [P, D // P])
        gmax = sb("gmax", [P, TT, 1]); g_oh = sb("g_oh", G8); g_tmp = sb("g_tmp", G8); g_exp = sb("g_exp", G8); g_w = sb("g_w", [P, TT])
        sel4 = sb("sel4", GE); esel = sb("esel", E8); e_tmp = sb("e_tmp", E8); pick = [sb(f"pick{i}", E8) for i in range(2)]
        emax = [sb(f"emax{i}", [P, TT, 1]) for i in range(2)]; e_exp = sb("e_exp", [P, TT]); e_sum = sb("e_sum", [P, TT])
        hot = [sb(f"hot{i}", GE) for i in range(2)]
        both, rank, count, off = (stream[:, 8, i * TT * NE:(i + 1) * TT * NE].rearrange("p (t n) -> p t n", t=TT) for i in range(4))
        total = sb("total", [P, NE, 1])
        over = sb("over", [P, NE, TT - 1]); nb = sb("nb", [P, NE]); cum = sb("cum", [P, NE + 1]); base = sb("base", [P, 1, NE])
        destf = sb("destf", [P, 2, TT])
        r_const = sem("r_const"); d_ready = sem("d_ready"); d_exp = sem("d_exp"); hot_done = sem("hot_done"); ranked = sem("ranked")
        placed = sem("placed"); summed = sem("summed"); fill_out = sem("fill_out"); slots_made = sem("slots_made")
        flat = lambda a: a[:, :, :].rearrange("p t n -> p (t n)")

        def first_of_max(link, values, out_hot, maximum, weights, tmp3):
            shape = list(values.shape)
            link(nc.vector.tensor_reduce(maximum, values, AX.X, ALU.max))
            link(nc.vector.tensor_tensor(out_hot, values, maximum.to_broadcast(shape), ALU.is_equal))
            link(nc.vector.tensor_tensor(out_hot, out_hot, weights.to_broadcast(shape), ALU.mult))
            link(nc.vector.tensor_reduce(tmp3, out_hot, AX.X, ALU.max))
            link(nc.vector.tensor_tensor(out_hot, out_hot, tmp3.to_broadcast(shape), ALU.is_equal))

        def routing(dve, link):
            dve.wait_ge(r_const, 7)
            t1 = tmp[:, :].rearrange("p (t n) -> p t n", n=1)
            LG = L[:, :, 0:NG]
            LE = L[:, :, NG:].rearrange("p t (g e) -> p t g e", g=NG)
            spread = lambda oh: oh.rearrange("p t (g n) -> p t g n", n=1).to_broadcast(GE)
            first_of_max(link, LG, g_oh[:, :, :], gmax[:, :, :], w4[:, :, :], t1)
            nc.vector.tensor_tensor(g_tmp[:, :, :], LG, gmax[:, :, :].to_broadcast(G8), ALU.subtract).then_inc(d_ready, 1)
            link(nc.vector.tensor_tensor(sel4[:, :, :, :], LE, spread(g_oh[:, :, :]), ALU.mult))
            link(nc.vector.tensor_reduce(esel[:, :, :], sel4[:, :, :, :].rearrange("p t g e -> p t e g"), AX.X, ALU.add))
            first_of_max(link, esel[:, :, :], pick[0][:, :, :], emax[0][:, :, :], w8[:, :, :], t1)
            link(nc.vector.scalar_tensor_tensor(e_tmp[:, :, :], pick[0][:, :, :], -3e38, esel[:, :, :], ALU.mult, ALU.add))
            first_of_max(link, e_tmp[:, :, :], pick[1][:, :, :], emax[1][:, :, :], w8[:, :, :], t1)
            flat1 = lambda a: a[:, :, :].rearrange("p t n -> p (t n)")
            nc.vector.tensor_tensor(e_sum[:, :], flat1(emax[1]), flat1(emax[0]), ALU.subtract).then_inc(d_ready, 1)
            for i in range(2):
                link(nc.vector.tensor_tensor(hot[i][:, :, :, :], spread(g_oh[:, :, :]),
                                             pick[i][:, :, :].rearrange("p t (n e) -> p t n e", n=1).to_broadcast(GE), ALU.mult))
            h = [a[:, :, :, :].rearrange("p t g e -> p t (g e)") for a in hot]
            nc.vector.tensor_tensor(both[:, :, :], h[0], h[1], ALU.add).then_inc(hot_done, 1)
            dve.wait_ge(d_exp, 2)
            link(nc.vector.tensor_reduce(g_w[:, :], g_exp[:, :, :], AX.X, ALU.add))
            link(nc.vector.tensor_scalar(e_sum[:, :], e_exp[:, :], 1.0, None, ALU.add))
            link(nc.vector.tensor_tensor(e_sum[:, :], e_sum[:, :], g_w[:, :], ALU.mult))
            link(nc.vector.reciprocal(keep["w"][:, 0, :], e_sum[:, :]))
            link(nc.vector.tensor_tensor(keep["w"][:, 1, :], keep["w"][:, 0, :], e_exp[:, :], ALU.mult))
            dve.wait_ge(h2_out, 16 * TT)
            for i in range(2):
                dve.wait_ge(x1_out[i], 16 * TT // 2)
            link(nc.vector.memset(in_block, 0.0))
            dve.wait_ge(ranked, 2)
            link(nc.vector.tensor_copy(flat(count), psP[1][:, 0:TT * NE]))
            link(nc.vector.memset(off[:, 0, :], 0.0))
            for t in range(1, TT):
                link(nc.vector.tensor_tensor(off[:, t, :], off[:, t - 1, :], count[:, t - 1, :], ALU.add))
            tot = total[:, :, :].rearrange("p e n -> p (e n)")
            link(nc.vector.tensor_tensor(tot, off[:, TT - 1, :], count[:, TT - 1, :], ALU.add))
            link(nc.vector.tensor_tensor(flat(rank), flat(off), psP[0][:, 0:TT * NE], ALU.add))
            link(nc.vector.tensor_tensor(over[:, :, :], total[:, :, :].to_broadcast([P, NE, TT - 1]), thr[:, :, :].to_broadcast([P, NE, TT - 1]), ALU.is_gt))
            link(nc.vector.tensor_reduce(nb[:, :], over[:, :, :], AX.X, ALU.add))
            link(nc.vector.tensor_scalar(nb[:, :], nb[:, :], 1.0, None, ALU.add))
            link(nc.vector.memset(cum[:, 0:1], 0.0))
            link(nc.vector.tensor_tensor_scan(cum[:, 1:NE + 1], c["ones"][:, 0:NE], nb[:, :], 0.0, ALU.mult, ALU.add))
            link(nc.vector.tensor_copy(keep["cum"][:, :], cum[:, :]))
            link(nc.vector.tensor_scalar(keep["last"][:, :], cum[:, 1:NE + 1], -1.0, None, ALU.add))
            link(nc.vector.tensor_scalar(base[:, 0, :], cum[:, 0:NE], float(BLOCK), None, ALU.mult))
            link(nc.vector.tensor_tensor(rank[:, :, :], rank[:, :, :], base[:, :, :].to_broadcast(TE), ALU.add))
            for i in range(2):
                link(nc.vector.tensor_tensor(off[:, :, :], h[i], rank[:, :, :], ALU.mult))
                link(nc.vector.tensor_reduce(destf[:, i, :], off[:, :, :], AX.X, ALU.add))
            link(nc.vector.tensor_copy(keep["dest"][:, :, :], destf[:, :, :]))
            slot_table(dve, link)

        def slot_table(dve, link):
            dest = destf[:, :, :].rearrange("p i (t n) -> p (i t) n", n=1)
            shape = [P, 2 * TT, NS + 1]
            link(nc.vector.tensor_tensor(passed, dest.to_broadcast(shape), edges[:, :, :].to_broadcast(shape), ALU.is_ge))
            link(nc.vector.tensor_reduce(n_edges[:, :, :], passed, AX.X, ALU.add))
            link(nc.vector.tensor_tensor(in_block[:, :, 0:NS], passed[:, :, 0:NS], passed[:, :, 1:NS + 1], ALU.subtract))
            for i in range(2):
                v = in_block[:, i * TT:(i + 1) * TT, 0:NS]
                link(nc.vector.tensor_tensor(v, v, tok[:, :, :].to_broadcast([P, TT, NS]), ALU.mult))
            link(nc.vector.scalar_tensor_tensor(dest, n_edges[:, :, :], -float(BLOCK), dest, ALU.mult, ALU.add))
            shape = [P, TT, BLOCK]
            for i in range(2):
                v = slice(i * TT, (i + 1) * TT)
                nc.vector.tensor_tensor(at_place[:, v], dest[:, v].to_broadcast(shape), places[:, :, :].to_broadcast(shape), ALU.is_equal).then_inc(placed, 1)
            dve.wait_ge(summed, 1)
            nc.vector.tensor_scalar(keep["slots"][:, :], psP[2][:, 0:NS], float(T), None, ALU.add).then_inc(slots_made, 1)

        def rank_products(pe):
            pe.wait_ge(hot_done, 1)
            pe.wait_ge(x1_done, 2 * TT)
            nc.tensor.matmul(psP[0][:, 0:TT * NE], c["below"], flat(both), start=True, stop=True).then_inc(ranked, 1)
            nc.tensor.matmul(psP[1][:, 0:TT * NE], c["ones"], flat(both), start=True, stop=True).then_inc(ranked, 1)
            for u in range(2 * TT):
                pe.wait_ge(placed, u // TT + 1)
                ins = nc.tensor.matmul(psP[2][:, 0:NSP], at_place[:, u, :], in_block[:, u, :], start=(u == 0), stop=(u == 2 * TT - 1))
            ins.then_inc(summed, 1)

        def routing_exps(act):
            act.wait_ge(d_ready, 2)
            nc.scalar.activation(g_exp[:, :, :], g_tmp[:, :, :], ACT.Exp).then_inc(d_exp, 1)
            nc.scalar.activation(e_exp[:, :], e_sum[:, :], ACT.Exp).then_inc(d_exp, 1)

        def routing_constants():
            iota = lambda out, pattern, base, mult: nc.gpsimd.iota(out, pattern, base=base, channel_multiplier=mult,
                                                                   allow_small_or_imprecise_dtypes=True).then_inc(r_const, 1)
            iota(w4[:, 0, :], [[-1, NG]], NG, 0)
            iota(w8[:, 0, :], [[-1, EPG]], EPG, 0)
            iota(thr[:, 0, :], [[BLOCK, TT - 1]], BLOCK, 0)
            iota(edges[:, 0, :], [[BLOCK, NS + 1]], 0, 0)
            iota(places[:, 0, :], [[1, BLOCK]], -BLOCK, 0)
            iota(tok[:, :, 0], [[P, TT]], -T, 1)
            nc.gpsimd.memset(zrow[:, :], 0.0).then_inc(r_const, 1)

        def zero_row(pool):
            pool.wait_ge(r_const, 7)
            pool.dma_start(dr["h2"][T:T + 1, :].rearrange("o (p n) -> (o p) n", p=P), zrow[:, :]).then_inc(fill_out, 16)
            pool.wait_ge(fill_out, 16)

        w_out = io["w_out"][0]
        sources = [w_out[2 * j * P:(2 * j + 2) * P, n * HALF:(n + 1) * HALF].rearrange("(k p) n -> p k n", p=P)
                   for n in range(2) for j in range(4)]

        def granule(g):
            if g < PAIRS:
                return stream[:, g]
            return stream[:, OB_SLOTS[g - PAIRS]] if g < 8 else raw[:, g % 8 % RAW]

        with nc.Block() as block:
            @block.sync
            def _(sp):
                def load_raw(g):
                    sp.wait_ge(lo, g - RAW + 1 if g >= 8 + RAW else 8)
                    sp.dma_start(granule(g).rearrange("p (k n) -> p k n", k=2), sources[g - 8]).then_inc(raw_in[g % 8 % RAW], 16)

                sp.wait_ge(lo, 8)
                sp.dma_start(gain[:, :], io["norm_ffn"].to_broadcast([P, D])).then_inc(gain_in, 16)
                sp.wait_ge(wr_zero, 1)
                with nc.allow_non_contiguous_dma(reason="router columns, 144 bytes a row"):
                    sp.dma_start(wr[:, :, 0:NG], io["w_group_router"][0].rearrange("(k p) n -> p k n", p=P)).then_inc(wr_in, 16)
                    sp.dma_start(wr[:, :, NG:NG + NE], io["w_expert_router"][0].rearrange("(k p) n -> p k n", p=P)).then_inc(wr_in, 16)
                sp.dma_start(br[:, 0:NG], io["b_group_router"].to_broadcast([P, NG])).then_inc(wr_in, 16)
                sp.dma_start(br[:, NG:], io["b_expert_router"].to_broadcast([P, NE])).then_inc(wr_in, 16)
                load_expert_pair(sp, io, keep, 0, 0)
                for f in range(1, KT):
                    for half in range(2):
                        sp.wait_ge(gated, 2 * f + half - 1)
                        load_gates(sp, dr, keep, 2 * f + half)
                    if f + 1 < KT:
                        sp.wait_ge(u_split, f)
                        load_up(sp, io, keep, f + 1)
                for g in range(8, 16):
                    load_raw(g)
                sp.wait_ge(gated, 2 * KT)
                for t in range(TT):
                    if t == 2:
                        sp.wait_ge(lo, 16)
                        load_expert_pair(sp, io, keep, 0, 2)
                        load_expert_pair(sp, io, keep, 0, 4)
                    if t >= 2:
                        sp.wait_ge(x1_out[t % 2], 16 * (t // 2))
                        sp.wait_ge(h2_done, t - 1)
                    sp.dma_start(x1[:, t % 2], io["x"][0, t * P:(t + 1) * P, :]).then_inc(x_in[t % 2], 16)
                    for m in ([t - 1] if t < TT - 1 else [t - 1, t]):
                        if m >= 0:
                            sp.wait_ge(x1_done, 2 * m + 2)
                            sp.dma_start(dr["x1"][m * P:(m + 1) * P, :], x1[:, m % 2]).then_inc(x1_out[m % 2], 16)
                            sp.wait_ge(h2_done, m + 1)
                            sp.dma_start(dr["h2"][m * P:(m + 1) * P, :], hn).then_inc(h2_out, 16)
                sp.wait_ge(h2_out, 16 * TT)
                for i in range(2):
                    sp.wait_ge(x1_out[i], 16 * TT // 2)
                sp.wait_ge(slots_made, 1)
                for j in range(6, KT + FF // P, EPAIR):
                    load_expert_pair(sp, io, keep, 0, j)

            @block.gpsimd
            def _(pool):
                nc.gpsimd.memset(wr[:, :, :], 0.0).then_inc(wr_zero, 1)
                routing_constants()
                for f in range(KT):
                    pool.wait_ge(uraw_in[f % URAW], 32 * (f // URAW + 1))
                    if f >= UR:
                        pool.wait_ge(up, 4 * (f - UR + 1))
                    r = uraw[:, f % URAW, :]
                    h, l = (w[:, f % UR, :] for w in uS)
                    nc.gpsimd.tensor_tensor(h, r, c["ones"][:, 0:1].to_broadcast([P, D]), ALU.mult).then_inc(u_hi, 1)
                    pool.wait_ge(u_hi, f + 1)
                    nc.gpsimd.tensor_tensor(l, r, h.bitcast(F32), ALU.subtract).then_inc(u_split, 1)
                zero_row(pool)

            @block.scalar
            def _(act):
                link = Chain(act, act_step)

                def high(g):
                    if PAIRS <= g < 8:
                        act.wait_ge(keep["ob_in"], 16 * PAIRS)
                    if g >= 8:
                        act.wait_ge(raw_in[g % 8 % RAW], 16 * (g % 8 // RAW + 1))
                        act.wait_ge(up, 4 * KT)
                    nc.scalar.copy(oS[0][:, g % 8, :], granule(g)).then_inc(hi, 1)
                for g in range(8):
                    high(g)
                for n in range(2 * KT):
                    f, half = divmod(n, 2)
                    act.wait_ge(m_sum, n + 1)
                    nc.scalar.copy(mS[0][:, f, half * HALF:(half + 1) * HALF], ta[:, :]).then_inc(m_hi, 1)
                for g in range(8, 16):
                    high(g)
                act.wait_ge(u_split, KT)
                for t in range(TT):
                    act.wait_ge(x1_done, 2 * t + 2)
                    if t >= 1:
                        act.wait_ge(turned, 2 * t)
                        act.wait_ge(h2_out, 16 * t)
                    nc.scalar.activation(hn, x1[:, t % 2], ACT.Square, accum_out=ssq[:, t:t + 1]).then_inc(ssq_done, 1)
                    act.wait_ge(ssq_done, t + 1)
                    nc.scalar.activation(srt[:, t:t + 1], ssq[:, t:t + 1], ACT.Sqrt, bias=c["eps"], scale=1.0 / D).then_inc(srt_done, 1)
                    for h in range(2):
                        act.wait_ge(turned, 2 * t + h + 1)
                        if t >= 1:
                            act.wait_ge(logits, t)
                        nc.scalar.copy(h2T[:, 4 * h:4 * h + 4, :], psT[h][:, :].rearrange("p (k n) -> p k n", k=4)).then_inc(h2T_done, 1)
                routing_exps(act)

            @block.vector
            def _(dve):
                link = Chain(dve, dve_step)

                def low(g):
                    dve.wait_ge(hi, g + 1)
                    nc.vector.tensor_tensor(oS[1][:, g % 8, :], granule(g), oS[0][:, g % 8, :].bitcast(F32), ALU.subtract).then_inc(lo, 1)
                for g in range(8):
                    low(g)
                for n in range(2 * KT):
                    f, half = divmod(n, 2)
                    dve.wait_ge(gate_in[n % 2], 32 * (n // 2 + 1))
                    dve.wait_ge(up, 2 * n + 2)
                    if n >= 1:
                        dve.wait_ge(m_hi, n)
                    link(nc.vector.tensor_tensor(ta[:, :], psP[(2 * n) % 4][:, :], gate[:, n % 2, 0], ALU.mult))
                    nc.vector.tensor_tensor(tb[:, :], psP[(2 * n + 1) % 4][:, :], gate[:, n % 2, 1], ALU.mult).then_inc(gated, 1)
                    dve.wait_ge(gated, n + 1)
                    nc.vector.tensor_tensor(ta[:, :], ta[:, :], tb[:, :], ALU.add).then_inc(m_sum, 1)
                    dve.wait_ge(m_sum, n + 1)
                    dve.wait_ge(m_hi, n + 1)
                    cols = slice(half * HALF, (half + 1) * HALF)
                    nc.vector.tensor_tensor(mS[1][:, f, cols], ta[:, :], mS[0][:, f, cols].bitcast(F32), ALU.subtract).then_inc(m_done, 1)
                    dve.wait_ge(m_done, n + 1)
                for g in range(8, 16):
                    low(g)
                dve.wait_ge(gain_in, 16)
                dve.wait_ge(wr_in, 64)
                for t in range(TT):
                    dve.wait_ge(x_in[t % 2], 16 * (t // 2 + 1))
                    for n in range(2):
                        u = 2 * t + n
                        dve.wait_ge(out, u + 1)
                        v = x1[:, t % 2, n * HALF:(n + 1) * HALF]
                        nc.vector.tensor_tensor(v, v, psP[u % 4][:, :], ALU.add).then_inc(x1_done, 1)
                    dve.wait_ge(x1_done, 2 * t + 2)
                    dve.wait_ge(srt_done, t + 1)
                    refined_rstd(nc, link, rstd[:, t:t + 1], ssq[:, t:t + 1], srt[:, t:t + 1], tmp[:, 0:1], D)
                    nc.vector.scalar_tensor_tensor(hn, x1[:, t % 2], rstd[:, t:t + 1], gain[:, :], ALU.mult, ALU.mult).then_inc(h2_done, 1)
                    if t >= 1:
                        dve.wait_ge(logits, t)
                        nc.vector.tensor_tensor(L[:, t - 1, :], psP[4 + (t - 1) % 2][:, 0:NG + NE], br[:, :], ALU.add).then_inc(L_done, 1)
                dve.wait_ge(logits, TT)
                nc.vector.tensor_tensor(L[:, TT - 1, :], psP[4 + (TT - 1) % 2][:, 0:NG + NE], br[:, :], ALU.add).then_inc(L_done, 1)
                dve.wait_ge(L_done, TT)
                routing(dve, link)

            @block.tensor
            def _(pe):
                for n in range(2 * KT):
                    f, half = divmod(n, 2)
                    pe.wait_ge(u_split, f + 1)
                    for i in range(2):
                        if n >= 2:
                            pe.wait_ge(gated, n - 1)
                        steps = [(k, a, b) for k in range(4) for a, b in PARTS]
                        for j, (k, a, b) in enumerate(steps):
                            if n == 0:
                                pe.wait_ge(lo, 4 * i + k + 1)
                            ins = nc.tensor.matmul(psP[(2 * n + i) % 4][:, :], uS[a][:, f % UR, i * HALF + k * P:i * HALF + (k + 1) * P],
                                                   oS[b][:, 4 * i + k, half * HALF:(half + 1) * HALF], start=(j == 0), stop=(j == len(steps) - 1))
                        ins.then_inc(up, 1)

                def route(t):
                    pe.wait_ge(h2T_done, 2 * t + 2)
                    if t == 0:
                        pe.wait_ge(wr_in, 64)
                    if t >= 2:
                        pe.wait_ge(L_done, t - 1)
                    for k in range(KT):
                        ins = nc.tensor.matmul(psP[4 + t % 2][:, 0:NR], h2T[:, k, :], wr[:, k, :], start=(k == 0), stop=(k == KT - 1))
                    ins.then_inc(logits, 1)

                def turn(t):
                    pe.wait_ge(h2_done, t + 1)
                    for h in range(2):
                        if t >= 1:
                            pe.wait_ge(h2T_done, 2 * t - 1 + h)
                        for k in range(4):
                            ins = nc.tensor.transpose(psT[h][:, k * P:(k + 1) * P], hn[:, (4 * h + k) * P:(4 * h + k + 1) * P], c["ident"])
                        ins.then_inc(turned, 1)

                pe.wait_ge(m_done, 2 * KT)
                for t in range(TT):
                    for n in range(2):
                        u = 2 * t + n
                        if u >= 4:
                            pe.wait_ge(x1_done, u - 3)
                        steps = [(k, a, b) for k in range(KT) for a, b in PARTS]
                        for j, (k, a, b) in enumerate(steps):
                            if t == 0:
                                pe.wait_ge(lo, 8 + 4 * n + k // 2 + 1)
                            ins = nc.tensor.matmul(psP[u % 4][:, :], mS[a][:, k, t * P:(t + 1) * P],
                                                   oS[b][:, 4 * n + k // 2, (k % 2) * HALF:(k % 2 + 1) * HALF],
                                                   start=(j == 0), stop=(j == len(steps) - 1))
                        ins.then_inc(out, 1)
                    if t >= 1:
                        turn(t - 1)
                        if t >= 2:
                            route(t - 2)
                turn(TT - 1)
                route(TT - 2)
                route(TT - 1)
                rank_products(pe)


def load_embedding_pair(sp, io, keep, j):
    w, k = (io["w_ple_proj"], j) if j < PLE // P else (io["w_ple_gate"], j - PLE // P)
    sp.dma_start(keep["stream"][:, j:j + EPAIR, :], w[0, k * P:(k + EPAIR) * P, :].rearrange("(k p) n -> p k n", p=P)).then_inc(keep["stream_in"][j // EPAIR], 16)


def experts(nc, c, io, dr, keep):
    with ExitStack() as ctx:
        sb = lambda name, shape, dt=F32: ctx.enter_context(nc.sbuf_tensor("e_" + name, shape, dt))
        ps = lambda name, shape: ctx.enter_context(nc.psum_tensor("e_" + name, shape, F32))
        sem = lambda name: ctx.enter_context(nc.semaphore("e_" + name))
        FK = FF // P
        NGR = KT + FK
        EARLY = 6
        AHEAD = 2
        raw, raw_in = keep["stream"], keep["stream_in"]
        wS = [sb(f"w{i}", [P, NGR, D], F32R) for i in range(2)]
        idx = sb("idx", [P, 1], I32)
        xg = sb("xg", [P, D])
        xS = [sb(f"x{i}", [P, KT, P], F32R) for i in range(2)]
        sil = sb("sil", [P, FF])
        hid = sb("hid", [P, FF])
        hS = [sb(f"h{i}", [P, FK, P], F32R) for i in range(2)]
        y = sb("y", [P, D])
        nothing = sb("nothing", [P, 1])
        psX = [ps(f"psX{i}", [P, HALF]) for i in range(2)]
        psG = ps("psG", [P, FF])
        psU = ps("psU", [P, FF])
        psH = [ps(f"psH{i}", [P, 2 * P]) for i in range(2)]
        psY = [ps(f"psY{i}", [P, HALF]) for i in range(2)]
        w_hi = sem("w_hi"); w_lo = [sem(f"w_lo{i}") for i in range(2)]; used = sem("used")
        idx_set = sem("idx_set"); held = sem("held"); xg_in = sem("xg_in"); y_out = sem("y_out");
        x_turned = sem("x_turned"); x_hi = sem("x_hi"); x_lo = sem("x_lo"); gate_done = sem("gate_done")
        silu = sem("silu"); h_done = sem("h_done"); h_turned = sem("h_turned"); h_hi = sem("h_hi"); h_lo = sem("h_lo")
        y_copied = sem("y_copied")
        by_vector = [j for j in range(NGR) if j % 3 != 2]
        by_pool = [j for j in range(NGR) if j % 3 == 2]

        def parts_ready(eng, q, j):
            i, maker = (1, by_pool) if j in by_pool else (0, by_vector)
            eng.wait_ge(w_lo[i], len(maker) * q + (maker.index(j) + 1))

        def blocks(eng, e):
            return eng.value_load(keep["cum"][0:1, bass.ds(e, 1)], min_val=0, max_val=MAXB - 1)

        def all_but_last(eng, first, last, body):
            with eng.If(last > first):
                with eng.Fori(first, last) as g:
                    body(g)

        def last_block(eng, e):
            return eng.value_load(keep["last"][0:1, bass.ds(e, 1)], min_val=0, max_val=MAXB - 2)

        with nc.Block() as block:
            @block.sync
            def _(sp):
                def load(e, before):
                    for j in range(0, NGR, EPAIR):
                        if j + EPAIR - 1 in by_pool or j in by_pool:
                            parts_ready(sp, before, j)
                            sp.sem_inc(held, 1)
                        parts_ready(sp, before, j + EPAIR - 1)
                        load_expert_pair(sp, io, keep, e, j)

                def put_y(g):
                    sp.wait_ge(y_copied, g + 2)
                    sp.dma_start(dr["ys"][bass.ds(g * BLOCK, BLOCK), :], y[:, :]).then_inc(y_out, 16)
                load(1, 0)
                with sp.Fori(0, NE - 2) as q:
                    first, last = blocks(sp, q), last_block(sp, q)
                    all_but_last(sp, first, last, put_y)
                    load(q + 2, q + 1)
                    put_y(last)
                n = blocks(sp, NE)
                end = blocks(sp, NE - 1)
                with sp.Fori(blocks(sp, NE - 2), end) as g:
                    put_y(g)
                parts_ready(sp, NE - 1, by_pool[-1])
                sp.sem_inc(held, 1)
                parts_ready(sp, NE - 1, by_vector[-1])
                sp.sem_inc(held, 1)
                for j in range(0, PLE // P + KT, EPAIR):
                    load_embedding_pair(sp, io, keep, j)
                with sp.Fori(end, n) as g:
                    put_y(g)
                sp.wait_ge(y_out, 16 * n + 16)
                sp.sem_inc(held, 1)

            @block.gpsimd
            def _(pool):
                def gather(g):
                    if not (isinstance(g, int) and g == 0):
                        pool.wait_ge(xg_in, 16 * g)
                    nc.gpsimd.tensor_copy(idx[:, :], keep["slots"][:, bass.ds(g, 1)]).then_inc(idx_set, 1)
                    pool.wait_ge(x_turned, g + 1)
                    pool.sem_inc(held, 1)
                    pool.wait_ge(idx_set, g + 1)
                    pool.sem_inc(held, 1)
                    nc.gpsimd.indirect_dma_start(out=xg[:, :], out_offset=None, in_=dr["h2"],
                                                 in_offset=bass.IndirectOffsetOnAxis(ap=idx[:, 0:1], axis=0)).then_inc(xg_in, 16)

                def plain(g):
                    gather(g + 2)

                def lows(q, js):
                    for j in js:
                        pool.wait_ge(w_hi, NGR * q + j + 1)
                        nc.gpsimd.tensor_tensor(wS[1][:, j], raw[:, slot(j)], wS[0][:, j].bitcast(F32), ALU.subtract).then_inc(w_lo[1], 1)
                gather(0)
                lows(0, by_pool[:1])
                gather(1)
                lows(0, by_pool[1:])
                with pool.Fori(0, NE - 1) as q:
                    first, last = blocks(pool, q), last_block(pool, q)
                    all_but_last(pool, first, last, plain)
                    lows(q + 1, by_pool[:2])
                    gather(last + 2)
                    lows(q + 1, by_pool[2:])
                with pool.Fori(blocks(pool, NE - 1), blocks(pool, NE)) as g:
                    plain(g)
                pool.wait_ge(xg_in, 16 * blocks(pool, NE) + 32)
                pool.sem_inc(held, 1)

            @block.scalar
            def _(act):
                def highs(q, js, before):
                    for j in js:
                        act.wait_ge(raw_in[j // EPAIR], 16 * q + 16)
                        if before is not None:
                            act.wait_ge(used, before + (j + 1))
                        nc.scalar.copy(wS[0][:, j], raw[:, slot(j)]).then_inc(w_hi, 1)

                def high_x(g):
                    for h in range(2):
                        act.wait_ge(x_turned, g + 2)
                        nc.scalar.copy(xS[0][:, 4 * h:4 * h + 4, :], psX[h][:, :].rearrange("p (k n) -> p k n", k=4)).then_inc(x_hi, 1)

                def hidden(g):
                    for i in range(2):
                        cols = slice(i * 2 * P, (i + 1) * 2 * P)
                        act.wait_ge(gate_done, g + 1)
                        nc.scalar.activation(sil[:, cols], psG[:, cols], ACT.Silu).then_inc(silu, 1)
                    for i in range(2):
                        act.wait_ge(h_turned, 2 * g + i + 1)
                        nc.scalar.copy(hS[0][:, 2 * i:2 * i + 2, :], psH[i][:, :].rearrange("p (k n) -> p k n", k=2)).then_inc(h_hi, 1)

                def plain(g):
                    hidden(g)
                    high_x(g + 1)
                nc.scalar.preload_act_table_set("silu_and_others")
                highs(0, range(EARLY), None)
                high_x(0)
                highs(0, range(EARLY, NGR), None)
                with act.Fori(0, NE - 1) as q:
                    first, last = blocks(act, q), last_block(act, q)
                    all_but_last(act, first, last, plain)
                    before = NGR * last + NGR
                    highs(q + 1, range(0, EARLY), before)
                    plain(last)
                    highs(q + 1, range(EARLY, NGR), before)
                with act.Fori(blocks(act, NE - 1), blocks(act, NE)) as g:
                    plain(g)

            @block.vector
            def _(dve):
                def lows(q, js):
                    for j in js:
                        if j in by_vector:
                            dve.wait_ge(w_hi, NGR * q + j + 1)
                            nc.vector.tensor_tensor(wS[1][:, j], raw[:, slot(j)], wS[0][:, j].bitcast(F32), ALU.subtract).then_inc(w_lo[0], 1)

                def low_x(g):
                    for h in range(2):
                        dve.wait_ge(x_hi, 2 * g + h + 1)
                        nc.vector.tensor_tensor(xS[1][:, 4 * h:4 * h + 4, :], psX[h][:, :].rearrange("p (k n) -> p k n", k=4),
                                                xS[0][:, 4 * h:4 * h + 4, :].bitcast(F32), ALU.subtract).then_inc(x_lo, 1)

                def hidden(g):
                    dve.wait_ge(used, NGR * g + (NGR + KT))
                    for i in range(2):
                        cols = slice(i * 2 * P, (i + 1) * 2 * P)
                        dve.wait_ge(silu, 2 * g + i + 1)
                        nc.vector.tensor_tensor(hid[:, cols], sil[:, cols], psU[:, cols], ALU.mult).then_inc(h_done, 1)
                    for i in range(2):
                        dve.wait_ge(h_hi, 2 * g + i + 1)
                        nc.vector.tensor_tensor(hS[1][:, 2 * i:2 * i + 2, :], psH[i][:, :].rearrange("p (k n) -> p k n", k=2),
                                                hS[0][:, 2 * i:2 * i + 2, :].bitcast(F32), ALU.subtract).then_inc(h_lo, 1)

                def take_y(g):
                    dve.wait_ge(used, NGR * g + 2 * NGR)
                    dve.wait_ge(y_out, 16 * g + 16)
                    nc.vector.tensor_copy(y[:, 0:HALF], psY[0][:, :])
                    nc.vector.tensor_copy(y[:, HALF:D], psY[1][:, :]).then_inc(y_copied, 1)

                def plain(g):
                    hidden(g)
                    low_x(g + 1)
                    take_y(g)
                for signal, count in ((h_done, 2), (y_copied, 1), (y_out, 16), (used, NGR), (x_turned, 1)):
                    nc.vector.memset(nothing[:, :], 0.0).then_inc(signal, count)
                    if signal is not x_turned:
                        dve.wait_ge(signal, count)
                lows(0, range(EARLY))
                low_x(0)
                lows(0, range(EARLY, NGR))
                with dve.Fori(0, NE - 1) as q:
                    first, last = blocks(dve, q), last_block(dve, q)
                    all_but_last(dve, first, last, plain)
                    lows(q + 1, range(0, EARLY))
                    hidden(last)
                    low_x(last + 1)
                    lows(q + 1, range(EARLY, NGR))
                    take_y(last)
                with dve.Fori(blocks(dve, NE - 1), blocks(dve, NE)) as g:
                    plain(g)

            @block.tensor
            def _(pe):
                def turn_x(g):
                    pe.wait_ge(xg_in, 16 * g + 16)
                    for k in range(KT):
                        ins = nc.tensor.transpose(psX[k // 4][:, (k % 4) * P:(k % 4 + 1) * P], xg[:, k * P:(k + 1) * P], c["ident"])
                    ins.then_inc(x_turned, 1)

                def gate(k):
                    for a, b in PARTS:
                        ins = nc.tensor.matmul(psG[:, :], xS[a][:, k, :], wS[b][:, k, 0:FF], start=(k == 0 and (a, b) == PARTS[0]),
                                               stop=(k == KT - 1 and (a, b) == PARTS[-1]))
                    return ins

                def up(k):
                    for a, b in PARTS:
                        ins = nc.tensor.matmul(psU[:, :], xS[a][:, k, :], wS[b][:, k, FF:2 * FF], start=(k == 0 and (a, b) == PARTS[0]),
                                               stop=(k == KT - 1 and (a, b) == PARTS[-1]))
                    ins.then_inc(used, 1)
                    return ins

                def gate_up(q, g):
                    pe.wait_ge(x_lo, 2 * g + 2)
                    for k in range(KT):
                        parts_ready(pe, q, k)
                        ins = gate(k)
                        if k < KT - AHEAD:
                            up(k)
                    ins.then_inc(gate_done, 1)
                    for k in range(KT - AHEAD, KT):
                        ins = up(k)
                    return ins

                def turn_h(g):
                    for i in range(2):
                        pe.wait_ge(h_done, 2 * g + i + 3)
                        for k in range(2 * i, 2 * i + 2):
                            ins = nc.tensor.transpose(psH[i][:, k % 2 * P:(k % 2 + 1) * P], hid[:, k * P:(k + 1) * P], c["ident"])
                        ins.then_inc(h_turned, 1)

                def down(q, g):
                    pe.wait_ge(y_copied, g + 1)
                    for k in range(FK):
                        if k % 2 == 0:
                            pe.wait_ge(h_lo, 2 * g + k // 2 + 1)
                        parts_ready(pe, q, KT + k)
                        for n in range(2):
                            for a, b in PARTS:
                                ins = nc.tensor.matmul(psY[n][:, :], hS[a][:, k, :], wS[b][:, KT + k, n * HALF:(n + 1) * HALF],
                                                       start=(k == 0 and (a, b) == PARTS[0]), stop=(k == FK - 1 and (a, b) == PARTS[-1]))
                        ins.then_inc(used, 1)

                pe.wait_ge(x_turned, 1)
                turn_x(0)
                with pe.Fori(0, NE) as q:
                    with pe.Fori(blocks(pe, q), blocks(pe, q + 1)) as g:
                        gate_up(q, g)
                        turn_x(g + 1)
                        turn_h(g)
                        down(q, g)


def combine_and_embed(nc, c, io, dr, keep):
    with ExitStack() as ctx:
        sb = lambda name, shape, dt=F32: ctx.enter_context(nc.sbuf_tensor("p_" + name, shape, dt))
        ps = lambda name, shape: ctx.enter_context(nc.psum_tensor("p_" + name, shape, F32))
        sem = lambda name: ctx.enter_context(nc.semaphore("p_" + name))
        PK = PLE // P
        FIRST = 8
        NW = KT + PK
        wS = [sb(f"w{i}", [P, NW, D], F32R) for i in range(2)]
        XR = 4
        raw, raw_in = keep["stream"], keep["stream_in"]
        xs = sb("xs", [P, XR, D])
        ys = sb("ys", [P, 2, 2, D])
        pt = sb("pt", [P, 2, PLE])
        sq = sb("sq", [P, D])
        hn = sb("hn", [P, 2, D])
        sig = sb("sig", [P, D])
        gain = sb("gain", [P, D])
        hS = [sb(f"h{i}", [P, 2, KT, P], F32R) for i in range(2)]
        pS = [sb(f"pe{i}", [P, 2, PK, P], F32R) for i in range(2)]
        ssq = sb("ssq", [P, TT]); srt = sb("srt", [P, TT]); rstd = sb("rstd", [P, TT]); tmp = sb("tmp", [P, TT])
        psT = [ps(f"psT{i}", [P, HALF]) for i in range(2)]
        psQ = ps("psQ", [P, HALF])
        psG = [ps(f"psG{i}", [P, HALF]) for i in range(2)]
        psE = [ps(f"psE{i}", [P, HALF]) for i in range(2)]
        gain_in = sem("gain_in");
        x_in = [sem(f"x_in{i}") for i in range(XR)]; p_in = [sem(f"p_in{i}") for i in range(2)]; y_in = [sem(f"y_in{i}") for i in range(2)]
        w_hi = sem("w_hi"); w_lo = [sem(f"w_lo{i}") for i in range(2)]
        dve_step = sem("dve_step"); x2_done = sem("x2_done"); ssq_done = sem("ssq_done"); srt_done = sem("srt_done"); hn_done = sem("hn_done")
        turned = sem("turned"); p_turned = sem("p_turned"); h_hi = sem("h_hi"); h_lo = sem("h_lo"); p_hi = sem("p_hi"); p_lo = sem("p_lo")
        gated = sem("gated"); embedded = sem("embedded"); sig_done = sem("sig_done"); e_done = sem("e_done"); o_done = sem("o_done")
        o_out = [sem(f"o_out{i}") for i in range(XR)]
        rows = lambda a, t: a[t * P:(t + 1) * P, :]

        by_vector = [j for j in range(NW) if j % 3 != 2]
        by_pool = [j for j in range(NW) if j % 3 == 2]

        def parts_ready(eng, j):
            i, maker = (1, by_pool) if j in by_pool else (0, by_vector)
            eng.wait_ge(w_lo[i], maker.index(j) + 1)

        def low_weight(eng, ns, j):
            eng.wait_ge(w_hi, j + 1)
            ns.tensor_tensor(wS[1][:, j, :], raw[:, j], wS[0][:, j, :].bitcast(F32), ALU.subtract).then_inc(w_lo[j in by_pool], 1)

        with nc.Block() as block:
            @block.sync
            def _(sp):
                def load_tile(t):
                    if t >= XR:
                        sp.wait_ge(o_out[t % XR], 16 * (t // XR))
                    sp.dma_start(xs[:, t % XR], rows(dr["x1"], t)).then_inc(x_in[t % XR], 16)
                    if t >= 2:
                        sp.wait_ge(p_turned, t - 1)
                    sp.dma_start(pt[:, t % 2], rows(io["p"][0, 0], t)).then_inc(p_in[t % 2], 16)
                load_tile(0)
                sp.wait_ge(y_in[0], 32)
                sp.dma_start(gain[:, :], io["norm_ple"].to_broadcast([P, D])).then_inc(gain_in, 16)
                load_tile(1)
                sp.wait_ge(x2_done, 1)
                for t in range(2, XR):
                    load_tile(t)
                for t in range(TT):
                    sp.wait_ge(o_done, 2 * t + 2)
                    sp.dma_start(rows(io["out"][0], t), xs[:, t % XR]).then_inc(o_out[t % XR], 16)
                    if t + XR < TT:
                        load_tile(t + XR)
                for i in range(XR):
                    sp.wait_ge(o_out[i], 16 * len(range(i, TT, XR)))

            @block.gpsimd
            def _(pool):
                for t in range(TT):
                    if 1 <= t <= 2:
                        for j in by_pool[:2] if t == 1 else by_pool[2:]:
                            low_weight(pool, nc.gpsimd, j)
                    if t >= 2:
                        pool.wait_ge(x2_done, t - 1)
                    for i in range(2):
                        nc.gpsimd.indirect_dma_start(out=ys[:, t % 2, i, :], out_offset=None, in_=dr["ys"],
                                                     in_offset=bass.IndirectOffsetOnAxis(ap=keep["dest"][:, i, t:t + 1], axis=0)).then_inc(y_in[t % 2], 16)

            @block.scalar
            def _(act):
                def square(t):
                    act.wait_ge(x2_done, t + 1)
                    if t >= 1:
                        act.wait_ge(ssq_done, t)
                    nc.scalar.activation(sq[:, :], xs[:, t % XR], ACT.Square, accum_out=ssq[:, t:t + 1]).then_inc(ssq_done, 1)
                    act.wait_ge(ssq_done, t + 1)
                    nc.scalar.activation(srt[:, t:t + 1], ssq[:, t:t + 1], ACT.Sqrt, bias=c["eps"], scale=1.0 / D).then_inc(srt_done, 1)

                def high(t):
                    act.wait_ge(p_turned, t + 1)
                    if t >= 2:
                        act.wait_ge(embedded, 2 * t - 2)
                    nc.scalar.copy(pS[0][:, t % 2], psQ[:, 0:PK * P].rearrange("p (k n) -> p k n", k=PK)).then_inc(p_hi, 1)
                    for h in range(2):
                        act.wait_ge(turned, 2 * t + h + 1)
                        nc.scalar.copy(hS[0][:, t % 2, 4 * h:4 * h + 4, :], psT[h][:, :].rearrange("p (k n) -> p k n", k=4)).then_inc(h_hi, 1)

                def sigmoid(t):
                    for n in range(2):
                        act.wait_ge(gated, 2 * t + n + 1)
                        if t >= 1:
                            act.wait_ge(o_done, 2 * t)
                        nc.scalar.activation(sig[:, n * HALF:(n + 1) * HALF], psG[n][:, :], ACT.Sigmoid).then_inc(sig_done, 1)
                def high_weight(g):
                    act.wait_ge(raw_in[g // EPAIR], 16 * NE + 16)
                    nc.scalar.copy(wS[0][:, g, :], raw[:, g]).then_inc(w_hi, 1)
                nc.scalar.preload_act_table_set("sqrt_and_others")
                for g in range(FIRST):
                    high_weight(g)
                square(0)
                for g in range(FIRST, NW):
                    high_weight(g)
                for t in range(TT + 1):
                    if t < TT:
                        high(t)
                    if t + 1 < TT:
                        square(t + 1)
                    if t >= 1:
                        sigmoid(t - 1)

            @block.vector
            def _(dve):
                link = Chain(dve, dve_step)

                def sum_experts(t):
                    dve.wait_ge(y_in[t % 2], 32 * (t // 2 + 1))
                    dve.wait_ge(x_in[t % XR], 16 * (t // XR + 1))
                    x = xs[:, t % XR]
                    link(nc.vector.scalar_tensor_tensor(x, ys[:, t % 2, 0, :], keep["w"][:, 0, t:t + 1], x, ALU.mult, ALU.add))
                    nc.vector.scalar_tensor_tensor(x, ys[:, t % 2, 1, :], keep["w"][:, 1, t:t + 1], x, ALU.mult, ALU.add).then_inc(x2_done, 1)

                def norm(t):
                    dve.wait_ge(x2_done, t + 1)
                    dve.wait_ge(srt_done, t + 1)
                    refined_rstd(nc, link, rstd[:, t:t + 1], ssq[:, t:t + 1], srt[:, t:t + 1], tmp[:, 0:1], D)
                    if t >= 2:
                        dve.wait_ge(turned, 2 * t - 2)
                    nc.vector.scalar_tensor_tensor(hn[:, t % 2, :], xs[:, t % XR], rstd[:, t:t + 1], gain[:, :], ALU.mult, ALU.mult).then_inc(hn_done, 1)

                def low(t):
                    dve.wait_ge(p_hi, t + 1)
                    nc.vector.tensor_tensor(pS[1][:, t % 2], psQ[:, 0:PK * P].rearrange("p (k n) -> p k n", k=PK),
                                            pS[0][:, t % 2].bitcast(F32), ALU.subtract).then_inc(p_lo, 1)
                    for h in range(2):
                        dve.wait_ge(h_hi, 2 * t + h + 1)
                        nc.vector.tensor_tensor(hS[1][:, t % 2, 4 * h:4 * h + 4, :], psT[h][:, :].rearrange("p (k n) -> p k n", k=4),
                                                hS[0][:, t % 2, 4 * h:4 * h + 4, :].bitcast(F32), ALU.subtract).then_inc(h_lo, 1)

                def finish(t):
                    for n in range(2):
                        cols = slice(n * HALF, (n + 1) * HALF)
                        dve.wait_ge(sig_done, 2 * t + n + 1)
                        dve.wait_ge(embedded, 2 * t + n + 1)
                        nc.vector.tensor_tensor(sig[:, cols], sig[:, cols], psE[n][:, :], ALU.mult).then_inc(e_done, 1)
                        dve.wait_ge(e_done, 2 * t + n + 1)
                        nc.vector.tensor_tensor(xs[:, t % XR, cols], xs[:, t % XR, cols], sig[:, cols], ALU.add).then_inc(o_done, 1)

                for j in by_vector[:3]:
                    low_weight(dve, nc.vector, j)
                sum_experts(0)
                low_weight(dve, nc.vector, by_vector[3])
                dve.wait_ge(gain_in, 16)
                norm(0)
                for j in by_vector[4:5]:
                    low_weight(dve, nc.vector, j)
                low(0)
                for j in by_vector[5:]:
                    low_weight(dve, nc.vector, j)
                sum_experts(1)
                for t in range(TT + 1):
                    if 1 <= t < TT:
                        low(t)
                    if t + 1 < TT:
                        norm(t + 1)
                    if t + 2 < TT:
                        sum_experts(t + 2)
                    if t >= 1:
                        finish(t - 1)

            @block.tensor
            def _(pe):
                def turn(t):
                    pe.wait_ge(p_in[t % 2], 16 * (t // 2 + 1))
                    if t >= 1:
                        pe.wait_ge(p_lo, t)
                    for k in range(PK):
                        ins = nc.tensor.transpose(psQ[:, k * P:(k + 1) * P], pt[:, t % 2, k * P:(k + 1) * P], c["ident"])
                    ins.then_inc(p_turned, 1)
                    pe.wait_ge(hn_done, t + 1)
                    for h in range(2):
                        if t >= 1:
                            pe.wait_ge(h_lo, 2 * t - 1 + h)
                        for k in range(4):
                            ins = nc.tensor.transpose(psT[h][:, k * P:(k + 1) * P], hn[:, t % 2, (4 * h + k) * P:(4 * h + k + 1) * P], c["ident"])
                        ins.then_inc(turned, 1)

                def product(t, bank, n, parts, weights, kts, g0, done):
                    steps = [(k, a, b) for k in range(kts) for a, b in PARTS]
                    for j, (k, a, b) in enumerate(steps):
                        ins = nc.tensor.matmul(bank[:, :], parts[a][:, t % 2, k, :], weights[b][:, g0 + k, n * HALF:(n + 1) * HALF],
                                               start=(j == 0), stop=(j == len(steps) - 1))
                    ins.then_inc(done, 1)
                turn(0)
                for t in range(TT):
                    if t >= 1 and t + 1 < TT:
                        turn(t + 1)
                    pe.wait_ge(p_lo, t + 1)
                    for n in range(2):
                        if t == 0:
                            parts_ready(pe, n)
                        else:
                            pe.wait_ge(e_done, 2 * t - 1 + n)
                    for n in range(2):
                        product(t, psE[n], n, pS, wS, PK, 0, embedded)
                    pe.wait_ge(h_lo, 2 * t + 2)
                    if t == 0:
                        for k in range(KT):
                            parts_ready(pe, PK + k)
                            for n in range(2):
                                for a, b in PARTS:
                                    ins = nc.tensor.matmul(psG[n][:, :], hS[a][:, 0, k, :], wS[b][:, PK + k, n * HALF:(n + 1) * HALF],
                                                           start=(k == 0 and (a, b) == PARTS[0]), stop=(k == KT - 1 and (a, b) == PARTS[-1]))
                                if k == KT - 1:
                                    ins.then_inc(gated, 1)
                        turn(1)
                    else:
                        for n in range(2):
                            pe.wait_ge(sig_done, 2 * t - 1 + n)
                            product(t, psG[n], n, hS, wS, KT, PK, gated)


INPUTS = ["x", "p", "norm_mix", "w_in", "q_norm", "k_norm", "sgu_norm", "w_spatial", "b_spatial", "w_up_a", "w_up_b",
          "w_out", "norm_ffn", "w_group_router", "b_group_router", "w_expert_router", "b_expert_router",
          "w_expert_in", "w_expert_out", "norm_ple", "w_ple_gate", "w_ple_proj"]


def trunk_layer(nc, io):
    with ExitStack() as ctx:
        scratch = lambda name, shape, dt=F32: nc.dram_tensor("d_" + name, shape, dt, kind="Internal").ap()
        sb = lambda name, shape, dt=F32: ctx.enter_context(nc.sbuf_tensor("k_" + name, shape, dt))
        dr = {
            "qk": scratch("qk", [2 * PAIRS, P, T]),
            "v": scratch("v", [T, SBW]),
            "ob": scratch("ob", [PAIRS, P, T]),
            "gates": scratch("gates", [2 * KT, P, T]),
            "x1": scratch("x1", [T, D]),
            "h2": scratch("h2", [T + 1, D]),
            "ys": scratch("ys", [BLOCK * MAXB, D]),
        }
        keep = {"w": sb("w", [P, 2, TT]), "dest": sb("dest", [P, 2, TT], I32), "last": sb("last", [P, NE], I32), "cum": sb("cum", [P, NE + 1], I32),
                "slots": sb("slots", [P, MAXB + 2], I32)}
        c = constants(nc, ctx)
        mix_projection(nc, c, io, dr)
        keep["stream"] = sb("stream", [P, KT + FF // P, D])
        own = lambda name: ctx.enter_context(nc.semaphore("k_" + name))
        keep["stream_in"] = [own(f"stream_in{i}") for i in range(len(range(0, KT + FF // P, EPAIR)))]
        keep["ob_in"] = own("ob_in")
        keep["up_in"] = [own(f"up_in{i}") for i in range(2)]
        keep["gate_in"] = [own(f"gate_in{i}") for i in range(2)]
        attention(nc, c, io, dr, keep)
        merge_and_route(nc, c, io, dr, keep)
        experts(nc, c, io, dr, keep)
        combine_and_embed(nc, c, io, dr, keep)


def kernel(**inputs):
    import numpy as np
    import concourse.bacc as bacc
    from concourse.bass_utils import run_bass_kernel_spmd

    nc = bacc.Bacc("TRN2", target_bir_lowering=False, num_devices=1)
    arrays = {name: np.ascontiguousarray(inputs[name]) for name in INPUTS}
    io = {name: nc.dram_tensor(name, a.shape, mybir.dt.from_np(a.dtype), kind="ExternalInput").ap() for name, a in arrays.items()}
    io["out"] = nc.dram_tensor("out", [1, T, D], F32, kind="ExternalOutput").ap()
    trunk_layer(nc, io)
    r = run_bass_kernel_spmd(nc, [arrays], core_ids=[0])
    return r.results[0]["out"]
```
